# Optimizing a Trainium2 kernel written in Bass

```python
import math
import jax, jax.numpy as jnp
from jax import lax
import numpy as np

D_MODEL = 1024
BATCH = 1
SEQ = 128
DEPTH = 2
DEC_BATCH = 1
DEC_SEQ = 1024
PAST_LEN = 128

GRID_W = 64
N_EVEN = (DEPTH + 1) // 2
N_ODD = DEPTH // 2
EPS = 1e-6
NEG = -1e30
CONV_W = 4
D_RNN = D_MODEL // 2
RG_BLOCKS = 8
RG_BLOCK = D_RNN // RG_BLOCKS
RG_C = 8.0
N_HEADS = 8
N_KV = 2
HEAD_DIM = 64
Q_GROUP = N_HEADS // N_KV
WINDOW = 128
ATT_BLOCK = 128
ROPE_AXIS = HEAD_DIM // 2
ROPE_BASE = 10000.0
EVEN_SPLIT = [D_RNN, 2 * D_RNN, 2 * D_RNN + N_HEADS * HEAD_DIM, 2 * D_RNN + (N_HEADS + N_KV) * HEAD_DIM]
EVEN_IN = 2 * D_RNN + (N_HEADS + 2 * N_KV) * HEAD_DIM
EVEN_OUT = D_RNN + N_HEADS * HEAD_DIM
DN_HEADS = 8
DN_DK = 128
DN_DV = 128
DN_CHUNK = 64
DN_HK = DN_HEADS * DN_DK
DN_HV = DN_HEADS * DN_DV
DN_QKV = 2 * DN_HK + DN_HV
ODD_IN = DN_QKV + DN_HV + 4 * DN_HEADS
D_FF = -(-8 * D_MODEL // (3 * 256)) * 256

kernel_name = "hybrid_flow_prefix_rglru_swa_gdn_step"

def rmsnorm(x, gain):
    xf = x.astype(jnp.float32)
    y = xf * lax.rsqrt(jnp.mean(xf * xf, axis=-1, keepdims=True) + EPS)
    return (y * gain.astype(jnp.float32)).astype(x.dtype)

def l2norm(x):
    return x * lax.rsqrt(jnp.sum(x * x, axis=-1, keepdims=True) + EPS)

def centred_conv(x, w, b=None):
    T = x.shape[1]
    left = CONV_W // 2
    xp = jnp.pad(x, ((0, 0), (left, CONV_W - 1 - left), (0, 0)))
    y = xp[:, 0:T] * w[0]
    for j in range(1, CONV_W):
        y = y + xp[:, j:j + T] * w[j]
    return y if b is None else y + b

def _lin_combine(left, right):
    a_l, b_l = left
    a_r, b_r = right
    return a_l * a_r, a_r * b_l + b_r

def rglru_scan(xc, w_a, b_a, w_x, b_x, lam, h0):
    B, T, _ = xc.shape
    xb = xc.reshape(B, T, RG_BLOCKS, RG_BLOCK)
    r = jax.nn.sigmoid(jnp.einsum('btnc,ncd->btnd', xb, w_a).reshape(B, T, D_RNN) + b_a)
    i = jax.nn.sigmoid(jnp.einsum('btnc,ncd->btnd', xb, w_x).reshape(B, T, D_RNN) + b_x)
    log_a = -RG_C * r * jax.nn.softplus(-lam.astype(jnp.float32))
    a = jnp.exp(log_a)
    b = jnp.sqrt(-jnp.expm1(2.0 * log_a)) * (i * xc)
    a_cum, b_cum = lax.associative_scan(_lin_combine, (a, b), axis=1)
    h = a_cum * h0[:, None, :] + b_cum
    return h, h[:, -1]

def axial_angles(n_tokens):
    rows = n_tokens // GRID_W
    row = jnp.repeat(jnp.arange(rows, dtype=jnp.float32), GRID_W)
    col = jnp.tile(jnp.arange(GRID_W, dtype=jnp.float32), rows)
    inv = ROPE_BASE ** (-jnp.arange(0, ROPE_AXIS, 2, dtype=jnp.float32) / ROPE_AXIS)
    return row[:, None] * inv, col[:, None] * inv

def rope_1d(x, ang):
    x1, x2 = jnp.split(x.astype(jnp.float32), 2, axis=-1)
    cos = jnp.cos(ang)[None, :, None, :]
    sin = jnp.sin(ang)[None, :, None, :]
    return jnp.concatenate([x1 * cos - x2 * sin, x1 * sin + x2 * cos], axis=-1)

def axial_rope(x, ang_r, ang_c):
    return jnp.concatenate([rope_1d(x[..., :ROPE_AXIS], ang_r), rope_1d(x[..., ROPE_AXIS:], ang_c)], axis=-1).astype(x.dtype)

def context_attention(q, k, v, sink):
    B, L = q.shape[:2]
    nb = L // ATT_BLOCK
    scale = HEAD_DIM ** -0.5
    qb = jnp.moveaxis(q.reshape(B, nb, ATT_BLOCK, N_KV, Q_GROUP, HEAD_DIM), 1, 0)
    sk = sink.astype(jnp.float32).reshape(N_KV, Q_GROUP)[None, :, :, None, None]

    def block(q_n):
        s = jnp.einsum('bikgd,bjkd->bkgij', q_n, k).astype(jnp.float32) * scale
        m = jnp.maximum(jnp.max(s, axis=-1, keepdims=True), sk)
        p = jnp.exp(s - m)
        den = jnp.sum(p, axis=-1, keepdims=True) + jnp.exp(sk - m)
        return jnp.einsum('bkgij,bjkd->bikgd', (p / den).astype(v.dtype), v)

    o = lax.map(block, qb)
    return jnp.moveaxis(o, 0, 1).reshape(B, L, N_HEADS * HEAD_DIM)

def latent_attention(q, k, v, ctx_k, ctx_v, sink):
    B, T = q.shape[:2]
    nb = T // ATT_BLOCK
    scale = HEAD_DIM ** -0.5
    qb = jnp.moveaxis(q.reshape(B, nb, ATT_BLOCK, N_KV, Q_GROUP, HEAD_DIM), 1, 0)
    pad = ((0, 0), (ATT_BLOCK, ATT_BLOCK), (0, 0), (0, 0))
    kp = jnp.pad(k, pad)
    vp = jnp.pad(v, pad)
    ctx_k = ctx_k.astype(q.dtype)
    ctx_v = ctx_v.astype(v.dtype)
    offs = jnp.arange(3 * ATT_BLOCK)[None, :] - ATT_BLOCK - jnp.arange(ATT_BLOCK)[:, None]
    in_window = jnp.abs(offs) <= WINDOW
    sk = sink.astype(jnp.float32).reshape(N_KV, Q_GROUP)[None, :, :, None, None]

    def block(args):
        n, q_n = args
        start = n * ATT_BLOCK
        k_n = lax.dynamic_slice_in_dim(kp, start, 3 * ATT_BLOCK, axis=1)
        v_n = lax.dynamic_slice_in_dim(vp, start, 3 * ATT_BLOCK, axis=1)
        kpos = start - ATT_BLOCK + jnp.arange(3 * ATT_BLOCK)
        valid = in_window & ((kpos >= 0) & (kpos < T))[None, :]
        s_w = jnp.einsum('bikgd,bjkd->bkgij', q_n, k_n).astype(jnp.float32) * scale
        s_w = jnp.where(valid, s_w, NEG)
        s_c = jnp.einsum('bikgd,bckd->bkgic', q_n, ctx_k).astype(jnp.float32) * scale
        m = jnp.maximum(jnp.maximum(jnp.max(s_w, axis=-1, keepdims=True), jnp.max(s_c, axis=-1, keepdims=True)), sk)
        p_w = jnp.exp(s_w - m)
        p_c = jnp.exp(s_c - m)
        den = jnp.sum(p_w, axis=-1, keepdims=True) + jnp.sum(p_c, axis=-1, keepdims=True) + jnp.exp(sk - m)
        return (jnp.einsum('bkgij,bjkd->bikgd', (p_w / den).astype(v.dtype), v_n)
                + jnp.einsum('bkgic,bckd->bikgd', (p_c / den).astype(v.dtype), ctx_v))

    o = lax.map(block, (jnp.arange(nb), qb))
    return jnp.moveaxis(o, 0, 1).reshape(B, T, N_HEADS * HEAD_DIM)

def chunk_gated_delta(q, k, v, g, beta, s0):
    B, T, H, _ = q.shape
    dv = v.shape[-1]
    n, C = T // DN_CHUNK, DN_CHUNK

    def chunks(t):
        return jnp.moveaxis(t.reshape((B, n, C, H) + t.shape[3:]), (1, 3), (0, 2))

    qc, kc, vc, bc = chunks(q), chunks(k), chunks(v), chunks(beta)
    gc = jnp.cumsum(chunks(g), axis=-1)
    idx = jnp.arange(C)
    incl = idx[:, None] >= idx[None, :]
    strict = idx[:, None] > idx[None, :]
    decay = jnp.exp(jnp.where(incl, gc[..., :, None] - gc[..., None, :], NEG))
    kk = jnp.einsum('nbhid,nbhjd->nbhij', kc, kc)
    a_mat = jnp.where(strict, bc[..., :, None] * kk * decay, 0.0) + jnp.eye(C, dtype=jnp.float32)
    rhs = jnp.concatenate([vc * bc[..., None], kc * (bc * jnp.exp(gc))[..., None]], axis=-1)
    sol = lax.linalg.triangular_solve(a_mat, rhs, left_side=True, lower=True, unit_diagonal=True)
    u, w = sol[..., :dv], sol[..., dv:]
    qk = jnp.einsum('nbhid,nbhjd->nbhij', qc, kc) * decay
    qg = qc * jnp.exp(gc)[..., None]
    kd = kc * jnp.exp(gc[..., -1:] - gc)[..., None]
    g_last = jnp.exp(gc[..., -1])

    def step(S, xs):
        qg_c, kd_c, u_c, w_c, qk_c, gl_c = xs
        v_new = u_c - jnp.einsum('bhck,bhkv->bhcv', w_c, S)
        o = jnp.einsum('bhck,bhkv->bhcv', qg_c, S) + jnp.einsum('bhij,bhjv->bhiv', qk_c, v_new)
        S = S * gl_c[..., None, None] + jnp.einsum('bhck,bhcv->bhkv', kd_c, v_new)
        return S, o

    s_final, o = lax.scan(step, s0, (qg, kd, u, w, qk, g_last))
    o = jnp.moveaxis(o, (0, 2), (1, 3)).reshape(B, T, H, dv)
    return o, s_final

def even_mixer(h, w_in, conv_w, conv_b, rg_wa, rg_ba, rg_wx, rg_bx, rg_lam, sink, w_out, ctx_k, ctx_v, h0):
    B, T, _ = h.shape
    xr, gr, q, k, v = jnp.split(h @ w_in, EVEN_SPLIT, axis=-1)
    xc = centred_conv(xr, conv_w, conv_b).astype(jnp.float32)
    hf, sf = rglru_scan(xc, rg_wa[0], rg_ba[0], rg_wx[0], rg_bx[0], rg_lam[0], h0[:, 0])
    hb, sb = rglru_scan(xc[:, ::-1], rg_wa[1], rg_ba[1], rg_wx[1], rg_bx[1], rg_lam[1], h0[:, 1])
    y_r = (hf + hb[:, ::-1]).astype(h.dtype) * jax.nn.gelu(gr)
    q = q.reshape(B, T, N_HEADS, HEAD_DIM)
    k = k.reshape(B, T, N_KV, HEAD_DIM)
    v = v.reshape(B, T, N_KV, HEAD_DIM)
    if ctx_k is None:
        y_a = context_attention(q, k, v, sink)
    else:
        ang_r, ang_c = axial_angles(T)
        q = axial_rope(q, ang_r, ang_c)
        k = axial_rope(k, ang_r, ang_c)
        y_a = latent_attention(q, k, v, ctx_k, ctx_v, sink)
    out = jnp.concatenate([y_r, y_a], axis=-1) @ w_out
    return out, jnp.stack([sf, sb], axis=1), k, v

def odd_mixer(h, w_in, conv_w, a_log, dt_bias, o_norm, w_out, s0):
    B, T, _ = h.shape
    qkv, z, ab = jnp.split(h @ w_in, [DN_QKV, DN_QKV + DN_HV], axis=-1)
    qkv = jax.nn.silu(centred_conv(qkv, conv_w)).astype(jnp.float32)
    q, k, v = jnp.split(qkv, [DN_HK, 2 * DN_HK], axis=-1)
    q = l2norm(q.reshape(B, T, DN_HEADS, DN_DK)) * (DN_DK ** -0.5)
    k = l2norm(k.reshape(B, T, DN_HEADS, DN_DK))
    v = v.reshape(B, T, DN_HEADS, DN_DV)
    ab = ab.astype(jnp.float32).reshape(B, T, 2, 2, DN_HEADS)
    g = -jnp.exp(a_log.astype(jnp.float32)) * jax.nn.softplus(ab[:, :, 0] + dt_bias.astype(jnp.float32))
    beta = jax.nn.sigmoid(ab[:, :, 1])
    o_f, s_f = chunk_gated_delta(q, k, v, g[:, :, 0], beta[:, :, 0], s0[:, 0])
    o_b, s_b = chunk_gated_delta(q[:, ::-1], k[:, ::-1], v[:, ::-1], g[:, ::-1, 1], beta[:, ::-1, 1], s0[:, 1])
    o = rmsnorm(o_f + o_b[:, ::-1], o_norm) * jax.nn.silu(z.astype(jnp.float32).reshape(B, T, DN_HEADS, DN_DV))
    out = o.reshape(B, T, DN_HV).astype(h.dtype) @ w_out
    return out, jnp.stack([s_f, s_b], axis=1)

def swiglu(h, w_gu, w_down):
    gate, up = jnp.split(h @ w_gu, 2, axis=-1)
    return (jax.nn.silu(gate) * up) @ w_down

def run_trunk(x, cond, weights, caches):
    (w_mod, b_mod, g_mix, g_ffn, g_final, w_in_even, conv_rg, conv_rg_b, rg_wa, rg_ba, rg_wx, rg_bx,
     rg_lam, attn_sink, w_out_even, w_in_odd, conv_dn, dn_a_log, dn_dt_bias, dn_o_norm, w_out_odd,
     w_gu, w_down) = weights
    B = x.shape[0]
    ks, vs, rgs, dns = [], [], [], []
    for l in range(DEPTH):
        i = l // 2
        sh1, sc1, ga1, sh2, sc2, ga2 = jnp.split(jax.nn.silu(cond) @ w_mod[l] + b_mod[l], 6, axis=-1)
        h = rmsnorm(x, g_mix[l]) * (1 + sc1) + sh1
        if l % 2 == 0:
            if caches is None:
                ck, cv = None, None
                h0 = jnp.zeros((B, 2, D_RNN), jnp.float32)
            else:
                ck, cv, h0 = caches[0][:, i], caches[1][:, i], caches[2][:, i].astype(jnp.float32)
            out, st, k, v = even_mixer(h, w_in_even[i], conv_rg[i], conv_rg_b[i], rg_wa[i], rg_ba[i], rg_wx[i],
                                       rg_bx[i], rg_lam[i], attn_sink[i], w_out_even[i], ck, cv, h0)
            ks.append(k)
            vs.append(v)
            rgs.append(st)
        else:
            if caches is None:
                s0 = jnp.zeros((B, 2, DN_HEADS, DN_DK, DN_DV), jnp.float32)
            else:
                s0 = caches[3][:, i].astype(jnp.float32)
            out, st = odd_mixer(h, w_in_odd[i], conv_dn[i], dn_a_log[i], dn_dt_bias[i], dn_o_norm[i], w_out_odd[i], s0)
            dns.append(st)
        x = x + ga1 * out
        h = rmsnorm(x, g_ffn[l]) * (1 + sc2) + sh2
        x = x + ga2 * swiglu(h, w_gu[l], w_down[l])
    y = rmsnorm(x, g_final)
    return y, jnp.stack(ks, axis=1), jnp.stack(vs, axis=1), jnp.stack(rgs, axis=1), jnp.stack(dns, axis=1)

def setup_inputs(seed: int = 0) -> dict:
    key = jax.random.key(seed)
    keys = iter(jax.random.split(key, 40))

    def nrm(shape, scale):
        return jax.random.normal(next(keys), shape, jnp.float32) * scale

    def unif(shape, lo, hi):
        return jax.random.uniform(next(keys), shape, jnp.float32, lo, hi)

    x_prompt = nrm((BATCH, SEQ, D_MODEL), 1.0)
    x_sample = nrm((DEC_BATCH, DEC_SEQ, D_MODEL), 1.0)
    c = nrm((DEC_BATCH, D_MODEL), 1.0)
    cache_attn_k = nrm((DEC_BATCH, N_EVEN, PAST_LEN, N_KV, HEAD_DIM), 1.0)
    cache_attn_v = nrm((DEC_BATCH, N_EVEN, PAST_LEN, N_KV, HEAD_DIM), 1.0)
    state_rglru = nrm((DEC_BATCH, N_EVEN, 2, D_RNN), 0.5)
    state_delta = nrm((DEC_BATCH, N_ODD, 2, DN_HEADS, DN_DK, DN_DV), 0.1)
    c_ctx = nrm((D_MODEL,), 1.0)
    w_mod = nrm((DEPTH, D_MODEL, 6 * D_MODEL), D_MODEL ** -0.5)
    b_mod = nrm((DEPTH, 6 * D_MODEL), 0.02)
    g_mix = 1.0 + nrm((DEPTH, D_MODEL), 0.05)
    g_ffn = 1.0 + nrm((DEPTH, D_MODEL), 0.05)
    g_final = 1.0 + nrm((D_MODEL,), 0.05)
    w_in_even = nrm((N_EVEN, D_MODEL, EVEN_IN), D_MODEL ** -0.5)
    conv_rg = nrm((N_EVEN, CONV_W, D_RNN), CONV_W ** -0.5)
    conv_rg_b = nrm((N_EVEN, D_RNN), 0.02)
    rg_wa = nrm((N_EVEN, 2, RG_BLOCKS, RG_BLOCK, RG_BLOCK), RG_BLOCK ** -0.5)
    rg_ba = nrm((N_EVEN, 2, D_RNN), 0.02)
    rg_wx = nrm((N_EVEN, 2, RG_BLOCKS, RG_BLOCK, RG_BLOCK), RG_BLOCK ** -0.5)
    rg_bx = nrm((N_EVEN, 2, D_RNN), 0.02)
    a_c = unif((N_EVEN, 2, D_RNN), 0.9, 0.999) ** (1.0 / RG_C)
    rg_lam = jnp.log(a_c) - jnp.log1p(-a_c)
    attn_sink = nrm((N_EVEN, N_HEADS), 0.5)
    w_out_even = nrm((N_EVEN, EVEN_OUT, D_MODEL), EVEN_OUT ** -0.5)
    w_in_odd = nrm((N_ODD, D_MODEL, ODD_IN), D_MODEL ** -0.5)
    conv_dn = nrm((N_ODD, CONV_W, DN_QKV), CONV_W ** -0.5)
    dn_a_log = jnp.log(unif((N_ODD, 2, DN_HEADS), 1.0, 16.0))
    dt = jnp.exp(unif((N_ODD, 2, DN_HEADS), math.log(1e-3), math.log(1e-1)))
    dn_dt_bias = dt + jnp.log(-jnp.expm1(-dt))
    dn_o_norm = 1.0 + nrm((N_ODD, DN_DV), 0.05)
    w_out_odd = nrm((N_ODD, DN_HV, D_MODEL), DN_HV ** -0.5)
    w_gu = nrm((DEPTH, D_MODEL, 2 * D_FF), D_MODEL ** -0.5)
    w_down = nrm((DEPTH, D_FF, D_MODEL), D_FF ** -0.5)
    return {"x_prompt": x_prompt, "x_sample": x_sample, "c": c,
            "cache_attn_k": cache_attn_k, "cache_attn_v": cache_attn_v,
            "state_rglru": state_rglru, "state_delta": state_delta, "c_ctx": c_ctx,
            "w_mod": w_mod, "b_mod": b_mod, "g_mix": g_mix, "g_ffn": g_ffn, "g_final": g_final,
            "w_in_even": w_in_even, "conv_rg": conv_rg, "conv_rg_b": conv_rg_b, "rg_wa": rg_wa,
            "rg_ba": rg_ba, "rg_wx": rg_wx, "rg_bx": rg_bx, "rg_lam": rg_lam, "attn_sink": attn_sink,
            "w_out_even": w_out_even, "w_in_odd": w_in_odd, "conv_dn": conv_dn, "dn_a_log": dn_a_log,
            "dn_dt_bias": dn_dt_bias, "dn_o_norm": dn_o_norm, "w_out_odd": w_out_odd,
            "w_gu": w_gu, "w_down": w_down}

def reference(x_prompt, x_sample, c, cache_attn_k, cache_attn_v, state_rglru, state_delta, c_ctx,
              w_mod, b_mod, g_mix, g_ffn, g_final, w_in_even, conv_rg, conv_rg_b, rg_wa, rg_ba, rg_wx,
              rg_bx, rg_lam, attn_sink, w_out_even, w_in_odd, conv_dn, dn_a_log, dn_dt_bias, dn_o_norm,
              w_out_odd, w_gu, w_down):
    weights = (w_mod, b_mod, g_mix, g_ffn, g_final, w_in_even, conv_rg, conv_rg_b, rg_wa, rg_ba, rg_wx,
               rg_bx, rg_lam, attn_sink, w_out_even, w_in_odd, conv_dn, dn_a_log, dn_dt_bias, dn_o_norm,
               w_out_odd, w_gu, w_down)
    y_prompt, new_k, new_v, new_rg, new_dn = run_trunk(x_prompt, c_ctx[None, None, :], weights, None)
    y_sample = run_trunk(x_sample, c[:, None, :], weights,
                         (cache_attn_k, cache_attn_v, state_rglru, state_delta))[0]
    return (y_prompt, y_sample, new_k, new_v, new_rg, new_dn)


_drawn_inputs = setup_inputs


def setup_inputs(seed=0):
    import zlib

    import numpy as np

    out = dict(_drawn_inputs(seed))
    spreads = {}
    factors = {'cache_attn_k': 5.475,
     'cache_attn_v': 5.275,
     'state_delta': 4.224,
     'rg_ba': 27.357,
     'rg_bx': 7.819,
     'attn_sink': 64.0,
     'dn_o_norm': 5.037}
    for name, (base, spread) in spreads.items():
        noise = np.random.default_rng([zlib.crc32(name.encode()), seed]).standard_normal(out[name].shape)
        drawn = base * np.exp(spread * noise) if base else spread * noise
        out[name] = __import__('jax').numpy.asarray(drawn.astype(out[name].dtype))
    for name, factor in factors.items():
        out[name] = (out[name] * factor).astype(out[name].dtype)
    return out
```

```python
from contextlib import ExitStack

import numpy as np

import concourse.bass as bass
from concourse import mybir

F32 = mybir.dt.float32
F32R = mybir.dt.float32r
BF16 = mybir.dt.bfloat16
ACT = mybir.ActivationFunctionType
ALU = mybir.AluOpType
AX = mybir.AxisListType
ds = bass.ds

P = 128
D = 1024
KC = D // P
TP = 128
TL = 1024
T = TP + TL
NT = T // P
TW = 384
TT = T // TW
EPS = 1e-6
NEG = -1e30
RG_CH = 4
RG_C = 8.0
HD = 64
HEADS = 8
GRID_W = 64
ROPE_BASE = 10000.0
DN_H = 8
FF_CH = 22
FF_G = FF_CH // 2
EVEN_PANELS = 14
ODD_PANELS = 4 * DN_H
OUT_PANELS = 8
FFN_PANELS = 6 * FF_G
STREAM = EVEN_PANELS + OUT_PANELS + FFN_PANELS + 1 + ODD_PANELS + OUT_PANELS + FFN_PANELS
PAD = 2
SH1, SC1, GA1, SH2, SC2, GA2 = range(6)


def three_products(pe, out, wh, wl, xh, xl, first, last):
    pe.matmul(out, wh, xh, start=first, stop=False)
    pe.matmul(out, wh, xl, start=False, stop=False)
    return pe.matmul(out, wl, xh, start=False, stop=last)


class Count:

    def __init__(self, nc, ctx, name):
        self.sem = ctx.enter_context(nc.semaphore(name))
        self.base = 0

    def wait(self, eng, n):
        eng.wait_ge(self.sem, n + self.base)


class Trunk:

    def __init__(self, nc, ctx, I, O):
        self.nc, self.ctx, self.I, self.O = nc, ctx, I, O
        self.top = (nc.sbuf_base + 31) // 32 * 32

        def sb(name, shape, dt=F32):
            t = self.at(name, shape, dt, self.top)
            self.top = (self.top + self.size(shape, dt) + 31) // 32 * 32
            return t

        self.psum = ctx.enter_context(nc.psum_tensor("psum", [P, 8, 512], F32))
        self.mod = sb("mod", [P, 96, 2])
        self.bmod = sb("bmod", [P, 96])
        self.gain = sb("gain", [P, 5, KC])
        self.ones = sb("ones", [P, P])
        self.ident = sb("ident", [P, P])
        self.onep = sb("one_plus_scale", [P, KC, 2])
        self.eps = sb("eps", [P, 1])
        self.cond = sb("cond", [P, KC, 2])
        self.silu_cond = sb("silu_cond", [P, KC, 2])
        self.raw = [sb(f"panel_raw{i}", [P, 1024]) for i in range(2)]
        self.wh = [sb(f"panel_high{i}", [P, 1024], F32R) for i in range(2)]
        self.wl = [sb(f"panel_low{i}", [P, 1024], F32R) for i in range(2)]
        self.h_at = self.top
        self.hh = sb("h_high", [P, KC, T], F32R)
        self.hl = sb("h_low", [P, KC, T], F32R)
        self.x_at = self.top
        self.x = sb("x", [P, KC, T])
        self.rest = self.top
        self.mw = [self.at(f"mod_panel{i}", [P, 1024], F32, self.rest + 4 * T * EVEN_PANELS + 4096 * i)
                   for i in range(2)]
        self.hi_chunk = self.h_at
        self.lo_chunk = self.h_at + 4 * KC * T

        def count(name, credit=0):
            c = Count(nc, ctx, name)
            c.credit = credit
            self.counts.append(c)
            return c

        self.counts = []
        self.raw_full = [count(f"raw_full{i}") for i in range(2)]
        self.split_high = count("split_high")
        self.split_low = count("split_low")
        self.panel_used = count("panel_used")
        self.p0 = 0
        self.modvec_ready = count("modvec_ready")
        self.squared = count("squared")
        self.mean_ready = count("mean_ready")
        self.std_ready = count("std_ready")
        self.rstd_ready = count("rstd_ready")
        self.normed = count("normed")
        self.high_ready = count("high_ready")
        self.low_ready = count("low_ready")
        self.set_free = count("set_free", 2)
        self.gate_ready = count("gate_ready")
        self.prod_ready = count("prod_ready")
        self.mid_high = count("mid_high")
        self.mid_low = count("mid_low")
        self.added = count("added", 1)
        self.down_full = count("down_full")
        self.mw_full = [count(f"mw_full{i}") for i in range(2)]
        self.mw_used = count("mw_used")
        self.mod_free = count("mod_free", 2)

    def at(self, name, shape, dt, offset):
        return self.nc.alloc_sbuf_tensor_at(name, shape, dt, offset=offset)

    @staticmethod
    def size(shape, dt=F32):
        n = 2 if dt == BF16 else 4
        for x in shape[1:]:
            n *= x
        return n

    def placer(self, stage, offset, end):
        where = [offset]

        def sb(name, shape, dt=F32):
            t = self.at(f"{stage}_{name}", shape, dt, where[0])
            where[0] = (where[0] + self.size(shape, dt) + 31) // 32 * 32
            assert where[0] <= end, (stage, name, where[0] - end)
            return t
        return sb

    def sp_load(self, sp, p, buf):
        sp.wait_ge(self.split_low.sem, p - 1)
        src = self.I["stream"][p] if isinstance(p, int) else self.I["stream"][ds(p, 1)].rearrange("a p n -> p (a n)")
        sp.dma_start(self.raw[buf][:], src).then_inc(self.raw_full[buf].sem, 16)

    def sp_stream(self, sp, n):
        p0 = self.p0
        with sp.Fori(0, n // 2) as g:
            for i in range(2):
                self.sp_load(sp, 2 * g + (p0 + 2 + i), (p0 + i) % 2)
        if n % 2:
            self.sp_load(sp, p0 + n + 1, (p0 + n + 1) % 2)

    def act_split(self, act, p, buf):
        act.wait_ge(self.raw_full[buf].sem, (p + (2 - buf)) * 8)
        act.wait_ge(self.panel_used.sem, p - 1)
        act.activation(self.wh[buf][:], self.raw[buf][:], ACT.Copy).then_inc(self.split_high.sem, 1)

    def pool_split(self, pool, p, buf):
        pool.wait_ge(self.split_high.sem, p + 1)
        pool.tensor_tensor(self.wl[buf][:], self.raw[buf][:], self.wh[buf][:].bitcast(F32),
                           ALU.subtract).then_inc(self.split_low.sem, 1)

    def pool_stream(self, pool, n):
        p0 = self.p0
        with pool.Fori(0, n // 2) as g:
            for i in range(2):
                self.pool_split(pool, 2 * g + (p0 + 1 + i), (p0 + 1 + i) % 2)
        if n % 2:
            self.pool_split(pool, p0 + n, (p0 + n) % 2)


def segments(t):
    return [(0, TP, 0), (TP, TW - TP, 1)] if t == 0 else [(0, TW, 1)]


def sp_mod(s, sp, g, first=False):
    for i in range(8):
        if not (first and i < 2):
            sp.wait_ge(s.mw_used.sem, g * 8 + (i - 1))
        src = s.I["wmod"][ds(g * 8 + i, 1)].rearrange("a p n -> p (a n)")
        sp.dma_start(s.mw[i % 2][:], src).then_inc(s.mw_full[i % 2].sem, 16)


def pe_mod(s, pe, g, par):
    pe.wait_ge(s.mod_free.sem, g + 1)
    for i in range(8):
        pe.wait_ge(s.mw_full[i % 2].sem, (g * 4 + (i // 2 + 1)) * 16)
        for k in range(KC):
            mm = pe.matmul(s.psum[:, 6 + par, 2 * i:2 * i + 2], s.mw[i % 2][:, k * P:(k + 1) * P],
                           s.silu_cond[:, k, :], start=k == 0, stop=k == KC - 1)
        mm.then_inc(s.mw_used.sem, 1)


def dve_mod(s, dve, g, par):
    dve.wait_ge(s.mw_used.sem, g * 8 + 8)
    for m in range(2):
        v = dve.tensor_tensor(s.mod[:, ds(g * 8, 8), m], s.psum[:, 6 + par, m:16:2],
                              s.bmod[:, ds(g * 8, 8)], ALU.add)
    v.then_inc(s.mod_free.sem, 1)


def load_stage(s):
    nc, I = s.nc, s.I
    with ExitStack() as ctx:
        loaded = ctx.enter_context(nc.semaphore("loaded"))
        cond_ready = ctx.enter_context(nc.semaphore("cond_ready"))
        silu_ready = ctx.enter_context(nc.semaphore("silu_ready"))
        block = ctx.enter_context(nc.Block())

        @block.sync
        def _(sp):
            sp.dma_start(s.cond[:], I["cond"]).then_inc(cond_ready, 16)
            for g in range(2):
                sp_mod(s, sp, g, g == 0)
            for p in range(2):
                sp.dma_start(s.raw[p][:], I["stream"][p]).then_inc(s.raw_full[p].sem, 16)
            sp.wait_ge(loaded, 16 * 6)

        @block.scalar
        def _(act):
            for t, name in ((s.bmod, "bmod"), (s.gain, "gain"), (s.ones, "ones"), (s.ident, "ident"),
                            (s.eps, "eps")):
                act.dma_start(t[:], I[name]).then_inc(loaded, 16)
            act.wait_ge(cond_ready, 16)
            act.activation(s.silu_cond[:], s.cond[:], ACT.Silu).then_inc(silu_ready, 1)
            act.dma_start(s.x[:], I["x"]).then_inc(loaded, 16)
            act.wait_ge(s.raw_full[0].sem, 16)
            act.activation(s.wh[0][:], s.raw[0][:], ACT.Copy).then_inc(s.split_high.sem, 1)

        @block.gpsimd
        def _(pool):
            s.pool_split(pool, 0, 0)

        @block.tensor
        def _(pe):
            pe.wait_ge(silu_ready, 1)
            for g in range(2):
                pe_mod(s, pe, g, g)

        @block.vector
        def _(dve):
            dve.sem_inc(s.set_free.sem, 2)
            dve.sem_inc(s.mod_free.sem, 2)
            dve.sem_inc(s.added.sem, 1)
            dve.wait_ge(loaded, 16 * 6)
            for g in range(2):
                dve_mod(s, dve, g, g)


def norm_stage(s, layer, which):
    nc, x, psum = s.nc, s.x, s.psum
    shift, scale = (SH1, SC1) if which == 0 else (SH2, SC2)
    sh = (layer * 6 + shift) * 8
    sc = (layer * 6 + scale) * 8
    sb = s.placer(f"norm{layer}{which}", s.rest, s.rest + 64512)
    sq = [sb(f"square{i}", [P, KC, TW]) for i in range(2)]
    std = [sb(f"std{i}", [P, TW]) for i in range(2)]
    rstd = [sb(f"rstd{i}", [P, TW]) for i in range(2)]
    xn = sb("x_scaled", [P, KC, TW])
    with nc.Block() as block:

        @block.scalar
        def _(act):
            def square(t):
                if t >= 2:
                    s.mean_ready.wait(act, t - 1)
                act.activation(sq[t % 2][:], x[:, :, t * TW:(t + 1) * TW], ACT.Square
                               ).then_inc(s.squared.sem, 1)
            square(0)
            square(1)
            for t in range(TT):
                s.mean_ready.wait(act, t + 1)
                if t >= 2:
                    s.rstd_ready.wait(act, t - 1)
                act.activation(std[t % 2][:], psum[:, t % 2, 0:TW], ACT.Sqrt, bias=s.eps[:, 0:1]
                               ).then_inc(s.std_ready.sem, 1)
                if t + 2 < TT:
                    square(t + 2)
                for c in range(KC):
                    s.normed.wait(act, t * KC + c + 1)
                    for o, w, m in segments(t):
                        a = act.activation(s.hh[:, c, t * TW + o:t * TW + o + w], xn[:, c, o:o + w],
                                           ACT.Identity, bias=s.mod[:, sh + c, m:m + 1])
                    a.then_inc(s.high_ready.sem, 1)

        @block.tensor
        def _(pe):
            for t in range(TT):
                s.squared.wait(pe, t + 1)
                if t >= 2:
                    s.std_ready.wait(pe, t - 1)
                for c in range(KC):
                    mm = pe.matmul(psum[:, t % 2, 0:TW], s.ones[:], sq[t % 2][:, c, :],
                                   start=c == 0, stop=c == KC - 1)
                mm.then_inc(s.mean_ready.sem, 1)

        @block.vector
        def _(dve):
            for m in range(2):
                v = dve.scalar_tensor_tensor(s.onep[:, :, m], s.mod[:, sc:sc + KC, m], 1.0,
                                             s.gain[:, 2 * layer + which, :], ALU.add, ALU.mult)
            v.then_inc(s.modvec_ready.sem, 1)
            s.modvec_ready.wait(dve, 1)
            for t in range(TT):
                s.std_ready.wait(dve, t + 1)
                dve.reciprocal(rstd[t % 2][:], std[t % 2][:]).then_inc(s.rstd_ready.sem, 1)
                s.rstd_ready.wait(dve, t + 1)
                for c in range(KC):
                    if t >= 1:
                        s.low_ready.wait(dve, (t - 1) * KC + c + 1)
                    for o, w, m in segments(t):
                        v = dve.scalar_tensor_tensor(xn[:, c, o:o + w], x[:, c, t * TW + o:t * TW + o + w],
                                                     s.onep[:, c, m:m + 1], rstd[t % 2][:, o:o + w],
                                                     ALU.mult, ALU.mult)
                    v.then_inc(s.normed.sem, 1)
                for c in range(KC):
                    s.high_ready.wait(dve, t * KC + c + 1)
                    for o, w, m in segments(t):
                        cols = slice(t * TW + o, t * TW + o + w)
                        v = dve.scalar_tensor_tensor(s.hl[:, c, cols], xn[:, c, o:o + w],
                                                     s.mod[:, sh + c, m:m + 1],
                                                     s.hh[:, c, cols].bitcast(F32), ALU.add, ALU.subtract)
                    v.then_inc(s.low_ready.sem, 1)
    s.modvec_ready.base += 1
    for c in (s.squared, s.mean_ready, s.std_ready, s.rstd_ready):
        c.base += TT
    for c in (s.normed, s.high_ready, s.low_ready):
        c.base += TT * KC


def pe_panel(s, pe, p, buf, group):
    pe.wait_ge(s.split_low.sem, p + 1)
    for t in range(TT):
        for k in range(KC):
            mm = three_products(pe, s.psum[:, 3 * group + t, 0:TW], s.wh[buf][:, k * P:(k + 1) * P],
                                s.wl[buf][:, k * P:(k + 1) * P], s.hh[:, k, t * TW:(t + 1) * TW],
                                s.hl[:, k, t * TW:(t + 1) * TW], k == 0, k == KC - 1)
    mm.then_inc(s.panel_used.sem, 1)


def banks(s, group):
    return s.psum[:, 3 * group:3 * group + TT, 0:TW]


def tiled(ap):
    return ap.rearrange("p (t w) -> p t w", w=TW)


def row(ap, c):
    return ap[:, c, :] if isinstance(c, int) else ap[:, ds(c, 1), :].rearrange("p a t -> p (a t)")


def in_proj_stage(s, out, n):
    p0 = s.p0
    with s.nc.Block() as block:

        @block.sync
        def _(sp):
            s.sp_stream(sp, n)

        @block.gpsimd
        def _(pool):
            s.pool_stream(pool, n)

        @block.scalar
        def _(act):
            with act.Fori(0, n // 2) as g:
                for i in range(2):
                    s.act_split(act, 2 * g + (p0 + i + 1), (p0 + i + 1) % 2)
                    act.wait_ge(s.panel_used.sem, 2 * g + (p0 + i + 1))
                    act.activation(tiled(row(out, 2 * g + i)), banks(s, i), ACT.Copy
                                   ).then_inc(s.set_free.sem, 1)

        @block.tensor
        def _(pe):
            with pe.Fori(0, n // 2) as g:
                for i in range(2):
                    s.set_free.wait(pe, 2 * g + (i + 1))
                    pe_panel(s, pe, 2 * g + (p0 + i), (p0 + i) % 2, i)
    s.p0 += n
    s.set_free.base += n


def add_gated(s, dve, f, group, gate):
    xf = row(s.x, f)
    g = [s.mod[:, ds(gate + f, 1), m:m + 1].rearrange("p a b -> p (a b)") for m in range(2)]
    b0 = 3 * group
    dve.scalar_tensor_tensor(xf[:, 0:TP], s.psum[:, b0, 0:TP], g[0], xf[:, 0:TP], ALU.mult, ALU.add)
    dve.scalar_tensor_tensor(xf[:, TP:TW], s.psum[:, b0, TP:TW], g[1], xf[:, TP:TW], ALU.mult, ALU.add)
    later = xf[:, TW:T].rearrange("p (t w) -> p t w", w=TW)
    return dve.scalar_tensor_tensor(later, s.psum[:, b0 + 1:b0 + 3, 0:TW], g[1], later, ALU.mult, ALU.add)


def out_proj_stage(s, layer):
    p0, n = s.p0, OUT_PANELS
    with s.nc.Block() as block:

        @block.sync
        def _(sp):
            s.sp_stream(sp, n)

        @block.gpsimd
        def _(pool):
            s.pool_stream(pool, n)

        @block.scalar
        def _(act):
            with act.Fori(0, n // 2) as g:
                for i in range(2):
                    s.act_split(act, 2 * g + (p0 + i + 1), (p0 + i + 1) % 2)

        @block.tensor
        def _(pe):
            with pe.Fori(0, n // 2) as g:
                for i in range(2):
                    s.set_free.wait(pe, 2 * g + (i + 1))
                    pe_panel(s, pe, 2 * g + (p0 + i), (p0 + i) % 2, i)

        @block.vector
        def _(dve):
            with dve.Fori(0, n // 2) as g:
                for i in range(2):
                    dve.wait_ge(s.panel_used.sem, 2 * g + (p0 + i + 1))
                    add_gated(s, dve, 2 * g + i, i, (layer * 6 + GA1) * 8).then_inc(s.set_free.sem, 1)
    s.p0 += n
    s.set_free.base += n


def ffn_stage(s, layer):
    p0 = s.p0
    gate_vec = (layer * 6 + GA2) * 8
    sb = s.placer(f"ffn{layer}", s.rest, s.rest + 74592)
    mid_h = [sb(f"mid_high{i}", [P, T], F32R) for i in range(2)]
    mid_l = [sb(f"mid_low{i}", [P, T], F32R) for i in range(2)]
    silu = sb("silu_gate", [P, T])
    prod = sb("product", [P, T])
    added, used = s.added, s.panel_used

    def gate_panel(c):
        return 3 * c + (p0 - 1)

    with s.nc.Block() as block:

        @block.sync
        def _(sp):
            s.sp_stream(sp, FFN_PANELS)

        @block.gpsimd
        def _(pool):
            s.pool_stream(pool, FFN_PANELS)

        @block.scalar
        def _(act):
            def hidden(c, par, g_panel, buf):
                s.act_split(act, g_panel + 1, (buf + 1) % 2)
                act.wait_ge(used.sem, g_panel + 1)
                s.prod_ready.wait(act, c)
                act.activation(tiled(silu[:]), banks(s, 0), ACT.Silu).then_inc(s.gate_ready.sem, 1)
                s.act_split(act, g_panel + 2, buf)
                s.prod_ready.wait(act, c + 1)
                act.activation(mid_h[par][:], prod[:], ACT.Copy).then_inc(s.mid_high.sem, 1)

            hidden(0, 0, p0, p0 % 2)
            with act.Fori(0, (FF_CH - 2) // 2) as g:
                for i in range(2):
                    buf = (p0 + i) % 2
                    hidden(2 * g + (1 + i), 1 - i, 6 * g + (p0 + 2 + 3 * i), buf)
                    s.act_split(act, 6 * g + (p0 + 5 + 3 * i), (buf + 1) % 2)
            last = FF_CH - 1
            hidden(last, last % 2, gate_panel(last), gate_panel(last) % 2)
            for p in range(gate_panel(last) + 3, p0 + FFN_PANELS + 1):
                s.act_split(act, p, p % 2)

        @block.tensor
        def _(pe):
            def down(c, p, buf, par, last=False):
                pe.wait_ge(s.split_low.sem, p + 1)
                s.mid_low.wait(pe, c + 1)
                for f in range(KC):
                    if f == 0 and not last:
                        s.gate_ready.wait(pe, c + 2)
                    elif f == 1 and not last:
                        s.prod_ready.wait(pe, c + 2)
                    else:
                        added.wait(pe, 8 * c + f)
                    for t in range(TT):
                        mm = three_products(pe, s.psum[:, 3 * (f % 2) + t, 0:TW],
                                            s.wh[buf][:, f * P:(f + 1) * P], s.wl[buf][:, f * P:(f + 1) * P],
                                            mid_h[par][:, t * TW:(t + 1) * TW],
                                            mid_l[par][:, t * TW:(t + 1) * TW], True, True)
                    if f < KC - 1:
                        mm.then_inc(s.down_full.sem, 1)
                mm.then_inc(used.sem, 1)

            pe_panel(s, pe, p0, p0 % 2, 0)
            pe_panel(s, pe, p0 + 1, (p0 + 1) % 2, 1)

            def chunk(c, g_panel, buf, par):
                s.gate_ready.wait(pe, c)
                added.wait(pe, 8 * c - 8)
                pe_panel(s, pe, g_panel, buf, 0)
                s.prod_ready.wait(pe, c)
                added.wait(pe, 8 * c - 7)
                pe_panel(s, pe, g_panel + 1, (buf + 1) % 2, 1)
                down(c - 1, g_panel + 2, buf, 1 - par)

            with pe.Fori(0, (FF_CH - 2) // 2) as g:
                for i in range(2):
                    chunk(2 * g + (1 + i), 6 * g + (p0 + 2 + 3 * i), (p0 + i) % 2, 1 - i)
            last = FF_CH - 1
            chunk(last, gate_panel(last), gate_panel(last) % 2, last % 2)
            down(last, p0 + FFN_PANELS - 1, (p0 + FFN_PANELS - 1) % 2, last % 2, True)

        @block.vector
        def _(dve):
            def product(c, u_used):
                s.gate_ready.wait(dve, c + 1)
                dve.wait_ge(used.sem, u_used)
                s.mid_high.wait(dve, c)
                s.mid_low.wait(dve, c)
                dve.tensor_tensor(tiled(prod[:]), tiled(silu[:]), banks(s, 1), ALU.mult
                                  ).then_inc(s.prod_ready.sem, 1)

            def low(c, par):
                s.mid_high.wait(dve, c + 1)
                dve.tensor_tensor(mid_l[par][:], prod[:], mid_h[par][:].bitcast(F32), ALU.subtract
                                  ).then_inc(s.mid_low.sem, 1)

            def add(c, f, d_used):
                if f < KC - 1:
                    s.down_full.wait(dve, 7 * c + (f + 1))
                else:
                    dve.wait_ge(used.sem, d_used)
                added.wait(dve, 8 * c + f)
                add_gated(s, dve, f, f % 2, gate_vec).then_inc(added.sem, 1)

            def chunk(c, g_panel, par):
                product(c, g_panel + 2)
                for f in range(KC):
                    add(c - 1, f, g_panel + 3)
                    if f == 1:
                        low(c, par)

            product(0, p0 + 2)
            low(0, 0)
            with dve.Fori(0, (FF_CH - 2) // 2) as g:
                for i in range(2):
                    chunk(2 * g + (1 + i), 6 * g + (p0 + 2 + 3 * i), 1 - i)
            last = FF_CH - 1
            chunk(last, gate_panel(last), last % 2)
            for f in range(KC):
                add(last, f, p0 + FFN_PANELS)
    s.p0 += FFN_PANELS
    for c, n in ((s.gate_ready, FF_CH), (s.prod_ready, FF_CH), (s.mid_high, FF_CH), (s.mid_low, FF_CH),
                 (s.down_full, 7 * FF_CH), (s.added, 8 * FF_CH)):
        c.base += n


def final_stage(s):
    nc, x, psum = s.nc, s.x, s.psum
    sb = s.placer("final", s.rest, s.rest + 64512)
    sq = [sb(f"square{i}", [P, KC, TW]) for i in range(2)]
    std = [sb(f"std{i}", [P, TW]) for i in range(2)]
    rstd = [sb(f"rstd{i}", [P, TW]) for i in range(2)]
    with nc.semaphore("y_stored") as y_stored, nc.Block() as block:

        @block.scalar
        def _(act):
            def square(t):
                if t >= 2:
                    s.mean_ready.wait(act, t - 1)
                act.activation(sq[t % 2][:], x[:, :, t * TW:(t + 1) * TW], ACT.Square
                               ).then_inc(s.squared.sem, 1)
            square(0)
            square(1)
            for t in range(TT):
                s.mean_ready.wait(act, t + 1)
                if t >= 2:
                    s.rstd_ready.wait(act, t - 1)
                act.activation(std[t % 2][:], psum[:, t % 2, 0:TW], ACT.Sqrt, bias=s.eps[:, 0:1]
                               ).then_inc(s.std_ready.sem, 1)
                if t + 2 < TT:
                    square(t + 2)

        @block.tensor
        def _(pe):
            for t in range(TT):
                s.squared.wait(pe, t + 1)
                if t >= 2:
                    s.std_ready.wait(pe, t - 1)
                for c in range(KC):
                    mm = pe.matmul(psum[:, t % 2, 0:TW], s.ones[:], sq[t % 2][:, c, :],
                                   start=c == 0, stop=c == KC - 1)
                mm.then_inc(s.mean_ready.sem, 1)

        @block.vector
        def _(dve):
            for t in range(TT):
                s.std_ready.wait(dve, t + 1)
                dve.reciprocal(rstd[t % 2][:], std[t % 2][:]).then_inc(s.rstd_ready.sem, 1)
                s.rstd_ready.wait(dve, t + 1)
                s.squared.wait(dve, t + 1)
                for c in range(KC):
                    xt = x[:, c, t * TW:(t + 1) * TW]
                    v = dve.scalar_tensor_tensor(xt, xt, s.gain[:, 4, c:c + 1], rstd[t % 2][:],
                                                 ALU.mult, ALU.mult)
                v.then_inc(s.normed.sem, 1)

        @block.sync
        def _(sp):
            for t in range(TT):
                s.normed.wait(sp, t + 1)
                sp.dma_start(s.O["y"][:, :, t * TW:(t + 1) * TW], x[:, :, t * TW:(t + 1) * TW]
                             ).then_inc(y_stored, 16)
            sp.wait_ge(y_stored, 16 * TT)
            for i in range(2):
                n = (STREAM + PAD + 1 - i) // 2
                sp.wait_ge(s.raw_full[i].sem, 16 * n)


def even_buffer(s):
    return s.at("even", [P, EVEN_PANELS, T], F32, s.rest)


def rg_stage(s, even):
    nc, psum, I = s.nc, s.psum, s.I
    sb = s.placer("rg", s.hi_chunk + 16 * T, s.lo_chunk)
    den = s.at("rg_den", [P, T], F32, s.hi_chunk + 12 * T)
    gate = [sb(f"gate{j}", [P, T]) for j in range(4)]
    sb = s.placer("rg_lo", s.lo_chunk + 16 * T, s.x_at)
    mult = [sb(f"mult{d}", [P, T]) for d in range(2)]
    xc = sb("xc", [P, T])
    gw = sb("gate_weights", [P, 4 * P])
    conv = sb("conv", [P, RG_CH, 5])
    bias = sb("gate_bias", [P, RG_CH, 4])
    lam = sb("lam", [P, RG_CH, 2])
    h0 = sb("h0", [P, RG_CH, 2])
    sp_ = [sb(f"softplus{i}", [P, RG_CH, 2]) for i in range(4)]
    last = sb("last", [P, RG_CH, 2])
    with ExitStack() as ctx:
        def sem(name):
            return ctx.enter_context(nc.semaphore("rg_" + name))
        small, gelu_ready, sp_step, sp_done = sem("small"), sem("gelu"), sem("sp_step"), sem("sp_done")
        gw_full, gates_done, gate_full, gate_read = sem("gw_full"), sem("gates_done"), sem("gate_full"), sem("gate_read")
        conv_step, tanh_ready, a_ready = sem("conv_step"), sem("tanh_ready"), sem("a_ready")
        m_step, m_ready, root_ready, b_step, scanned = sem("m_step"), sem("m_ready"), sem("root_ready"), sem("b_step"), sem("scanned")
        y_step, y_high, chunk_done, stored = sem("y_step"), sem("y_high"), sem("chunk_done"), sem("stored")
        ib_ready = sem("ib_ready")
        block = ctx.enter_context(nc.Block())

        def scalar(t, c, j):
            return t[:, ds(c, 1), j:j + 1].rearrange("p a b -> p (a b)")

        @block.sync
        def _(sp):
            for t, name in ((conv, "conv_rg"), (bias, "rgb"), (lam, "lam"), (h0, "h0")):
                sp.dma_start(t[:], I[name]).then_inc(small, 16)
            sp.dma_start(s.O["k"], even[:, 12, 0:TP]).then_inc(stored, 16)
            sp.dma_start(s.O["v"], even[:, 13, 0:TP]).then_inc(stored, 16)
            with sp.Fori(0, RG_CH) as c:
                sp.wait_ge(gates_done, c)
                sp.dma_start(gw[:], I["rgw"][ds(c, 1)].rearrange("a p n -> p (a n)")).then_inc(gw_full, 16)
                for j in range(2):
                    sp_mod(s, sp, 2 * c + (2 + j))
            for g in (10, 11):
                sp_mod(s, sp, g)
            sp.wait_ge(chunk_done, RG_CH)
            sp.dma_start(s.O["rg"], last[:]).then_inc(stored, 16)
            sp.wait_ge(stored, 48)

        @block.tensor
        def _(pe):
            with pe.Fori(0, RG_CH) as c:
                pe.wait_ge(gw_full, 16 * c + 16)
                pe.wait_ge(conv_step, 7 * c + 7)
                for j in range(4):
                    pe.wait_ge(gate_read, 4 * c + (j + 1))
                    for t in range(TT):
                        mm = pe.matmul(psum[:, 3 * (j % 2) + t, 0:TW], gw[:, j * P:(j + 1) * P],
                                       xc[:, t * TW:(t + 1) * TW], start=True, stop=True)
                    if j == 3:
                        mm.then_inc(gates_done, 1)
                    else:
                        mm.then_inc(gate_full, 1)
                for j in range(2):
                    pe_mod(s, pe, 2 * c + (2 + j), j)
            for g in (10, 11):
                pe_mod(s, pe, g, g % 2)

        @block.scalar
        def _(act):
            act.sem_inc(gate_read, 2)
            act.activation(even[:, 4:8, :], even[:, 4:8, :], ACT.Gelu_apprx_tanh).then_inc(gelu_ready, 1)
            act.wait_ge(small, 64)
            act.activation(sp_[0][:], lam[:], ACT.Abs).then_inc(sp_step, 1)
            act.wait_ge(sp_step, 1)
            act.activation(sp_[1][:], sp_[0][:], ACT.Exp, scale=-1.0).then_inc(sp_step, 1)
            act.wait_ge(sp_done, 1)
            act.activation(sp_[0][:], sp_[2][:], ACT.Ln).then_inc(sp_step, 1)
            act.wait_ge(sp_done, 6)
            with act.Fori(0, RG_CH) as c:
                act.wait_ge(chunk_done, c)
                for j in range(4):
                    if j < 3:
                        act.wait_ge(gate_full, 3 * c + (j + 1))
                    else:
                        act.wait_ge(gates_done, c + 1)
                    act.activation(tiled(gate[j][:]), banks(s, j % 2), ACT.Sigmoid,
                                   bias=scalar(bias, c, j)).then_inc(gate_read, 1)
                act.wait_ge(gate_read, 4 * c + 6)
                for d in range(2):
                    act.activation(mult[d][:], gate[2 * d][:], ACT.Tanh, scale=scalar(sp_[0], c, d)
                                   ).then_inc(tanh_ready, 1)
                for d in range(2):
                    act.wait_ge(tanh_ready, 2 * c + (d + 1))
                    act.activation(gate[2 * d][:], gate[2 * d][:], ACT.Exp, scale=scalar(sp_[1], c, d)
                                   ).then_inc(a_ready, 1)
                for d in range(2):
                    act.wait_ge(m_ready, 2 * c + (d + 1))
                    act.activation(mult[d][:], mult[d][:], ACT.Sqrt, scale=2.0).then_inc(root_ready, 1)
                act.wait_ge(y_step, 2 * c + 2)
                act.activation(row(s.hh, c), xc[:], ACT.Copy).then_inc(y_high, 1)

        @block.gpsimd
        def _(pool):
            with pool.Fori(0, RG_CH) as c:
                for d in range(2):
                    pool.wait_ge(gate_read, 4 * c + (2 * d + 4))
                    pool.tensor_tensor(gate[2 * d + 1][:], gate[2 * d + 1][:], xc[:], ALU.mult
                                       ).then_inc(ib_ready, 1)

        @block.vector
        def _(dve):
            dve.wait_ge(small, 64)
            dve.wait_ge(sp_step, 2)
            dve.tensor_scalar(sp_[2][:], sp_[1][:], 1.0, None, ALU.add).then_inc(sp_done, 1)
            dve.wait_ge(sp_done, 1)
            dve.scalar_tensor_tensor(sp_[3][:], sp_[2][:], -1.0, sp_[1][:], ALU.add, ALU.subtract
                                     ).then_inc(sp_done, 1)
            dve.wait_ge(sp_step, 3)
            dve.reciprocal(sp_[2][:], sp_[2][:]).then_inc(sp_done, 1)
            dve.wait_ge(sp_done, 3)
            dve.tensor_tensor(sp_[3][:], sp_[3][:], sp_[2][:], ALU.mult)
            dve.tensor_scalar(sp_[1][:], lam[:], -RG_C, 0.0, ALU.mult, ALU.max).then_inc(sp_done, 1)
            dve.wait_ge(sp_done, 4)
            dve.tensor_tensor(sp_[0][:], sp_[0][:], sp_[3][:], ALU.subtract).then_inc(sp_done, 1)
            dve.wait_ge(sp_done, 5)
            dve.scalar_tensor_tensor(sp_[0][:], sp_[0][:], RG_C, sp_[1][:], ALU.mult, ALU.add
                                     ).then_inc(sp_step, 1)
            dve.wait_ge(sp_step, 4)
            dve.tensor_scalar(sp_[1][:], sp_[0][:], -1.0, None, ALU.mult).then_inc(sp_done, 1)
            with dve.Fori(0, RG_CH) as c:
                xr = row(even, c)
                dve.wait_ge(ib_ready, 2 * c)
                dve.wait_ge(chunk_done, c)
                dve.tensor_scalar(xc[:], xr, scalar(conv, c, 2), scalar(conv, c, 4), ALU.mult, ALU.add
                                  ).then_inc(conv_step, 1)
                for n, (tap, off) in enumerate(((0, -2), (1, -1), (3, 1))):
                    for m, (lo, hi) in enumerate(((0, TP), (TP, T))):
                        a, b = (lo - off, hi) if off < 0 else (lo, hi - off)
                        dve.wait_ge(conv_step, 7 * c + (2 * n + m + 1) if n else 7 * c + 1)
                        v = dve.scalar_tensor_tensor(xc[:, a:b], xr[:, a + off:b + off], scalar(conv, c, tap),
                                                     xc[:, a:b], ALU.mult, ALU.add).then_inc(conv_step, 1)
                for d in range(2):
                    dve.wait_ge(tanh_ready, 2 * c + (d + 1))
                    dve.wait_ge(m_ready, 2 * c + d)
                    dve.tensor_scalar(den[:], mult[d][:], 1.0, None, ALU.add).then_inc(m_step, 1)
                    dve.wait_ge(m_step, 4 * c + (2 * d + 1))
                    dve.reciprocal(den[:], den[:]).then_inc(m_step, 1)
                    dve.wait_ge(m_step, 4 * c + (2 * d + 2))
                    dve.tensor_tensor(mult[d][:], mult[d][:], den[:], ALU.mult).then_inc(m_ready, 1)
                for d in range(2):
                    a, b, h = gate[2 * d], gate[2 * d + 1], mult[d]
                    dve.wait_ge(root_ready, 2 * c + (d + 1))
                    dve.wait_ge(ib_ready, 2 * c + (d + 1))
                    dve.wait_ge(a_ready, 2 * c + (d + 1))
                    dve.tensor_tensor(b[:], b[:], h[:], ALU.mult).then_inc(b_step, 1)
                    dve.wait_ge(b_step, 2 * c + (d + 1))
                    for m, (lo, hi) in enumerate(((0, TP), (TP, T))):
                        cols = slice(lo, hi) if d == 0 else slice(hi - 1, lo - 1 if lo else None, -1)
                        v = dve.tensor_tensor_scan(h[:, cols], a[:, cols], b[:, cols],
                                                   0.0 if m == 0 else scalar(h0, c, d), ALU.mult, ALU.add)
                    v.then_inc(scanned, 1)
                dve.wait_ge(scanned, 2 * c + 2)
                for d in range(2):
                    at = TP - 1 if d == 0 else 0
                    dve.tensor_copy(scalar(last, c, d), mult[d][:, at:at + 1])
                dve.tensor_tensor(xc[:], mult[0][:], mult[1][:], ALU.add).then_inc(y_step, 1)
                dve.wait_ge(y_step, 2 * c + 1)
                dve.wait_ge(gelu_ready, 1)
                dve.tensor_tensor(xc[:], xc[:], row(even, c + 4), ALU.mult).then_inc(y_step, 1)
                dve.wait_ge(y_high, c + 1)
                dve.wait_ge(y_step, 2 * c + 2)
                dve.tensor_tensor(row(s.hl, c), xc[:], row(s.hh, c).bitcast(F32), ALU.subtract
                                  ).then_inc(chunk_done, 1)
                for j in range(2):
                    dve_mod(s, dve, 2 * c + (2 + j), j)
            for g in (10, 11):
                dve_mod(s, dve, g, g % 2)


def attention_stage(s, even):
    nc, psum, I = s.nc, s.psum, s.I
    sb = s.placer("att", s.rest, s.rest + 8 * 4 * T)
    cos, sin, turned = sb("cos", [P, TL]), sb("sin", [P, TL]), sb("turned", [P, TL])
    rope = sb("rope", [P, P])
    ctx_k = sb("ctx_k", [P, P])
    vt = sb("v_tokens", [P, NT + 1, P])
    window = sb("window", [P, 8, 2, P], BF16)
    ident_bf = sb("ident_bf", [P, P], BF16)
    q_blk = sb("q_block", [P, 2, 4, P])
    prob = sb("prob", [P, 2, 512])
    prob_t = sb("prob_t", [P, 2, 512])
    sb = s.placer("att_hi", s.rest + EVEN_PANELS * 4 * T, s.rest + 74592)
    o_sb = sb("o", [P, 512])
    sink, nsink = sb("sink", [P, HEADS]), sb("neg_sink", [P, HEADS])
    top, negm, rows, es, den, rden = (sb(n, [P, HEADS]) for n in ("top", "negm", "rows", "es", "den", "rden"))
    scale = HD ** -0.5
    with ExitStack() as ctx:
        def sem(name):
            return ctx.enter_context(nc.semaphore("att_" + name))
        loaded, turn_full, turn_step, roped, v_full, vt_ready = (
            sem(n) for n in ("loaded", "turn_full", "turn_step", "roped", "v_full", "vt_ready"))
        q_ready, s_full, top_step, negm_ready, p_ready, pt_full, pt_act, pt_dve = (
            sem(n) for n in ("q_ready", "s_full", "top_step", "negm_ready", "p_ready", "pt_full", "pt_act", "pt_dve"))
        pv_done, es_ready, den_step, o_ready, y_full, y_high, y_low, nsink_ready = (
            sem(n) for n in ("pv_done", "es_ready", "den_step", "o_ready", "y_full", "y_high", "y_low", "nsink_ready"))
        q_zero = sem("q_zero")
        block = ctx.enter_context(nc.Block())

        @block.sync
        def _(sp):
            for t, name in ((rope, "rope"), (sin, "sin"), (cos, "cos"), (ctx_k, "ctx_k"), (window, "window"),
                            (ident_bf, "ident_bf"), (sink, "sink")):
                sp.dma_start(t[:], I[name]).then_inc(loaded, 16)
            sp.dma_start(vt[:, NT, :], I["ctx_v"]).then_inc(loaded, 16)

        def scores(pe, c, b, prompt):
            for h in range(2):
                q = q_blk[:, h, c, :]
                out = psum[:, 2 * (c % 2) + h, :]
                if prompt:
                    mm = pe.matmul(out[:, 0:P], q, even[:, 12, 0:P], start=True, stop=True)
                    continue
                pe.matmul(out[:, 0:TW], q, 
                          even[:, 12:14, :].rearrange("p a t -> p (a t)")[:, ds(b * P, TW)], start=True, stop=False,
                          skip_group_check=True)
                pe.matmul(out[:, TW:512], q, ctx_k[:], start=False, stop=False, skip_group_check=True)
                for j in range(2):
                    mm = pe.matmul(out[:, 2 * j * P:(2 * j + 1) * P], ident_bf[:],
                                   window[:, ds(b, 1), j, :].rearrange("p a n -> p (a n)"), start=False,
                                   stop=j == 1, skip_group_check=True)
            mm.then_inc(s_full, 1)

        @block.tensor
        def _(pe):
            pe.wait_ge(loaded, 16 * 8)
            with pe.Fori(0, 5) as c:
                pe.wait_ge(turn_step, 3 * c)
                for t in range(2):
                    mm = pe.matmul(psum[:, t, :], rope[:], even[:, ds(c + 8, 1), TP + 512 * t:TP + 512 * (t + 1)]
                                   .rearrange("p a t -> p (a t)"), start=True, stop=True)
                mm.then_inc(turn_full, 1)
            for n in range(NT):
                mm = pe.transpose(psum[:, 2 + n // 4, (n % 4) * P:(n % 4 + 1) * P],
                                  even[:, 13, n * P:(n + 1) * P], s.ident[:])
            mm.then_inc(v_full, 1)
            pe.wait_ge(roped, 1)
            pe.wait_ge(vt_ready, 1)

            def block_of(i, b, prompt):
                nk = 1 if prompt else 4

                def weigh(c):
                    pe.wait_ge(p_ready, 8 * i + (2 * c + 2))
                    pe.wait_ge(pt_act, 4 * i + c)
                    pe.wait_ge(pt_dve, 4 * i + c)
                    for h in range(2):
                        for k in range(nk):
                            mm = pe.transpose(psum[:, 4 + h, k * P:(k + 1) * P],
                                              prob[:, h, k * P:(k + 1) * P], s.ident[:])
                    mm.then_inc(pt_full, 1)
                    pe.wait_ge(pt_act, 4 * i + (c + 1))
                    pe.wait_ge(pt_dve, 4 * i + (c + 1))
                    if c == 0:
                        pe.wait_ge(o_ready, i)
                    for h in range(2):
                        out = psum[:, 6, c * P + HD * h:c * P + HD * h + HD]
                        for k in range(nk):
                            if prompt:
                                v = vt[:, 0, HD * h:HD * h + HD]
                            elif k == 3:
                                v = vt[:, NT, HD * h:HD * h + HD]
                            else:
                                v = vt[:, ds(b + k, 1), HD * h:HD * h + HD].rearrange("p a n -> p (a n)")
                            mm = pe.matmul(out, prob_t[:, h, k * P:(k + 1) * P], v, start=k == 0, stop=k == nk - 1)
                    mm.then_inc(pv_done, 1)

                pe.wait_ge(q_ready, i + 1)
                for c in range(4):
                    if c < 2:
                        pe.wait_ge(p_ready, 8 * i)
                    else:
                        pe.wait_ge(p_ready, 8 * i + (2 * c - 2))
                    scores(pe, c, b, prompt)
                    if c >= 1:
                        weigh(c - 1)
                weigh(3)
                pe.wait_ge(o_ready, i + 1)
                pe.wait_ge(y_low, i)
                for c in range(4):
                    mm = pe.transpose(psum[:, 7, c * P:(c + 1) * P], o_sb[:, c * P:(c + 1) * P], s.ident[:])
                mm.then_inc(y_full, 1)

            block_of(0, 0, True)
            with pe.Fori(0, 8) as b:
                block_of(b + 1, b, False)

        @block.gpsimd
        def _(pool):
            pool.wait_ge(loaded, 16 * 8)
            pool.tensor_scalar(nsink[:], sink[:], -1.0, None, ALU.mult).then_inc(nsink_ready, 1)
            pool.memset(q_blk[:], 0.0).then_inc(q_zero, 1)
            pool.wait_ge(q_zero, 1)
            pool.wait_ge(roped, 1)

            def load_q(cols):
                pool.tensor_copy(q_blk[0:HD, 0], even[0:HD, 8:12, cols])
                pool.tensor_copy(q_blk[HD:P, 1], even[HD:P, 8:12, cols]).then_inc(q_ready, 1)
            load_q(slice(0, P))
            with pool.Fori(0, 8) as b:
                pool.wait_ge(s_full, 4 * b + 4)
                load_q(ds(b * P + TP, P))

        @block.scalar
        def _(act):
            def block_of(i, cols, prompt):
                wide = P if prompt else 512
                nk = 1 if prompt else 4
                for c in range(4):
                    act.wait_ge(negm_ready, 4 * i + (c + 1))
                    act.wait_ge(pt_full, 4 * i + c)
                    for h in range(2):
                        j = 2 * c + h
                        act.activation(prob[:, h, 0:wide], psum[:, 2 * (c % 2) + h, 0:wide], ACT.Exp,
                                       bias=negm[:, j:j + 1], scale=scale, accum_out=rows[:, j:j + 1]
                                       ).then_inc(p_ready, 1)
                    if c == 3:
                        act.activation(es[:], es[:], ACT.Exp).then_inc(es_ready, 1)
                    act.wait_ge(pt_full, 4 * i + (c + 1))
                    act.wait_ge(pv_done, 4 * i + c)
                    act.activation(prob_t[:, 0, 0:wide], psum[:, 4, 0:wide], ACT.Copy).then_inc(pt_act, 1)
                act.wait_ge(y_full, i + 1)
                act.activation(s.hh[:, 4:8, cols], psum[:, 7, :].rearrange("p (c w) -> p c w", w=P), ACT.Copy
                               ).then_inc(y_high, 1)
            block_of(0, slice(0, P), True)
            with act.Fori(0, 8) as b:
                block_of(b + 1, ds(b * P + TP, P), False)

        @block.vector
        def _(dve):
            dve.wait_ge(loaded, 16 * 8)
            with dve.Fori(0, 5) as c:
                x = even[:, ds(c + 8, 1), TP:T].rearrange("p a t -> p (a t)")
                dve.wait_ge(turn_full, c + 1)
                dve.wait_ge(turn_step, 3 * c)
                dve.tensor_tensor(turned[:].rearrange("p (a t) -> p a t", a=2), psum[:, 0:2, :],
                                  sin[:].rearrange("p (a t) -> p a t", a=2), ALU.mult).then_inc(turn_step, 1)
                dve.tensor_tensor(x, x, cos[:], ALU.mult).then_inc(turn_step, 1)
                dve.wait_ge(turn_step, 3 * c + 2)
                dve.tensor_tensor(x, x, turned[:], ALU.add).then_inc(turn_step, 1)
            dve.wait_ge(turn_step, 15)
            dve.sem_inc(roped, 1)
            dve.wait_ge(v_full, 1)
            dve.tensor_copy(vt[:, 0:8, :].rearrange("p (a n) w -> p a (n w)", a=2), psum[:, 2:4, :])
            dve.tensor_copy(vt[:, 8, :], psum[:, 4, 0:P]).then_inc(vt_ready, 1)
            dve.wait_ge(nsink_ready, 1)

            def block_of(i, cols, prompt):
                wide = P if prompt else 512

                def largest(c):
                    dve.wait_ge(s_full, 4 * i + (c + 1))
                    two = slice(2 * c, 2 * c + 2)
                    dve.tensor_reduce(top[:, two], psum[:, 2 * (c % 2):2 * (c % 2) + 2, 0:wide], AX.X, ALU.max
                                      ).then_inc(top_step, 1)
                    dve.wait_ge(top_step, 4 * i + (c + 1))
                    dve.wait_ge(p_ready, 8 * i)
                    if c == 0:
                        dve.wait_ge(es_ready, i)
                    dve.scalar_tensor_tensor(negm[:, two], top[:, two], -scale, nsink[:, two], ALU.mult, ALU.min
                                             ).then_inc(den_step, 1)
                    dve.wait_ge(den_step, 7 * i + (c + 1))
                    dve.tensor_tensor(es[:, two], negm[:, two], sink[:, two], ALU.add).then_inc(negm_ready, 1)

                def copy_t(c):
                    dve.wait_ge(pt_full, 4 * i + (c + 1))
                    dve.wait_ge(pv_done, 4 * i + c)
                    dve.tensor_copy(prob_t[:, 1, 0:wide], psum[:, 5, 0:wide]).then_inc(pt_dve, 1)

                largest(0)
                for c in range(1, 4):
                    largest(c)
                    copy_t(c - 1)
                copy_t(3)
                dve.wait_ge(es_ready, i + 1)
                dve.wait_ge(p_ready, 8 * i + 8)
                dve.tensor_tensor(den[:], rows[:], es[:], ALU.add).then_inc(den_step, 1)
                dve.wait_ge(den_step, 7 * i + 5)
                dve.reciprocal(rden[:], den[:]).then_inc(den_step, 1)
                dve.wait_ge(den_step, 7 * i + 6)
                dve.wait_ge(pv_done, 4 * i + 4)
                dve.wait_ge(y_full, i)
                dve.tensor_tensor(o_sb[:].rearrange("p (h w) -> p h w", w=HD),
                                  psum[:, 6, :].rearrange("p (h w) -> p h w", w=HD),
                                  rden[:].rearrange("p (h o) -> p h o", o=1).to_broadcast([P, HEADS, HD]),
                                  ALU.mult).then_inc(o_ready, 1)
                dve.wait_ge(y_high, i + 1)
                dve.sem_inc(den_step, 1)
                dve.tensor_tensor(s.hl[:, 4:8, cols], psum[:, 7, :].rearrange("p (c w) -> p c w", w=P),
                                  s.hh[:, 4:8, cols].bitcast(F32), ALU.subtract).then_inc(y_low, 1)
            block_of(0, slice(0, P), True)
            with dve.Fori(0, 8) as b:
                block_of(b + 1, ds(b * P + TP, P), False)


LEVELS = [2, 4, 8, 16, 32, 64]
NL = len(LEVELS)
NB = 3
SLOTS = NL * NB
(G_, GC_, EG_, EK_, EL_, BETA_, NBETA_) = range(7)


class Delta:

    def __init__(self, s):
        sb = s.placer("dn", s.x_at, s.rest + 74592)
        self.raw = {n: sb(f"raw_{n}", [P, T]) for n in "kqv"}
        self.silu_z = sb("silu_z", [P, T])
        self.kn, self.qn, self.vf = sb("kn", [P, T]), sb("qn", [P, T]), sb("vf", [P, T])
        self.k_tok, self.v_tok = sb("k_tok", [P, T]), sb("v_tok", [P, T])
        self.pt = [sb(f"pt{d}", [P, T]) for d in range(2)]
        self.wt = [sb(f"wt{d}", [P, T]) for d in range(2)]
        self.ub = [sb(f"ub{d}", [P, T]) for d in range(2)]
        self.qg = [sb(f"qg{d}", [P, T]) for d in range(2)]
        kd0 = sb("kd0", [P, T])
        self.kd = [kd0, self.k_tok]
        t0, tt0 = sb("t0", [P, T]), sb("tt0", [P, T])
        self.t, self.tt = [t0, self.vf], [tt0, self.raw["v"]]
        self.osum = sb("osum", [P, T])
        self.xl = [self.osum[:, i * TW:(i + 1) * TW] for i in range(2)]
        self.bm = [self.osum[:, 2 * TW:3 * TW], self.kn[:, 2 * TW:3 * TW]]
        self.fin = [self.kn[:, d * P:(d + 1) * P] for d in range(2)]
        self.vn = [self.kn[:, (3 + d) * P:(4 + d) * P] for d in range(2)]
        self.kk, self.qk = self.raw["k"], self.raw["q"]
        self.tok = sb("token_consts", [P, 7 * 2 * NT * DN_H])
        self.hs = sb("head_consts", [P, 7, 2, NT])
        self.level = sb("level_masks", [P, 2, NL + 1, P], BF16)
        self.low = sb("neg_masks", [P, 2, P], BF16)
        self.tri = sb("tri", [P, 2, P])
        self.state = [[sb(f"state{d}{i}", [P, P]) for i in range(2)] for d in range(2)]
        self.conv = sb("conv", [P, 24, 4])
        self.onorm = sb("onorm", [P, 1])


def decay_stage(s, dn):
    nc, psum, I, p0 = s.nc, s.psum, s.I, s.p0
    sb = s.placer("decay", s.rest, s.rest + 10 * 4 * T)
    gb, u, e, w, r, l = (sb(n, [48, T]) for n in ("gb", "u", "e", "w", "r", "l"))
    gb_tok = sb("gb_tok", [P, NT * 48])
    gl = sb("g_last", [P, 2, NT * DN_H])
    dts = sb("dt_bias", [16, 2])
    tok = dn.tok[:].rearrange("p (v d n) -> p v d n", v=7, d=2)
    with ExitStack() as ctx:
        def sem(name):
            return ctx.enter_context(nc.semaphore("decay_" + name))
        stored, loaded, act_step, dve_step, turned, sums, w_done = (
            sem(n) for n in ("stored", "loaded", "act_step", "dve_step", "turned", "sums", "scale_ready"))
        block = ctx.enter_context(nc.Block())

        @block.sync
        def _(sp):
            sp.dma_start(s.x_dram, s.x[:]).then_inc(stored, 16)
            sp.dma_start(dts[:], I["dts"]).then_inc(loaded, 16)
            sp.wait_ge(stored, 16)
            for t, name in ((dn.level, "level"), (dn.low, "low"), (dn.tri, "tri"), (dn.conv, "conv_dn"),
                            (dn.onorm, "onorm")):
                sp.dma_start(t[:], I[name]).then_inc(loaded, 16)
            s.sp_load(sp, p0 + 2, p0 % 2)

        @block.gpsimd
        def _(pool):
            s.pool_split(pool, p0 + 1, (p0 + 1) % 2)

        @block.tensor
        def _(pe):
            s.set_free.wait(pe, 1)
            pe_panel(s, pe, p0, p0 % 2, 0)
            pe.wait_ge(dve_step, 8)
            pe.wait_ge(act_step, 5)
            for n in range(NT):
                mm = pe.transpose(psum[:, 3, n * 48:(n + 1) * 48], gb[:, n * P:(n + 1) * P], s.ident[0:48, 0:48])
            mm.then_inc(turned, 1)
            pe.wait_ge(dve_step, 9)
            pe.wait_ge(loaded, 96)
            rhs = gb_tok[:].rearrange("p (n c) -> p n c", c=48)
            n = NT * DN_H
            for d in range(2):
                g = rhs[:, :, 8 * d:8 * d + 8]
                pe.matmul(psum[:, 4, d * n:(d + 1) * n], dn.tri[:, d, :], g, start=True, stop=True)
                mm = pe.matmul(psum[:, 5, d * n:(d + 1) * n], s.ones[:], g, start=True, stop=True)
            mm.then_inc(sums, 1)

        @block.scalar
        def _(act):
            s.act_split(act, p0 + 1, (p0 + 1) % 2)
            act.wait_ge(dve_step, 1)
            act.activation(e[0:16], u[0:16], ACT.Abs).then_inc(act_step, 1)
            act.wait_ge(act_step, 1)
            act.activation(e[0:16], e[0:16], ACT.Exp, scale=-1.0).then_inc(act_step, 1)
            act.wait_ge(loaded, 96)
            act.activation(dts[:, 1:2], dts[:, 1:2], ACT.Exp).then_inc(act_step, 1)
            act.wait_ge(dve_step, 2)
            act.activation(l[0:16], w[0:16], ACT.Ln).then_inc(act_step, 1)
            act.wait_ge(dve_step, 3)
            act.activation(tiled(gb[32:48]), banks(s, 0)[32:48], ACT.Sigmoid).then_inc(act_step, 1)
            act.wait_ge(sums, 1)
            n = NT * DN_H
            act.activation(tok[:, GC_], psum[:, 4, 0:2 * n].rearrange("p (d n) -> p d n", d=2), ACT.Copy
                           ).then_inc(act_step, 1)
            act.activation(gl[:], psum[:, 5, 0:2 * n].rearrange("p (d n) -> p d n", d=2), ACT.Copy,
                           scale=float(D)).then_inc(act_step, 1)
            act.wait_ge(act_step, 7)
            act.activation(tok[:, EG_], tok[:, GC_], ACT.Exp)
            act.activation(tok[:, EL_], gl[:], ACT.Exp)
            act.wait_ge(dve_step, 13)
            act.activation(tok[:, EK_], tok[:, EK_], ACT.Exp)

        @block.vector
        def _(dve):
            dve.wait_ge(s.panel_used.sem, p0 + 1)
            dve.wait_ge(loaded, 96)
            dve.tensor_scalar(tiled(u[0:16]), banks(s, 0)[0:16], dts[:, 0:1], None, ALU.add).then_inc(dve_step, 1)
            dve.wait_ge(act_step, 2)
            dve.tensor_scalar(w[0:16], e[0:16], 1.0, None, ALU.add).then_inc(dve_step, 1)
            dve.memset(gb[:], 0.0).then_inc(dve_step, 1)
            dve.wait_ge(dve_step, 3)
            dve.scalar_tensor_tensor(e[0:16], w[0:16], -1.0, e[0:16], ALU.add, ALU.subtract).then_inc(dve_step, 1)
            dve.reciprocal(r[0:16], w[0:16]).then_inc(dve_step, 1)
            dve.wait_ge(dve_step, 5)
            dve.tensor_tensor(e[0:16], e[0:16], r[0:16], ALU.mult).then_inc(dve_step, 1)
            dve.wait_ge(act_step, 4)
            dve.scalar_tensor_tensor(u[0:16], u[0:16], 0.0, l[0:16], ALU.max, ALU.add).then_inc(dve_step, 1)
            dve.wait_ge(dve_step, 7)
            dve.tensor_tensor(u[0:16], u[0:16], e[0:16], ALU.subtract)
            dve.tensor_scalar(dts[:, 1:2], dts[:, 1:2], -1.0, None, ALU.mult).then_inc(w_done, 1)
            dve.wait_ge(w_done, 1)
            dve.tensor_scalar(gb[0:16], u[0:16], dts[:, 1:2], None, ALU.mult).then_inc(dve_step, 1)
            dve.wait_ge(turned, 1)
            dve.tensor_copy(gb_tok[:], psum[:, 3, 0:NT * 48]).then_inc(dve_step, 1)
            dve.wait_ge(dve_step, 9)
            by = gb_tok[:].rearrange("p (n c) -> p n c", c=48)
            for d in range(2):
                for q, o, f in ((G_, 0, 1.0), (BETA_, 32, 1.0), (NBETA_, 32, -1.0)):
                    v = dve.tensor_scalar(tok[:, q, d].rearrange("p (n h) -> p n h", h=DN_H),
                                          by[:, :, o + 8 * d:o + 8 * d + 8], f, None, ALU.mult)
            v.then_inc(dve_step, 3)
            dve.wait_ge(act_step, 7)
            dve.tensor_tensor(tok[:, EK_], gl[:], tok[:, GC_], ALU.subtract).then_inc(dve_step, 1)
            dve.sem_inc(s.set_free.sem, 1)
    s.p0 += 1
    s.set_free.base += 1


def delta_stage(s, dn):
    nc, psum, I, p0 = s.nc, s.psum, s.I, s.p0
    READS, FULLS = 16, 12
    with ExitStack() as ctx:
        def sem(name):
            return ctx.enter_context(nc.semaphore("dn_" + name))
        head_ready, conv_step, silu_done, sq_ready, recip_done, normed = (
            sem(n) for n in ("head_ready", "conv_step", "silu_done", "sq_ready", "recip_done", "normed"))
        grp_read, grp_full = sem("grp_read"), sem("grp_full")
        e_read, e_ready, d_ready, bt_step, bt_ready, tt_init = (
            sem(n) for n in ("e_read", "e_ready", "d_ready", "bt_step", "bt_ready", "tt_init"))
        qg_ready, pt_ready, kg_ready, kd_ready, bm_ready = (
            sem(n) for n in ("qg_ready", "pt_ready", "kg_ready", "kd_ready", "bm_ready"))
        xl_full, xl_ready, d_full, t_upd, u_full, ub_ready = (
            sem(n) for n in ("xl_full", "xl_ready", "d_full", "t_upd", "u_full", "ub_ready"))
        s_loaded, ws_full, vn_ready, sn_full, s_ready, o_full, o_act, o_dve = (
            sem(n) for n in ("s_loaded", "ws_full", "vn_ready", "sn_full", "s_ready", "o_full", "o_act", "o_dve"))
        fin_full, fin_ready, fin_stored, osq_ready, post_full, post_std, post_step, y_done, y_stored = (
            sem(n) for n in ("fin_full", "fin_ready", "fin_stored", "osq_ready", "post_full", "post_std",
                             "post_step", "y_done", "y_stored"))
        block = ctx.enter_context(nc.Block())

        def blk(t, n):
            return t[:, n * P:(n + 1) * P]

        def by_block(t):
            return t[:].rearrange("p (n w) -> p n w", w=P)

        def of_group(g):
            return psum[:, 3 * g:3 * g + 3, 0:TW].rearrange("p b (n w) -> p b n w", w=P)

        def by_bank(t):
            return t[:].rearrange("p (b n w) -> p b n w", b=3, w=P)

        def const(q, d):
            return dn.hs[:, q, d, :].rearrange("p (n o) -> p n o", o=1).to_broadcast([P, NT, P])

        def const_b(q, d):
            return dn.hs[:, q, d, :].rearrange("p (b n o) -> p b n o", b=3, o=1).to_broadcast([P, 3, 3, P])

        def mask(m, n):
            return m.rearrange("p (o w) -> p o w", o=1).to_broadcast([P, n, P])

        def at_head(t, part, h, j):
            return t[:, ds(h + part * DN_H, 1), j:j + 1].rearrange("p a b -> p (a b)")

        PART = {"q": 0, "k": 1, "v": 2}

        @block.sync
        def _(sp):
            def head(h, last):
                for j in range(4):
                    s.sp_load(sp, 4 * h + (p0 + 2 + j), (p0 + j) % 2)
                if not (isinstance(h, int) and h == 0):
                    sp.wait_ge(o_full, 17 * h)
                for d in range(2):
                    sp.dma_start(dn.state[d][0][:], I["state_delta"][d, ds(h, 1)].rearrange("a p n -> p (a n)")
                                 ).then_inc(s_loaded, 16)
                sp.wait_ge(fin_ready, 2 * h + 2)
                for d in range(2):
                    sp.dma_start(s.O["delta"][ds(h, 1), d].rearrange("a p n -> p (a n)"), dn.fin[d]
                                 ).then_inc(fin_stored, 16)
                sp.wait_ge(y_done, h + 1)
                sp.dma_start(s.y_dram[:, ds(h, 1), :].rearrange("p a t -> p (a t)"), dn.osum[:]
                             ).then_inc(y_stored, 16)
            head(0, False)
            with sp.Fori(1, DN_H) as h:
                head(h, False)
            sp.wait_ge(fin_stored, 32 * DN_H)
            sp.wait_ge(y_stored, 16 * DN_H)

        @block.gpsimd
        def _(pool):
            def mul(out, a, b):
                return pool.tensor_tensor(out, a, b, ALU.mult)

            with pool.Fori(0, DN_H) as h:
                for j in range(4):
                    s.pool_split(pool, 4 * h + (p0 + 1 + j), (p0 + 1 + j) % 2)

                def prepare(d):
                    if d == 0:
                        pool.wait_ge(head_ready, h + 1)
                        pool.wait_ge(normed, 2 * h + 2)
                    pool.wait_ge(grp_read, READS * h + 8 + d)
                    mul(dn.qg[d][:], dn.qn[:], dn.wt[d][:]).then_inc(qg_ready, 1)
                    mul(by_block(dn.ub[d]), by_block(dn.k_tok), const(EG_, d)).then_inc(kg_ready, 1)
                    if d == 0:
                        mul(by_block(dn.kd[0]), by_block(dn.k_tok), const(EK_, 0)).then_inc(kd_ready, 1)
                    else:
                        pool.wait_ge(kg_ready, 2 * h + 2)
                        pool.wait_ge(kd_ready, 2 * h + 1)
                        mul(by_block(dn.kd[1]), by_block(dn.k_tok), const(EK_, 1)).then_inc(kd_ready, 1)

                def decayed(d):
                    pool.wait_ge(d_ready, 2 * h + (d + 1))
                    pool.wait_ge(grp_read, READS * h + 11)
                    pool.wait_ge(bt_ready, 2 * h + (d + 1))
                    mul(dn.pt[d][:], dn.pt[d][:], dn.qk[:]).then_inc(pt_ready, 1)

                def masked(d, c):
                    n = 36 * h + (18 * d + c)
                    if c or d:
                        pool.wait_ge(xl_full, n - 1)
                    if c == 1 and d == 0:
                        pool.wait_ge(grp_full, FULLS * h + 7)
                    g = c % 3
                    cols = slice(g * TW, (g + 1) * TW)
                    mul(dn.bm[c % 2].rearrange("p (n w) -> p n w", w=P),
                        dn.wt[d][:, cols].rearrange("p (n w) -> p n w", w=P),
                        mask(dn.level[:, d, 1 + c // 3, :], 3)).then_inc(bm_ready, 1)

                prepare(0)
                pool.wait_ge(bt_ready, 2 * h + 1)
                masked(0, 0)
                masked(0, 1)
                decayed(0)
                for c in range(2, SLOTS):
                    if c == 6:
                        prepare(1)
                    masked(0, c)
                pool.wait_ge(bt_ready, 2 * h + 2)
                masked(1, 0)
                masked(1, 1)
                decayed(1)
                for c in range(2, SLOTS):
                    masked(1, c)

        @block.tensor
        def _(pe):
            def head(h):
                first = isinstance(h, int)

                def panel(j, g):
                    pe_panel(s, pe, 4 * h + (p0 + j), (p0 + j) % 2, g)

                def read(n):
                    pe.wait_ge(grp_read, READS * h + n)

                def sums(g, t):
                    for i in range(TT):
                        mm = pe.matmul(psum[:, 3 * g + i, 0:TW], s.ones[:], t[:, i * TW:(i + 1) * TW],
                                       start=True, stop=True)
                    return mm

                def nine(g, lhs, rhs, turn=False):
                    for n in range(NT):
                        out = psum[:, 3 * g + n // 3, (n % 3) * P:(n % 3 + 1) * P]
                        if turn:
                            mm = pe.transpose(out, blk(lhs, n), s.ident[:])
                        else:
                            mm = pe.matmul(out, lhs(n), rhs(n), start=True, stop=True)
                    return mm

                pe.wait_ge(post_std, h)
                panel(0, 0)
                panel(1, 1)
                read(1)
                pe.wait_ge(sq_ready, 2 * h + 1)
                sums(0, dn.osum).then_inc(grp_full, 1)
                read(2)
                panel(2, 1)
                read(3)
                pe.wait_ge(sq_ready, 2 * h + 2)
                sums(0, dn.t[0]).then_inc(grp_full, 1)
                read(4)
                pe.wait_ge(normed, 2 * h + 1)
                nine(1, dn.kn, None, True).then_inc(grp_full, 1)
                read(5)
                nine(0, lambda n: blk(dn.kn, n), lambda n: blk(dn.kn, n)).then_inc(grp_full, 1)
                pe.wait_ge(head_ready, h + 1)
                for d in range(2):
                    read(6 + d)
                    nine(1 - d, lambda n: dn.hs[:, G_, d, n:n + 1].to_broadcast([P, P]),
                         lambda n: dn.tri[:, d, :]).then_inc(grp_full, 1)
                read(8)
                pe.wait_ge(e_read, 2 * h + 1)
                panel(3, 1)
                read(9)
                pe.wait_ge(e_read, 2 * h + 2)
                pe.wait_ge(normed, 2 * h + 2)
                nine(0, lambda n: blk(dn.kn, n), lambda n: blk(dn.qn, n)).then_inc(grp_full, 1)
                read(10)
                pe.wait_ge(silu_done, 3 * h + 3)
                nine(1, dn.vf, None, True).then_inc(grp_full, 1)

                def levels(d):
                    read(11 if d == 0 else 13)
                    if d == 1:
                        pe.wait_ge(t_upd, 36 * h + 18)
                    pe.wait_ge(tt_init, 2 * h + (d + 1))
                    nine(0, dn.tt[d], None, True).then_inc(grp_full, 1)
                    read(13 + d)

                    def x_of(c):
                        n = 36 * h + (18 * d + c)
                        g = c % 3
                        pe.wait_ge(bm_ready, n + 1)
                        if c >= 3:
                            pe.wait_ge(t_upd, n - 2)
                        if d or c >= 2:
                            pe.wait_ge(xl_ready, n - 1)
                        for i in range(3):
                            mm = pe.matmul(psum[:, 6 + c % 2, i * P:(i + 1) * P],
                                           dn.bm[c % 2][:, i * P:(i + 1) * P], blk(dn.t[d], 3 * g + i),
                                           start=True, stop=True)
                        mm.then_inc(xl_full, 1)

                    def d_of(c):
                        g = c % 3
                        pe.wait_ge(xl_ready, 36 * h + (18 * d + c + 1))
                        for i in range(3):
                            x = dn.xl[c % 2][:, i * P:(i + 1) * P]
                            if c < SLOTS - NB:
                                pe.matmul(psum[:, g, i * P:(i + 1) * P], blk(dn.tt[d], 3 * g + i), x,
                                          start=True, stop=True)
                            mm = pe.matmul(psum[:, 3 + g, i * P:(i + 1) * P], x, blk(dn.tt[d], 3 * g + i),
                                           start=True, stop=True)
                        mm.then_inc(d_full, 1)
                    x_of(0)
                    for c in range(1, SLOTS):
                        x_of(c)
                        d_of(c - 1)
                    d_of(SLOTS - 1)

                levels(0)
                levels(1)
                for d in range(2):
                    if d == 0:
                        pe.wait_ge(t_upd, 36 * h + 36)
                    else:
                        read(15)
                        pe.wait_ge(ub_ready, 2 * h + 1)
                    pe.wait_ge(kg_ready, 2 * h + (d + 1))
                    nine(0, lambda n: blk(dn.ub[d], n), lambda n: blk(dn.tt[d], n)).then_inc(grp_full, 1)
                    nine(1, lambda n: blk(dn.tt[d], n), lambda n: blk(dn.v_tok, n)).then_inc(u_full, 1)
                read(16)
                pe.wait_ge(ub_ready, 2 * h + 2)
                pe.wait_ge(kd_ready, 2 * h + 2)
                pe.wait_ge(pt_ready, 2 * h + 2)
                pe.wait_ge(qg_ready, 2 * h + 2)
                for d in range(2):
                    mm = pe.matmul(psum[:, 4, 0:P], blk(dn.ub[d], 0), blk(dn.pt[d], 0), start=d == 0, stop=d == 1)
                mm.then_inc(o_full, 1)
                for d in range(2):
                    mm = pe.matmul(psum[:, 1 + 2 * d, 0:P], blk(dn.kd[d], 0), blk(dn.ub[d], 0),
                                   start=True, stop=True)
                mm.then_inc(fin_full, 1)
                pe.wait_ge(s_loaded, 32 * h + 32)
                for t in range(8):
                    n_of = (1 + t, 8 - t)
                    for d in range(2):
                        if t:
                            pe.wait_ge(s_ready, 14 * h + (2 * t - 1 + d))
                        pe.matmul(psum[:, 2 * d, 0:P], blk(dn.wt[d], n_of[d]), dn.state[d][t % 2][:],
                                  start=True, stop=True).then_inc(ws_full, 1)
                    for d in range(2):
                        k = 1 + 2 * t + d
                        if k >= 4:
                            j = k - 4
                            if j < 9:
                                pe.wait_ge(o_act, 9 * h + (j + 1))
                            else:
                                pe.wait_ge(o_dve, 8 * h + (j - 8))
                        pe.matmul(psum[:, 4 + k % 4, 0:P], dn.state[d][t % 2][:], blk(dn.qg[d], n_of[d]),
                                  start=True, stop=False)
                    for d in range(2):
                        k = 1 + 2 * t + d
                        pe.wait_ge(vn_ready, 16 * h + (2 * t + d + 1))
                        if t < 7:
                            if t == 0:
                                pe.wait_ge(fin_ready, 2 * h + 2)
                            pe.matmul(psum[:, 1 + 2 * d, 0:P], blk(dn.kd[d], n_of[d]), dn.vn[d],
                                      start=True, stop=True).then_inc(sn_full, 1)
                        pe.matmul(psum[:, 4 + k % 4, 0:P], dn.vn[d], blk(dn.pt[d], n_of[d]),
                                  start=False, stop=True).then_inc(o_full, 1)
                pe.wait_ge(osq_ready, h + 1)
                sums(0, dn.t[0]).then_inc(post_full, 1)
            with pe.Fori(0, DN_H) as h:
                head(h)

        @block.scalar
        def _(act):
            with act.Fori(0, DN_H) as h:
                def split(j):
                    s.act_split(act, 4 * h + (p0 + j), (p0 + j) % 2)

                def used(j):
                    act.wait_ge(s.panel_used.sem, 4 * h + (p0 + j + 1))

                def full(n):
                    act.wait_ge(grp_full, FULLS * h + n)

                def take(out, g, func=ACT.Copy, **kw):
                    return act.activation(tiled(out[:]), banks(s, g), func, **kw).then_inc(grp_read, 1)

                def silu(n, t, sq):
                    act.wait_ge(conv_step, 21 * h + 7 * n)
                    act.activation(t[:], t[:], ACT.Silu).then_inc(silu_done, 1)
                    if sq is not None:
                        act.wait_ge(silu_done, 3 * h + n)
                        act.activation(sq[:], t[:], ACT.Square).then_inc(sq_ready, 1)

                split(1)
                used(0)
                take(dn.raw["k"], 0)
                split(2)
                act.wait_ge(y_stored, 16 * h)
                silu(1, dn.kn, dn.osum)
                used(1)
                take(dn.raw["q"], 1)
                split(3)
                full(1)
                take(dn.osum, 0, ACT.Sqrt, scale=float(D), bias=s.eps[:, 0:1])
                silu(2, dn.qn, dn.t[0])
                used(2)
                act.wait_ge(y_done, h)
                take(dn.silu_z, 1, ACT.Silu)
                split(4)
                full(2)
                take(dn.t[0], 0, ACT.Sqrt, scale=float(D), bias=s.eps[:, 0:1])
                full(3)
                take(dn.k_tok, 1)
                full(4)
                take(dn.kk, 0)
                for d in range(2):
                    full(5 + d)
                    take(dn.wt[d], 1 - d, ACT.Exp)
                for d in range(2):
                    act.wait_ge(e_ready, 2 * h + (d + 1))
                    act.activation(dn.pt[d][:], dn.pt[d][:], ACT.Exp).then_inc(d_ready, 1)
                used(3)
                take(dn.raw["v"], 1)
                silu(3, dn.vf, None)
                full(7)
                take(dn.qk, 0)
                full(8)
                take(dn.v_tok, 1)
                full(9)
                take(dn.t[0], 0)

                def x_copies(d):
                    for c in range(SLOTS):
                        n = 36 * h + (18 * d + c)
                        act.wait_ge(xl_full, n + 1)
                        if d or c >= 2:
                            act.wait_ge(d_full, n - 1)
                        act.activation(dn.xl[c % 2], psum[:, 6 + c % 2, 0:TW], ACT.Copy).then_inc(xl_ready, 1)
                x_copies(0)
                full(10)
                take(dn.t[1], 0)
                x_copies(1)
                for d in range(2):
                    full(11 + d)
                    take(dn.wt[d], 0)
                act.wait_ge(o_full, 17 * h + 1)
                act.activation(blk(dn.osum, 0), psum[:, 4, 0:P], ACT.Copy).then_inc(o_act, 1)
                act.wait_ge(fin_full, h + 1)
                for d in range(2):
                    act.activation(dn.fin[d], psum[:, 1 + 2 * d, 0:P], ACT.Copy).then_inc(fin_ready, 1)
                for t in range(4):
                    for d in range(2):
                        k = 1 + 2 * t + d
                        act.wait_ge(o_full, 17 * h + (k + 1))
                        act.activation(blk(dn.osum, (1 + t, 8 - t)[d]), psum[:, 4 + k % 4, 0:P], ACT.Copy
                                       ).then_inc(o_act, 1)
                act.wait_ge(o_dve, 8 * h + 8)
                act.activation(dn.t[0][:], dn.osum[:], ACT.Square).then_inc(osq_ready, 1)
                act.wait_ge(post_full, h + 1)
                act.activation(tiled(dn.tt[0][:]), banks(s, 0), ACT.Sqrt, scale=float(D // P),
                               bias=s.eps[:, 0:1]).then_inc(post_std, 1)

        @block.vector
        def _(dve):
            tok = dn.tok[:].rearrange("p (v h) -> p v h", h=DN_H)
            with dve.Fori(0, DN_H) as h:
                dve.tensor_copy(dn.hs[:].rearrange("p a d n -> p (a d n)"),
                                tok[:, :, ds(h, 1)].rearrange("p v a -> p (v a)")).then_inc(head_ready, 1)

                def conv(n, name, out, reads):
                    part, x = PART[name], dn.raw[name]
                    dve.wait_ge(grp_read, READS * h + reads)
                    base = 21 * h + 7 * n
                    dve.tensor_scalar(out[:], x[:], at_head(dn.conv, part, h, 2), None, ALU.mult
                                      ).then_inc(conv_step, 1)
                    for i, (tap, off) in enumerate(((0, -2), (1, -1), (3, 1))):
                        for m, (lo, hi) in enumerate(((0, TP), (TP, T))):
                            a, b = (lo - off, hi) if off < 0 else (lo, hi - off)
                            dve.wait_ge(conv_step, base + (2 * i + m + 1 if i else 1))
                            dve.scalar_tensor_tensor(out[:, a:b], x[:, a + off:b + off],
                                                     at_head(dn.conv, part, h, tap), out[:, a:b],
                                                     ALU.mult, ALU.add).then_inc(conv_step, 1)

                def norm(n, std, t, scale, reads):
                    dve.wait_ge(grp_read, READS * h + reads)
                    dve.reciprocal(std[:], std[:]).then_inc(recip_done, 1)
                    dve.wait_ge(recip_done, 2 * h + n)
                    dve.scalar_tensor_tensor(t[:], t[:], scale, std[:], ALU.mult, ALU.mult).then_inc(normed, 1)

                dve.wait_ge(fin_stored, 32 * h)
                conv(0, "k", dn.kn, 1)
                conv(1, "q", dn.qn, 2)
                norm(1, dn.osum, dn.kn, 1.0, 3)
                norm(2, dn.t[0], dn.qn, P ** -0.5, 5)

                def decay(d):
                    dve.wait_ge(grp_read, READS * h + 8 + d)
                    dve.tensor_tensor(by_bank(dn.pt[d]), of_group(1 - d), const_b(GC_, d), ALU.subtract
                                      ).then_inc(e_read, 1)
                    dve.wait_ge(e_read, 2 * h + (d + 1))
                    dve.tensor_tensor(by_block(dn.pt[d]), by_block(dn.pt[d]), mask(dn.low[:, d, :], NT), ALU.min
                                      ).then_inc(e_ready, 1)

                def kk_beta(d):
                    dve.wait_ge(qg_ready, 2 * h + (d + 1))
                    dve.wait_ge(d_ready, 2 * h + (d + 1))
                    dve.tensor_tensor(dn.wt[d][:], dn.pt[d][:], dn.kk[:], ALU.mult).then_inc(bt_step, 1)
                    dve.wait_ge(bt_step, 4 * h + (2 * d + 1))
                    dve.tensor_tensor(by_block(dn.wt[d]), by_block(dn.wt[d]), const(BETA_, d), ALU.mult
                                      ).then_inc(bt_ready, 1)

                def t_start(d):
                    dve.wait_ge(bt_ready, 2 * h + (d + 1))
                    dve.tensor_tensor(by_block(dn.tt[d]), by_block(dn.wt[d]), mask(dn.level[:, d, 0, :], NT),
                                      ALU.mult).then_inc(bt_step, 1)
                    dve.wait_ge(bt_step, 4 * h + (2 * d + 2))
                    dve.tensor_tensor(by_block(dn.tt[d]), mask(s.ident[:], NT), by_block(dn.tt[d]), ALU.subtract
                                      ).then_inc(tt_init, 1)

                decay(0)
                decay(1)
                kk_beta(0)
                t_start(0)
                conv(2, "v", dn.vf, 10)
                for d in range(2):
                    for c in range(SLOTS):
                        n = 36 * h + (18 * d + c)
                        g = c % 3
                        cols = slice(g * TW, (g + 1) * TW)
                        dve.wait_ge(d_full, n + 1)
                        if c < SLOTS - NB:
                            dve.tensor_tensor(dn.t[d][:, cols], dn.t[d][:, cols], psum[:, g, 0:TW], ALU.subtract)
                        dve.tensor_tensor(dn.tt[d][:, cols], dn.tt[d][:, cols], psum[:, 3 + g, 0:TW],
                                          ALU.subtract).then_inc(t_upd, 1)
                        if d == 0 and c == 9:
                            kk_beta(1)
                        if d == 0 and c == 12:
                            t_start(1)
                for d in range(2):
                    dve.wait_ge(u_full, 2 * h + (d + 1))
                    dve.tensor_tensor(by_bank(dn.ub[d]), of_group(1), const_b(BETA_, d), ALU.mult
                                      ).then_inc(ub_ready, 1)
                for t in range(8):
                    n_of = (1 + t, 8 - t)
                    for d in range(2):
                        n = n_of[d]
                        dve.wait_ge(ws_full, 16 * h + (2 * t + d + 1))
                        if t:
                            dve.wait_ge(o_full, 17 * h + (2 * t + d))
                        else:
                            dve.wait_ge(ub_ready, 2 * h + 2)
                        dve.scalar_tensor_tensor(dn.vn[d], psum[:, 2 * d, 0:P], dn.hs[:, NBETA_, d, n:n + 1],
                                                 blk(dn.ub[d], n), ALU.mult, ALU.add).then_inc(vn_ready, 1)
                    if t < 7:
                        for d in range(2):
                            n = n_of[d]
                            dve.wait_ge(sn_full, 14 * h + (2 * t + d + 1))
                            if t:
                                dve.wait_ge(s_ready, 14 * h + (2 * t + d - 1))
                            dve.scalar_tensor_tensor(dn.state[d][(t + 1) % 2][:], dn.state[d][t % 2][:],
                                                     dn.hs[:, EL_, d, n:n + 1], psum[:, 1 + 2 * d, 0:P],
                                                     ALU.mult, ALU.add).then_inc(s_ready, 1)
                    if t >= 4:
                        for d in range(2):
                            k = 1 + 2 * t + d
                            dve.wait_ge(o_full, 17 * h + (k + 1))
                            dve.wait_ge(o_act, 9 * h + 9)
                            o = blk(dn.osum, n_of[d])
                            dve.tensor_tensor(o, o, psum[:, 4 + k % 4, 0:P], ALU.add).then_inc(o_dve, 1)
                dve.wait_ge(post_std, h + 1)
                dve.reciprocal(dn.tt[0][:], dn.tt[0][:]).then_inc(post_step, 1)
                dve.wait_ge(post_step, 2 * h + 1)
                dve.scalar_tensor_tensor(dn.osum[:], dn.osum[:], dn.onorm[:, 0:1], dn.tt[0][:], ALU.mult, ALU.mult
                                         ).then_inc(post_step, 1)
                dve.wait_ge(post_step, 2 * h + 2)
                dve.tensor_tensor(dn.osum[:], dn.osum[:], dn.silu_z[:], ALU.mult).then_inc(y_done, 1)
    s.p0 += ODD_PANELS


def reload_stage(s):
    nc = s.nc
    with ExitStack() as ctx:
        x_in = ctx.enter_context(nc.semaphore("x_in"))
        y_in = ctx.enter_context(nc.semaphore("y_in"))
        high = ctx.enter_context(nc.semaphore("y_high"))
        y = s.at("y_delta", [P, KC, T], F32, s.rest)
        block = ctx.enter_context(nc.Block())

        @block.sync
        def _(sp):
            sp.dma_start(y[:], s.y_dram).then_inc(y_in, 16)
            sp.dma_start(s.x[:], s.x_dram).then_inc(x_in, 16)
            sp.wait_ge(x_in, 16)

        @block.scalar
        def _(act):
            act.wait_ge(y_in, 16)
            for c in range(KC):
                act.activation(s.hh[:, c, :], y[:, c, :], ACT.Copy).then_inc(high, 1)

        @block.vector
        def _(dve):
            for c in range(KC):
                dve.wait_ge(high, c + 1)
                dve.tensor_tensor(s.hl[:, c, :], y[:, c, :], s.hh[:, c, :].bitcast(F32), ALU.subtract)


def pack_delta(f):
    bf = mybir.dt.np(BF16)
    i = np.arange(P)
    j, c = i[:, None], i[None, :]
    level = np.zeros((P, 2, NL + 1, P), np.float32)
    for n, b in enumerate([1] + LEVELS):
        pair = (j // (2 * b) == c // (2 * b)) & (j // b % 2 == 0) & (c // b % 2 == 1)
        level[:, 0, n], level[:, 1, n] = pair, pair.T
    low = np.stack([np.where(j <= c, 0, NEG), np.where(j >= c, 0, NEG)], 1)
    tri = np.stack([j <= c, j >= c], 1).astype(np.float32)
    return {
        "level": level.astype(bf), "low": low.astype(bf), "tri": tri,
        "dts": np.stack([f["dn_dt_bias"][0].reshape(16), f["dn_a_log"][0].reshape(16)], 1),
        "conv_dn": columns(f["conv_dn"][0]).transpose(0, 2, 1),
        "onorm": f["dn_o_norm"][0][:, None],
        "state_delta": f["state_delta"][0, 0],
    }


def build(nc, I, O):
    with ExitStack() as ctx:
        s = Trunk(nc, ctx, I, O)
        load_stage(s)
        norm_stage(s, 0, 0)
        even = even_buffer(s)
        in_proj_stage(s, even, EVEN_PANELS)
        rg_stage(s, even)
        attention_stage(s, even)
        out_proj_stage(s, 0)
        norm_stage(s, 0, 1)
        ffn_stage(s, 0)
        norm_stage(s, 1, 0)
        s.x_dram = nc.dram_tensor("x_spill", [P, KC, T], F32).ap()
        s.y_dram = nc.dram_tensor("y_spill", [P, KC, T], F32).ap()
        dn = Delta(s)
        decay_stage(s, dn)
        delta_stage(s, dn)
        reload_stage(s)
        out_proj_stage(s, 1)
        norm_stage(s, 1, 1)
        ffn_stage(s, 1)
        final_stage(s)


def feature_major(a):
    return np.asarray(a).T.reshape(-1, P, a.shape[0]).transpose(1, 0, 2)


def columns(v):
    v = np.asarray(v)
    return np.moveaxis(v.reshape(*v.shape[:-1], -1, P), -1, 0)


def panels(w):
    w = np.asarray(w)
    return w.reshape(KC, P, -1, P).transpose(2, 1, 0, 3).reshape(-1, P, 1024)


def pack(inp):
    f = {k: np.asarray(v) for k, v in inp.items()}
    qperm = np.concatenate([np.arange(HD) + HD * h for c in range(4) for h in (c, c + 4)])
    w_in = f["w_in_even"][0]
    w_in = np.concatenate([w_in[:, :1024], w_in[:, 1024:1536][:, qperm], w_in[:, 1536:]], axis=1)
    w_out = f["w_out_even"][0]
    w_out = np.concatenate([w_out[:512], w_out[512:][qperm]], axis=0)
    stream = [panels(w_in), panels(w_out)]

    def ffn(layer):
        gate_up = panels(f["w_gu"][layer])
        down = f["w_down"][layer].reshape(FF_CH, P, D)
        order = []
        for c in range(FF_CH):
            order += [gate_up[c], gate_up[FF_CH + c]]
            if c:
                order.append(down[c - 1])
        return np.stack(order + [down[FF_CH - 1]])

    stream.append(ffn(0))
    w_odd = f["w_in_odd"][0]
    ab = w_odd[:, 4096:].reshape(D, 2, 16)
    ab_panel = np.zeros((D, P), np.float32)
    ab_panel[:, 0:16], ab_panel[:, 32:48] = ab[:, 0], ab[:, 1]
    stream.append(panels(ab_panel))
    heads = panels(w_odd[:, :4096]).reshape(4, DN_H, P, 1024)[[1, 0, 3, 2]]
    stream.append(heads.transpose(1, 0, 2, 3).reshape(-1, P, 1024))
    stream += [panels(f["w_out_odd"][0]), ffn(1), np.zeros((PAD, P, 1024), np.float32)]

    rgw = np.zeros((RG_CH, P, 4, P), np.float32)
    for d in range(2):
        for j, w in enumerate((f["rg_wa"], f["rg_wx"])):
            for b in range(8):
                o = 64 * (b % 2)
                rgw[b // 2, o:o + 64, 2 * d + j, o:o + 64] = w[0, d, b]
    rgb = np.stack([f["rg_ba"][0], f["rg_bx"][0]], axis=1).reshape(4, 512)
    i = np.arange(P)
    prev = np.where(i[None, :] >= i[:, None], 0, NEG).astype(np.float32)
    nxt = np.where(i[None, :] <= i[:, None], 0, NEG).astype(np.float32)
    none = np.full((P, P), NEG, np.float32)
    window = np.stack([np.stack([none if b == 0 else prev, none if b == 7 else nxt], 1) for b in range(8)], 1)
    inv = ROPE_BASE ** (-np.arange(0, 32, 2, dtype=np.float32) / 32)
    tok = np.arange(TL)
    ang = [(tok // GRID_W)[None].astype(np.float32) * inv[:, None],
           (tok % GRID_W)[None].astype(np.float32) * inv[:, None]]
    ang = np.concatenate([ang[0], ang[0], ang[1], ang[1]] * 2).astype(np.float32)
    rope = np.zeros((P, P), np.float32)
    for m in range(P):
        if m % 32 < 16:
            rope[m + 16, m] = -1.0
        else:
            rope[m - 16, m] = 1.0
    head_of = [h for c in range(4) for h in (c, c + 4)]
    bf = mybir.dt.np(BF16)
    return {
        "x": feature_major(np.concatenate([f["x_prompt"][0], f["x_sample"][0]])),
        "cond": columns(np.stack([f["c_ctx"], f["c"][0]])).transpose(0, 2, 1),
        "stream": np.concatenate(stream),
        "wmod": np.concatenate([panels(w) for w in f["w_mod"]]),
        "bmod": columns(f["b_mod"].reshape(-1)),
        "gain": columns(np.stack([f["g_mix"][0], f["g_ffn"][0], f["g_mix"][1], f["g_ffn"][1], f["g_final"]])),
        "ones": np.full((P, P), 1.0 / D, np.float32),
        "ident": np.eye(P, dtype=np.float32),
        "eps": np.full((P, 1), EPS, np.float32),
        "conv_rg": columns(np.concatenate([f["conv_rg"][0], f["conv_rg_b"]])).transpose(0, 2, 1),
        "rgw": rgw.reshape(RG_CH, P, 4 * P),
        "rgb": columns(rgb).transpose(0, 2, 1),
        "lam": columns(f["rg_lam"][0]).transpose(0, 2, 1),
        "h0": columns(f["state_rglru"][0, 0]).transpose(0, 2, 1),
        "ctx_k": f["cache_attn_k"][0, 0].reshape(TP, P).T,
        "ctx_v": f["cache_attn_v"][0, 0].reshape(TP, P),
        "sink": np.broadcast_to(f["attn_sink"][0][head_of], (P, HEADS)),
        "window": window.astype(bf),
        "ident_bf": np.eye(P, dtype=bf),
        "cos": np.cos(ang), "sin": np.sin(ang), "rope": rope,
    } | pack_delta(f)


def kernel(**inputs):
    import concourse.bacc as bacc
    from concourse.bass_utils import run_bass_kernel_spmd

    arrays = {f"in_{k}": np.ascontiguousarray(v) for k, v in pack(inputs).items()}
    nc = bacc.Bacc("TRN2", target_bir_lowering=False, num_devices=1)
    I = {k[3:]: nc.dram_tensor(k, v.shape, mybir.dt.from_np(v.dtype), kind="ExternalInput").ap()
         for k, v in arrays.items()}
    O = {k: nc.dram_tensor(f"out_{k}", shape, F32, kind="ExternalOutput").ap() for k, shape in OUTS.items()}
    build(nc, I, O)
    r = run_bass_kernel_spmd(nc, [arrays], core_ids=[0]).results[0]
    return unpack({k: r[f"out_{k}"] for k in OUTS})


OUTS = {"y": (P, KC, T), "k": (P, TP), "v": (P, TP), "rg": (P, RG_CH, 2), "delta": (DN_H, 2, P, P)}


def unpack(r):
    y = r["y"].transpose(2, 1, 0).reshape(T, D)
    kv = [r[n].T.reshape(1, 1, TP, 2, HD) for n in ("k", "v")]
    rg = r["rg"].transpose(2, 1, 0).reshape(1, 1, 2, 512)
    delta = r["delta"].transpose(1, 0, 2, 3).reshape(1, 1, 2, DN_H, P, P)
    return (y[None, :TP], y[None, TP:], *(np.ascontiguousarray(a) for a in (*kv, rg, delta)))
```

```python
from contextlib import ExitStack

import numpy as np

import concourse.bass as bass
from concourse import mybir

F32 = mybir.dt.float32
F32R = mybir.dt.float32r
BF16 = mybir.dt.bfloat16
ACT = mybir.ActivationFunctionType
ALU = mybir.AluOpType
AX = mybir.AxisListType
ds = bass.ds

P = 128
D = 1024
KC = D // P
TP = 128
TL = 1024
T = TP + TL
NT = T // P
TW = 384
TT = T // TW
EPS = 1e-6
NEG = -1e30
RG_CH = 4
RG_C = 8.0
HD = 64
HEADS = 8
GRID_W = 64
ROPE_BASE = 10000.0
DN_H = 8
FF_CH = 22
FF_G = FF_CH // 2
EVEN_PANELS = 14
ODD_PANELS = 4 * DN_H
OUT_PANELS = 8
FFN_PANELS = 6 * FF_G
STREAM = EVEN_PANELS + OUT_PANELS + FFN_PANELS + 1 + ODD_PANELS + OUT_PANELS + FFN_PANELS
PAD = 2
SH1, SC1, GA1, SH2, SC2, GA2 = range(6)


def three_products(pe, out, wh, wl, xh, xl, first, last):
    pe.matmul(out, wh, xh, start=first, stop=False)
    pe.matmul(out, wh, xl, start=False, stop=False)
    return pe.matmul(out, wl, xh, start=False, stop=last)


class Count:

    def __init__(self, nc, ctx, name):
        self.sem = ctx.enter_context(nc.semaphore(name))
        self.base = 0

    def wait(self, eng, n):
        eng.wait_ge(self.sem, n + self.base)


class Trunk:

    def __init__(self, nc, ctx, I, O):
        self.nc, self.ctx, self.I, self.O = nc, ctx, I, O
        self.top = (nc.sbuf_base + 31) // 32 * 32

        def sb(name, shape, dt=F32):
            t = self.at(name, shape, dt, self.top)
            self.top = (self.top + self.size(shape, dt) + 31) // 32 * 32
            return t

        self.psum = ctx.enter_context(nc.psum_tensor("psum", [P, 8, 512], F32))
        self.mod = sb("mod", [P, 96, 2])
        self.gain = sb("gain", [P, 5, KC])
        self.ones = sb("ones", [P, P])
        self.ident = sb("ident", [P, P])
        self.onep = sb("one_plus_scale", [P, KC, 2])
        self.eps = sb("eps", [P, 1])
        self.acc = sb("mod_sums", [P, 2, 2])
        self.raw = [sb(f"panel_raw{i}", [P, 1024]) for i in range(2)]
        self.wh = [sb(f"panel_high{i}", [P, 1024], F32R) for i in range(2)]
        self.wl = [sb(f"panel_low{i}", [P, 1024], F32R) for i in range(2)]
        self.h_at = self.top
        self.hh = sb("h_high", [P, KC, T], F32R)
        self.hl = sb("h_low", [P, KC, T], F32R)
        self.x_at = self.top
        self.x = sb("x", [P, KC, T])
        self.rest = self.top
        self.hi_chunk = self.h_at
        self.lo_chunk = self.h_at + 4 * KC * T

        def count(name, credit=0):
            c = Count(nc, ctx, name)
            c.credit = credit
            self.counts.append(c)
            return c

        self.counts = []
        self.raw_full = [count(f"raw_full{i}") for i in range(2)]
        self.split_high = count("split_high")
        self.split_low = count("split_low")
        self.panel_used = count("panel_used")
        self.p0 = 0
        self.modvec_ready = count("modvec_ready")
        self.squared = count("squared")
        self.mean_ready = count("mean_ready")
        self.std_ready = count("std_ready")
        self.rstd_ready = count("rstd_ready")
        self.normed = count("normed")
        self.high_ready = count("high_ready")
        self.low_ready = count("low_ready")
        self.set_free = count("set_free", 2)
        self.gate_ready = count("gate_ready")
        self.prod_ready = count("prod_ready")
        self.mid_high = count("mid_high")
        self.mid_low = count("mid_low")
        self.added = count("added", 2)
        self.down_full = count("down_full")
        self.mod_full = [count(f"mod_full{i}") for i in range(2)]
        self.mod_step = count("mod_step")

    def at(self, name, shape, dt, offset):
        return self.nc.alloc_sbuf_tensor_at(name, shape, dt, offset=offset)

    @staticmethod
    def size(shape, dt=F32):
        n = 2 if dt == BF16 else 4
        for x in shape[1:]:
            n *= x
        return n

    def placer(self, stage, offset, end):
        where = [offset]

        def sb(name, shape, dt=F32):
            t = self.at(f"{stage}_{name}", shape, dt, where[0])
            where[0] = (where[0] + self.size(shape, dt) + 31) // 32 * 32
            assert where[0] <= end, (stage, name, where[0] - end)
            return t
        return sb

    def sp_load(self, sp, p, buf):
        sp.wait_ge(self.split_low.sem, p - 1)
        src = self.I["stream"][p] if isinstance(p, int) else self.I["stream"][ds(p, 1)].rearrange("a p n -> p (a n)")
        sp.dma_start(self.raw[buf][:], src).then_inc(self.raw_full[buf].sem, 16)

    def sp_stream(self, sp, n):
        p0 = self.p0
        with sp.Fori(0, n // 2) as g:
            for i in range(2):
                self.sp_load(sp, 2 * g + (p0 + 2 + i), (p0 + i) % 2)
        if n % 2:
            self.sp_load(sp, p0 + n + 1, (p0 + n + 1) % 2)

    def act_split(self, act, p, buf):
        act.wait_ge(self.raw_full[buf].sem, (p + (2 - buf)) * 8)
        if not (isinstance(p, int) and p < 2):
            act.wait_ge(self.panel_used.sem, p - 1)
        act.activation(self.wh[buf][:], self.raw[buf][:], ACT.Copy).then_inc(self.split_high.sem, 1)

    def pool_split(self, pool, p, buf):
        pool.wait_ge(self.split_high.sem, p + 1)
        pool.tensor_tensor(self.wl[buf][:], self.raw[buf][:], self.wh[buf][:].bitcast(F32),
                           ALU.subtract).then_inc(self.split_low.sem, 1)

    def pool_stream(self, pool, n):
        p0 = self.p0
        with pool.Fori(0, n // 2) as g:
            for i in range(2):
                self.pool_split(pool, 2 * g + (p0 + 1 + i), (p0 + 1 + i) % 2)
        if n % 2:
            self.pool_split(pool, p0 + n, (p0 + n) % 2)


def segments(t):
    return [(0, TP, 0), (TP, TW - TP, 1)] if t == 0 else [(0, TW, 1)]


FIRST_MOD = 8
MOD_LAYER = 24


class Mod:

    def __init__(self, s, name, offset, pairs=2):
        self.rows = s.at(f"{name}_cond_rows", [P, 2, D], F32, offset)
        self.panels = [s.at(f"{name}_mod_panels{i}", [P, 2, D], F32, offset + 8192 * (i + 1))
                       for i in range(pairs)]


def sp_mod(s, sp, m, g, par):
    if not (isinstance(g, int) and g < FIRST_MOD + 2):
        sp.wait_ge(s.mod_step.sem, 5 * g - 6)
    sp.dma_start(m.panels[par][:], s.I["wmod"][ds(2 * g, 2)].rearrange("a p n -> p a n")
                 ).then_inc(s.mod_full[par].sem, 16)


def dve_mod(s, dve, panels, rows, g):
    for a in range(2):
        for m in range(2):
            n = 2 * a + m
            if n or not isinstance(g, int) or g > 0:
                dve.wait_ge(s.mod_step.sem, 5 * g + n)
            s.nc.vector.tensor_tensor_reduce(
                out=s.psum[:, 6:8, :], in0=panels[:, a, :].rearrange("p (b w) -> p b w", b=2),
                in1=rows[:, m, :].rearrange("p (b w) -> p b w", b=2), scale=1.0, scalar=0.0,
                op0=ALU.mult, op1=ALU.add, accum_out=s.acc[:, a, m:m + 1]).then_inc(s.mod_step.sem, 1)
    dve.wait_ge(s.mod_step.sem, 5 * g + 4)
    to = s.mod[:, ds(2 * g, 2), :]
    dve.tensor_tensor(to, to, s.acc[:], ALU.add).then_inc(s.mod_step.sem, 1)


def dve_mod_ring(s, dve, m, g, par):
    dve.wait_ge(s.mod_full[par].sem, 8 * g - (48 + 8 * par))
    dve_mod(s, dve, m.panels[par], m.rows, g)


def norm_stage(s, layer, which, load=False):
    nc, x, psum, I = s.nc, s.x, s.psum, s.I
    shift, scale = (SH1, SC1) if which == 0 else (SH2, SC2)
    sh = (layer * 6 + shift) * 8
    sc = (layer * 6 + scale) * 8
    sb = s.placer(f"norm{layer}{which}", s.rest, s.rest + 64512)
    sq = [sb(f"square{i}", [P, KC, TW]) for i in range(2)]
    std = [sb(f"std{i}", [P, TW]) for i in range(2)]
    rstd = [sb(f"rstd{i}", [P, TW]) for i in range(2)]
    xn = sb("x_scaled", [P, KC, TW])
    with ExitStack() as ctx:
        if load:
            def sem(name):
                return ctx.enter_context(nc.semaphore(name))
            rows_full, rows_ready, small = (sem(n) for n in ("cond_full", "cond_ready", "constants_full"))
            x_full = [sem(f"x_full{t}") for t in range(TT)]
            pair_full = [sem(f"first_mod{i}") for i in range(FIRST_MOD)]
            m = Mod(s, "first", s.h_at, FIRST_MOD)
        block = ctx.enter_context(nc.Block())

        if load:
            @block.sync
            def _(sp):
                sp.dma_start(m.rows[:], I["cond"]).then_inc(rows_full, 16)
                for t, name in ((s.mod, "bmod"), (s.gain, "gain"), (s.ones, "ones"), (s.eps, "eps"),
                                (s.ident, "ident")):
                    sp.dma_start(t[:], I[name]).then_inc(small, 16)
                for g in range(FIRST_MOD):
                    sp.dma_start(m.panels[g][:], I["wmod"][2 * g:2 * g + 2].rearrange("a p n -> p a n")
                                 ).then_inc(pair_full[g], 16)
                    if g >= 2 and g < 2 + TT:
                        cols = slice((g - 2) * TW, (g - 1) * TW)
                        sp.dma_start(x[:, :, cols], I["x"][:, :, cols]).then_inc(x_full[g - 2], 16)
                for p in range(2):
                    sp.dma_start(s.raw[p][:], I["stream"][p]).then_inc(s.raw_full[p].sem, 16)

            @block.gpsimd
            def _(pool):
                s.pool_split(pool, 0, 0)

        @block.scalar
        def _(act):
            if load:
                act.wait_ge(rows_full, 16)
                act.activation(m.rows[:], m.rows[:], ACT.Silu).then_inc(rows_ready, 1)
                act.wait_ge(small, 16 * 5)

            def square(t):
                if t >= 2:
                    s.mean_ready.wait(act, t - 1)
                if load:
                    act.wait_ge(x_full[t], 16)
                act.activation(sq[t % 2][:], x[:, :, t * TW:(t + 1) * TW], ACT.Square
                               ).then_inc(s.squared.sem, 1)
            square(0)
            square(1)
            for t in range(TT):
                s.mean_ready.wait(act, t + 1)
                if t >= 2:
                    s.rstd_ready.wait(act, t - 1)
                act.activation(std[t % 2][:], psum[:, t % 2, 0:TW], ACT.Sqrt, bias=s.eps[:, 0:1]
                               ).then_inc(s.std_ready.sem, 1)
                if t + 2 < TT:
                    square(t + 2)
                if load and t == 0:
                    act.wait_ge(s.raw_full[0].sem, 16)
                    act.activation(s.wh[0][:], s.raw[0][:], ACT.Copy).then_inc(s.split_high.sem, 1)
                for c in range(KC):
                    s.normed.wait(act, t * KC + c + 1)
                    for o, w, i in segments(t):
                        a = act.activation(s.hh[:, c, t * TW + o:t * TW + o + w], xn[:, c, o:o + w],
                                           ACT.Identity, bias=s.mod[:, sh + c, i:i + 1])
                    a.then_inc(s.high_ready.sem, 1)

        @block.tensor
        def _(pe):
            for t in range(TT):
                s.squared.wait(pe, t + 1)
                if t >= 2:
                    s.std_ready.wait(pe, t - 1)
                for c in range(KC):
                    mm = pe.matmul(psum[:, t % 2, 0:TW], s.ones[:], sq[t % 2][:, c, :],
                                   start=c == 0, stop=c == KC - 1)
                mm.then_inc(s.mean_ready.sem, 1)

        @block.vector
        def _(dve):
            if load:
                dve.sem_inc(s.set_free.sem, 2)
                dve.sem_inc(s.added.sem, 2)
                dve.wait_ge(small, 16 * 5)
                dve.wait_ge(rows_ready, 1)
                for g in range(FIRST_MOD):
                    dve.wait_ge(pair_full[g], 16)
                    dve_mod(s, dve, m.panels[g], m.rows, g)
                dve.wait_ge(s.mod_step.sem, 5 * FIRST_MOD)
            for i in range(2):
                v = dve.scalar_tensor_tensor(s.onep[:, :, i], s.mod[:, sc:sc + KC, i], 1.0,
                                             s.gain[:, 2 * layer + which, :], ALU.add, ALU.mult)
            v.then_inc(s.modvec_ready.sem, 1)
            s.modvec_ready.wait(dve, 1)
            for t in range(TT):
                s.std_ready.wait(dve, t + 1)
                dve.reciprocal(rstd[t % 2][:], std[t % 2][:]).then_inc(s.rstd_ready.sem, 1)
                s.rstd_ready.wait(dve, t + 1)
                for c in range(KC):
                    if t >= 1:
                        s.low_ready.wait(dve, (t - 1) * KC + c + 1)
                    for o, w, i in segments(t):
                        v = dve.scalar_tensor_tensor(xn[:, c, o:o + w], x[:, c, t * TW + o:t * TW + o + w],
                                                     s.onep[:, c, i:i + 1], rstd[t % 2][:, o:o + w],
                                                     ALU.mult, ALU.mult)
                    v.then_inc(s.normed.sem, 1)
                for c in range(KC):
                    s.high_ready.wait(dve, t * KC + c + 1)
                    for o, w, i in segments(t):
                        cols = slice(t * TW + o, t * TW + o + w)
                        v = dve.scalar_tensor_tensor(s.hl[:, c, cols], xn[:, c, o:o + w],
                                                     s.mod[:, sh + c, i:i + 1],
                                                     s.hh[:, c, cols].bitcast(F32), ALU.add, ALU.subtract)
                    v.then_inc(s.low_ready.sem, 1)
    s.modvec_ready.base += 1
    for c in (s.squared, s.mean_ready, s.std_ready, s.rstd_ready):
        c.base += TT
    for c in (s.normed, s.high_ready, s.low_ready):
        c.base += TT * KC


def pe_panel(s, pe, p, buf, group):
    pe.wait_ge(s.split_low.sem, p + 1)
    for t in range(TT):
        for k in range(KC):
            mm = three_products(pe, s.psum[:, 3 * group + t, 0:TW], s.wh[buf][:, k * P:(k + 1) * P],
                                s.wl[buf][:, k * P:(k + 1) * P], s.hh[:, k, t * TW:(t + 1) * TW],
                                s.hl[:, k, t * TW:(t + 1) * TW], k == 0, k == KC - 1)
    mm.then_inc(s.panel_used.sem, 1)


def banks(s, group):
    return s.psum[:, 3 * group:3 * group + TT, 0:TW]


def tiled(ap):
    return ap.rearrange("p (t w) -> p t w", w=TW)


def row(ap, c):
    return ap[:, c, :] if isinstance(c, int) else ap[:, ds(c, 1), :].rearrange("p a t -> p (a t)")


def in_proj_stage(s, out, n):
    p0 = s.p0
    m = s.mods = Mod(s, "in", s.x_at)
    with s.nc.semaphore("in_rows_full") as rows_full, s.nc.semaphore("in_rows_ready") as rows_ready, \
            s.nc.Block() as block:

        @block.sync
        def _(sp):
            sp.dma_start(m.rows[:], s.I["cond"]).then_inc(rows_full, 16)
            for i in range(2):
                sp_mod(s, sp, m, FIRST_MOD + i, i)

            def body(g):
                for i in range(2):
                    s.sp_load(sp, 2 * g + (p0 + 2 + i), (p0 + i) % 2)
                    sp_mod(s, sp, m, 2 * g + (FIRST_MOD + 2 + i), i)
            with sp.Fori(0, n // 2) as g:
                body(g)

        @block.gpsimd
        def _(pool):
            s.pool_stream(pool, n)

        @block.scalar
        def _(act):
            act.wait_ge(rows_full, 16)
            act.activation(m.rows[:], m.rows[:], ACT.Silu).then_inc(rows_ready, 1)

            def body(g):
                for i in range(2):
                    s.act_split(act, 2 * g + (p0 + i + 1), (p0 + i + 1) % 2)
                    act.wait_ge(s.panel_used.sem, 2 * g + (p0 + i + 1))
                    act.activation(tiled(row(out, 2 * g + i)), banks(s, i), ACT.Copy
                                   ).then_inc(s.set_free.sem, 1)
            body(0)
            with act.Fori(1, n // 2) as g:
                body(g)

        @block.tensor
        def _(pe):
            with pe.Fori(0, n // 2) as g:
                for i in range(2):
                    s.set_free.wait(pe, 2 * g + (i + 1))
                    pe_panel(s, pe, 2 * g + (p0 + i), (p0 + i) % 2, i)

        @block.vector
        def _(dve):
            dve.wait_ge(rows_ready, 1)
            with dve.Fori(0, n // 2) as g:
                for i in range(2):
                    dve_mod_ring(s, dve, m, 2 * g + (FIRST_MOD + i), i)
            for i in range(2):
                dve_mod_ring(s, dve, m, n + FIRST_MOD + i, i)
    s.p0 += n
    s.set_free.base += n


def add_gated(s, dve, f, group, gate):
    xf = row(s.x, f)
    g = [s.mod[:, ds(gate + f, 1), m:m + 1].rearrange("p a b -> p (a b)") for m in range(2)]
    b0 = 3 * group
    dve.scalar_tensor_tensor(xf[:, 0:TP], s.psum[:, b0, 0:TP], g[0], xf[:, 0:TP], ALU.mult, ALU.add)
    dve.scalar_tensor_tensor(xf[:, TP:TW], s.psum[:, b0, TP:TW], g[1], xf[:, TP:TW], ALU.mult, ALU.add)
    later = xf[:, TW:T].rearrange("p (t w) -> p t w", w=TW)
    return dve.scalar_tensor_tensor(later, s.psum[:, b0 + 1:b0 + 3, 0:TW], g[1], later, ALU.mult, ALU.add)


def out_proj_stage(s, layer):
    p0, n = s.p0, OUT_PANELS
    with s.nc.Block() as block:

        @block.sync
        def _(sp):
            s.sp_stream(sp, n)

        @block.gpsimd
        def _(pool):
            s.pool_stream(pool, n)

        @block.scalar
        def _(act):
            with act.Fori(0, n // 2) as g:
                for i in range(2):
                    s.act_split(act, 2 * g + (p0 + i + 1), (p0 + i + 1) % 2)

        @block.tensor
        def _(pe):
            with pe.Fori(0, n // 2) as g:
                for i in range(2):
                    s.set_free.wait(pe, 2 * g + (i + 1))
                    pe_panel(s, pe, 2 * g + (p0 + i), (p0 + i) % 2, i)

        @block.vector
        def _(dve):
            with dve.Fori(0, n // 2) as g:
                for i in range(2):
                    dve.wait_ge(s.panel_used.sem, 2 * g + (p0 + i + 1))
                    add_gated(s, dve, 2 * g + i, i, (layer * 6 + GA1) * 8).then_inc(s.set_free.sem, 1)
    s.p0 += n
    s.set_free.base += n


def ffn_stage(s, layer):
    p0 = s.p0
    gate_vec = (layer * 6 + GA2) * 8
    sb = s.placer(f"ffn{layer}", s.rest, s.rest + 74592)
    mid_h = [sb(f"mid_high{i}", [P, T], F32R) for i in range(4)]
    mid_l = [sb(f"mid_low{i}", [P, T], F32R) for i in range(4)]
    silu = sb("silu_gate", [P, T])
    prod = sb("product", [P, T])
    added, used = s.added, s.panel_used
    has_mod = layer == 0
    if has_mod:
        mods = Mod(s, "ffn", s.rest + 10 * 4 * T)
    MOD0 = MOD_LAYER

    with ExitStack() as ctx:
        rows_full = ctx.enter_context(s.nc.semaphore(f"ffn{layer}_rows_full"))
        rows_ready = ctx.enter_context(s.nc.semaphore(f"ffn{layer}_rows_ready"))
        block = ctx.enter_context(s.nc.Block())

        def start(j):
            return 6 * j + (p0 - 2)

        @block.sync
        def _(sp):
            if has_mod:
                sp.dma_start(mods.rows[:], s.I["cond"]).then_inc(rows_full, 16)
                for i in range(2):
                    sp_mod(s, sp, mods, MOD0 + i, i)
            with sp.Fori(0, FFN_PANELS // 6) as g:
                if has_mod:
                    for k in range(2):
                        sp_mod(s, sp, mods, 2 * g + (MOD0 + 2 + k), k)
                for i in range(6):
                    s.sp_load(sp, 6 * g + (p0 + 2 + i), (p0 + i) % 2)

        @block.gpsimd
        def _(pool):
            s.pool_stream(pool, FFN_PANELS)

        @block.scalar
        def _(act):
            if has_mod:
                act.wait_ge(rows_full, 16)
                act.activation(mods.rows[:], mods.rows[:], ACT.Silu).then_inc(rows_ready, 1)

            def hidden(c, slot, g_panel, buf):
                s.act_split(act, g_panel + 1, (buf + 1) % 2)
                act.wait_ge(used.sem, g_panel + 1)
                if not (isinstance(c, int) and c == 0):
                    s.prod_ready.wait(act, c)
                act.activation(tiled(silu[:]), banks(s, 0), ACT.Silu).then_inc(s.gate_ready.sem, 1)
                s.act_split(act, g_panel + 2, buf)
                s.prod_ready.wait(act, c + 1)
                act.activation(mid_h[slot][:], prod[:], ACT.Copy).then_inc(s.mid_high.sem, 1)

            def pair(j, q, par):
                buf = p0 % 2
                hidden(2 * j, 2 * par, q, buf)
                hidden(2 * j + 1, 2 * par + 1, q + 2, buf)

            pair(0, p0, 0)
            with act.Fori(0, (FF_G - 1) // 2) as g:
                for i in range(2):
                    q = 12 * g + (start(1) + 6 * i)
                    pair(2 * g + (1 + i), q, 1 - i)
                    s.act_split(act, q + 5, (p0 + 1) % 2)
                    s.act_split(act, q + 6, p0 % 2)
            for p in range(p0 + FFN_PANELS - 1, p0 + FFN_PANELS + 1):
                s.act_split(act, p, p % 2)

        @block.tensor
        def _(pe):
            def gate_up(c, g_panel, adds=None):
                if not (isinstance(c, int) and c == 0):
                    s.gate_ready.wait(pe, c)
                if adds is not None:
                    added.wait(pe, adds)
                pe_panel(s, pe, g_panel, p0 % 2, 0)
                if not (isinstance(c, int) and c == 0):
                    s.prod_ready.wait(pe, c)
                if adds is not None:
                    added.wait(pe, adds + 1)
                pe_panel(s, pe, g_panel + 1, (p0 + 1) % 2, 1)

            def down(j, p, par, last=False):
                for f in range(KC):
                    buf = (p0 + f // 4) % 2
                    if f % 4 == 0:
                        pe.wait_ge(s.split_low.sem, p + (1 + f // 4))
                    if f == 0:
                        s.mid_low.wait(pe, 2 * j + 2)
                    if f < 2 and not last:
                        (s.gate_ready if f == 0 else s.prod_ready).wait(pe, 2 * j + 4)
                    else:
                        added.wait(pe, 8 * j + (f + 1))
                    for t in range(TT):
                        for i in range(2):
                            w = slice((4 * i + f % 4) * P, (4 * i + f % 4 + 1) * P)
                            cols = slice(t * TW, (t + 1) * TW)
                            mm = three_products(pe, s.psum[:, 3 * (f % 2) + t, 0:TW], s.wh[buf][:, w],
                                                s.wl[buf][:, w], mid_h[2 * par + i][:, cols],
                                                mid_l[2 * par + i][:, cols], i == 0, i == 1)
                    if f % 4 == 3:
                        mm.then_inc(used.sem, 1)
                    else:
                        mm.then_inc(s.down_full.sem, 1)

            gate_up(0, p0)
            gate_up(1, p0 + 2)
            with pe.Fori(0, (FF_G - 1) // 2) as g:
                for i in range(2):
                    j, q = 2 * g + (1 + i), 12 * g + (start(1) + 6 * i)
                    for k in range(2):
                        gate_up(2 * j + k, q + 2 * k, 8 * j - 7 if k == 0 else None)
                    down(2 * g + i, q + 4, i)
            last = FF_G - 1
            down(last, p0 + FFN_PANELS - 2, last % 2, True)

        @block.vector
        def _(dve):
            def product(c, u_used):
                s.gate_ready.wait(dve, c + 1)
                dve.wait_ge(used.sem, u_used)
                if not (isinstance(c, int) and c == 0):
                    s.mid_high.wait(dve, c)
                    s.mid_low.wait(dve, c)
                dve.tensor_tensor(tiled(prod[:]), tiled(silu[:]), banks(s, 1), ALU.mult
                                  ).then_inc(s.prod_ready.sem, 1)

            def low(c, slot):
                s.mid_high.wait(dve, c + 1)
                dve.tensor_tensor(mid_l[slot][:], prod[:], mid_h[slot][:].bitcast(F32), ALU.subtract
                                  ).then_inc(s.mid_low.sem, 1)

            def add(j, f, d_used):
                if f % 4 == 3:
                    dve.wait_ge(used.sem, d_used + f // 4)
                else:
                    s.down_full.wait(dve, 6 * j + (f + 1 - f // 4))
                added.wait(dve, 8 * j + (f + 1))
                add_gated(s, dve, f, f % 2, gate_vec).then_inc(added.sem, 1)

            if has_mod:
                dve.wait_ge(rows_ready, 1)
                for k in range(2):
                    dve_mod_ring(s, dve, mods, MOD0 + k, k)
            product(0, p0 + 2)
            low(0, 0)
            if has_mod:
                dve_mod_ring(s, dve, mods, MOD0 + 2, 0)
            product(1, p0 + 4)
            low(1, 1)
            if has_mod:
                dve_mod_ring(s, dve, mods, MOD0 + 3, 1)
            with dve.Fori(0, (FF_G - 1) // 2) as g:
                for i in range(2):
                    j, q = 2 * g + (1 + i), 12 * g + (start(1) + 6 * i)
                    for k in range(2):
                        product(2 * j + k, q + (2 + 2 * k))
                        if k == 0:
                            low(2 * j, 2 * (1 - i))
                            if has_mod:
                                for k_ in range(2):
                                    dve_mod_ring(s, dve, mods, 4 * g + (MOD0 + 4 + 2 * i + k_), k_)
                    for f in range(KC):
                        add(2 * g + i, f, q + 5)
                        if f == 1:
                            low(2 * j + 1, 2 * (1 - i) + 1)
            last = FF_G - 1
            for f in range(KC):
                add(last, f, p0 + FFN_PANELS - 1)
    s.p0 += FFN_PANELS
    for c, n in ((s.gate_ready, FF_CH), (s.prod_ready, FF_CH), (s.mid_high, FF_CH), (s.mid_low, FF_CH),
                 (s.down_full, 6 * FF_G), (s.added, 8 * FF_G)):
        c.base += n


def final_stage(s):
    nc, x, psum = s.nc, s.x, s.psum
    sb = s.placer("final", s.rest, s.rest + 64512)
    sq = [sb(f"square{i}", [P, KC, TW]) for i in range(2)]
    std = [sb(f"std{i}", [P, TW]) for i in range(2)]
    rstd = [sb(f"rstd{i}", [P, TW]) for i in range(2)]
    with nc.semaphore("y_stored") as y_stored, nc.Block() as block:

        @block.scalar
        def _(act):
            def square(t):
                if t >= 2:
                    s.mean_ready.wait(act, t - 1)
                act.activation(sq[t % 2][:], x[:, :, t * TW:(t + 1) * TW], ACT.Square
                               ).then_inc(s.squared.sem, 1)
            square(0)
            square(1)
            for t in range(TT):
                s.mean_ready.wait(act, t + 1)
                if t >= 2:
                    s.rstd_ready.wait(act, t - 1)
                act.activation(std[t % 2][:], psum[:, t % 2, 0:TW], ACT.Sqrt, bias=s.eps[:, 0:1]
                               ).then_inc(s.std_ready.sem, 1)
                if t + 2 < TT:
                    square(t + 2)

        @block.tensor
        def _(pe):
            for t in range(TT):
                s.squared.wait(pe, t + 1)
                if t >= 2:
                    s.std_ready.wait(pe, t - 1)
                for c in range(KC):
                    mm = pe.matmul(psum[:, t % 2, 0:TW], s.ones[:], sq[t % 2][:, c, :],
                                   start=c == 0, stop=c == KC - 1)
                mm.then_inc(s.mean_ready.sem, 1)

        @block.vector
        def _(dve):
            for t in range(TT):
                s.std_ready.wait(dve, t + 1)
                dve.reciprocal(rstd[t % 2][:], std[t % 2][:]).then_inc(s.rstd_ready.sem, 1)
                s.rstd_ready.wait(dve, t + 1)
                s.squared.wait(dve, t + 1)
                for c in range(KC):
                    xt = x[:, c, t * TW:(t + 1) * TW]
                    v = dve.scalar_tensor_tensor(xt, xt, s.gain[:, 4, c:c + 1], rstd[t % 2][:],
                                                 ALU.mult, ALU.mult)
                v.then_inc(s.normed.sem, 1)

        @block.sync
        def _(sp):
            for t in range(TT):
                s.normed.wait(sp, t + 1)
                sp.dma_start(s.O["y"][:, :, t * TW:(t + 1) * TW], x[:, :, t * TW:(t + 1) * TW]
                             ).then_inc(y_stored, 16)
            sp.wait_ge(y_stored, 16 * TT)
            for i in range(2):
                n = (STREAM + PAD + 1 - i) // 2
                sp.wait_ge(s.raw_full[i].sem, 16 * n)


def even_buffer(s):
    return s.at("even", [P, EVEN_PANELS, T], F32, s.rest)


def rg_stage(s, even):
    nc, psum, I = s.nc, s.psum, s.I
    sq = [s.at(f"rg_square{d}", [P, T], F32, at + 12 * T) for d, at in enumerate((s.hi_chunk, s.lo_chunk))]
    hi = s.placer("rg_hi", s.hi_chunk + 16 * T, s.lo_chunk)
    lo = s.placer("rg_lo", s.lo_chunk + 16 * T, s.x_at)
    up = s.placer("rg_x", s.x_at, s.rest)
    gate = [[sb(f"gate{i}{j}", [P, T]) for j in range(4)] for i, sb in enumerate((hi, up))]
    mult = [[sb(f"mult{i}{d}", [P, T]) for d in range(2)] for i, sb in enumerate((lo, up))]
    xc = [sb(f"xc{i}", [P, T]) for i, sb in enumerate((lo, up))]
    gw = lo("gate_weights", [P, 4 * P])
    conv = lo("conv", [P, RG_CH, 5])
    bias = lo("gate_bias", [P, RG_CH, 4])
    lam = lo("lam", [P, RG_CH, 2])
    h0 = lo("h0", [P, RG_CH, 2])
    sp_ = [lo(f"softplus{i}", [P, RG_CH, 2]) for i in range(4)]
    last = lo("last", [P, RG_CH, 2])
    with ExitStack() as ctx:
        def sem(name):
            return ctx.enter_context(nc.semaphore("rg_" + name))
        small, gelu_ready, sp_step, sp_done = sem("small"), sem("gelu"), sem("sp_step"), sem("sp_done")
        gw_full, gates_done, gate_full, gate_read = sem("gw_full"), sem("gates_done"), sem("gate_full"), sem("gate_read")
        conv_step, tanh_ready, a_ready, sq_ready = sem("conv_step"), sem("tanh_ready"), sem("a_ready"), sem("square_ready")
        m_ready, root_ready, b_step, scanned = sem("m_ready"), sem("root_ready"), sem("b_step"), sem("scanned")
        y_step, y_high, chunk_done, stored = sem("y_step"), sem("y_high"), sem("chunk_done"), sem("stored")
        ib_ready = sem("ib_ready")
        block = ctx.enter_context(nc.Block())

        def scalar(t, c, j):
            return t[:, ds(c, 1), j:j + 1].rearrange("p a b -> p (a b)")

        @block.sync
        def _(sp):
            for t, name in ((conv, "conv_rg"), (bias, "rgb"), (lam, "lam"), (h0, "h0")):
                sp.dma_start(t[:], I[name]).then_inc(small, 16)
            sp.dma_start(gw[:], I["rgw"][0]).then_inc(gw_full, 16)
            sp.dma_start(s.O["k"], even[:, 12, 0:TP]).then_inc(stored, 16)
            sp.dma_start(s.O["v"], even[:, 13, 0:TP]).then_inc(stored, 16)
            for c in range(1, RG_CH):
                sp.wait_ge(gates_done, c)
                sp.dma_start(gw[:], I["rgw"][c]).then_inc(gw_full, 16)
            sp.wait_ge(chunk_done, RG_CH)
            sp.dma_start(s.O["rg"], last[:]).then_inc(stored, 16)
            sp.wait_ge(stored, 48)

        @block.tensor
        def _(pe):
            with pe.Fori(0, RG_CH // 2) as g:
                for i in range(2):
                    c = 2 * g + i
                    pe.wait_ge(gw_full, 16 * c + 16)
                    pe.wait_ge(conv_step, 7 * c + 7)
                    for j in range(4):
                        pe.wait_ge(gate_read, 4 * c + (j + 1))
                        for t in range(TT):
                            mm = pe.matmul(psum[:, 3 * (j % 2) + t, 0:TW], gw[:, j * P:(j + 1) * P],
                                           xc[i][:, t * TW:(t + 1) * TW], start=True, stop=True)
                        if j == 3:
                            mm.then_inc(gates_done, 1)
                        else:
                            mm.then_inc(gate_full, 1)

        @block.scalar
        def _(act):
            act.sem_inc(gate_read, 2)
            act.activation(even[:, 4:8, :], even[:, 4:8, :], ACT.Gelu_apprx_tanh).then_inc(gelu_ready, 1)
            act.wait_ge(small, 64)
            act.activation(sp_[0][:], lam[:], ACT.Abs).then_inc(sp_step, 1)
            act.wait_ge(sp_step, 1)
            act.activation(sp_[1][:], sp_[0][:], ACT.Exp, scale=-1.0).then_inc(sp_step, 1)
            act.wait_ge(sp_done, 1)
            act.activation(sp_[0][:], sp_[2][:], ACT.Ln).then_inc(sp_step, 1)
            act.wait_ge(sp_done, 6)

            def front(c, i):
                if not (isinstance(c, int) and c < 2):
                    act.wait_ge(chunk_done, c - 1)
                for j in range(4):
                    if j < 3:
                        act.wait_ge(gate_full, 3 * c + (j + 1))
                    else:
                        act.wait_ge(gates_done, c + 1)
                    act.activation(tiled(gate[i][j][:]), banks(s, j % 2), ACT.Sigmoid,
                                   bias=scalar(bias, c, j)).then_inc(gate_read, 1)
                act.wait_ge(gate_read, 4 * c + 6)
                for d in range(2):
                    act.activation(mult[i][d][:], gate[i][2 * d][:], ACT.Tanh, scale=scalar(sp_[0], c, d)
                                   ).then_inc(tanh_ready, 1)
                for d in range(2):
                    act.wait_ge(tanh_ready, 2 * c + (d + 1))
                    act.activation(gate[i][2 * d][:], gate[i][2 * d][:], ACT.Exp, scale=scalar(sp_[1], c, d)
                                   ).then_inc(a_ready, 1)
                for d in range(2):
                    act.wait_ge(a_ready, 2 * c + (d + 1))
                    if not (isinstance(c, int) and c == 0):
                        act.wait_ge(m_ready, 2 * c + (d - 1))
                    act.activation(sq[d][:], gate[i][2 * d][:], ACT.Square).then_inc(sq_ready, 1)

            def root(c, i):
                for d in range(2):
                    act.wait_ge(m_ready, 2 * c + (d + 1))
                    act.activation(mult[i][d][:], mult[i][d][:], ACT.Sqrt).then_inc(root_ready, 1)

            def high(c, i):
                act.wait_ge(y_step, 2 * c + 2)
                act.activation(row(s.hh, c), xc[i][:], ACT.Copy).then_inc(y_high, 1)

            front(0, 0)
            root(0, 0)
            with act.Fori(0, RG_CH // 2 - 1) as g:
                for i in range(2):
                    c = 2 * g + i
                    front(2 * g + (i + 1), 1 - i)
                    high(c, i)
                    root(2 * g + (i + 1), 1 - i)
            front(RG_CH - 1, 1)
            high(RG_CH - 2, 0)
            root(RG_CH - 1, 1)
            high(RG_CH - 1, 1)

        @block.gpsimd
        def _(pool):
            with pool.Fori(0, RG_CH // 2) as g:
                for i in range(2):
                    c = 2 * g + i
                    for d in range(2):
                        pool.wait_ge(gate_read, 4 * c + (2 * d + 4))
                        pool.tensor_tensor(gate[i][2 * d + 1][:], gate[i][2 * d + 1][:], xc[i][:], ALU.mult
                                           ).then_inc(ib_ready, 1)

        @block.vector
        def _(dve):
            dve.wait_ge(small, 64)
            dve.wait_ge(sp_step, 2)
            dve.tensor_scalar(sp_[2][:], sp_[1][:], 1.0, None, ALU.add).then_inc(sp_done, 1)
            dve.wait_ge(sp_done, 1)
            dve.scalar_tensor_tensor(sp_[3][:], sp_[2][:], -1.0, sp_[1][:], ALU.add, ALU.subtract
                                     ).then_inc(sp_done, 1)
            dve.wait_ge(sp_step, 3)
            dve.reciprocal(sp_[2][:], sp_[2][:]).then_inc(sp_done, 1)
            dve.wait_ge(sp_done, 3)
            dve.tensor_tensor(sp_[3][:], sp_[3][:], sp_[2][:], ALU.mult)
            dve.tensor_scalar(sp_[1][:], lam[:], -RG_C, 0.0, ALU.mult, ALU.max).then_inc(sp_done, 1)
            dve.wait_ge(sp_done, 4)
            dve.tensor_tensor(sp_[0][:], sp_[0][:], sp_[3][:], ALU.subtract).then_inc(sp_done, 1)
            dve.wait_ge(sp_done, 5)
            dve.scalar_tensor_tensor(sp_[0][:], sp_[0][:], RG_C, sp_[1][:], ALU.mult, ALU.add
                                     ).then_inc(sp_step, 1)
            dve.wait_ge(sp_step, 4)
            dve.tensor_scalar(sp_[1][:], sp_[0][:], -1.0, None, ALU.mult).then_inc(sp_done, 1)

            def convolution(c, i):
                xr = row(even, c)
                if not (isinstance(c, int) and c < 2):
                    dve.wait_ge(chunk_done, c - 1)
                    dve.wait_ge(y_high, c - 1)
                dve.tensor_scalar(xc[i][:], xr, scalar(conv, c, 2), scalar(conv, c, 4), ALU.mult, ALU.add
                                  ).then_inc(conv_step, 1)
                for n, (tap, off) in enumerate(((0, -2), (1, -1), (3, 1))):
                    for m, (lo, hi) in enumerate(((0, TP), (TP, T))):
                        a, b = (lo - off, hi) if off < 0 else (lo, hi - off)
                        dve.wait_ge(conv_step, 7 * c + (2 * n + m + 1) if n else 7 * c + 1)
                        dve.scalar_tensor_tensor(xc[i][:, a:b], xr[:, a + off:b + off], scalar(conv, c, tap),
                                                 xc[i][:, a:b], ALU.mult, ALU.add).then_inc(conv_step, 1)

            def multiplier(c, i):
                for d in range(2):
                    dve.wait_ge(tanh_ready, 2 * c + (d + 1))
                    dve.wait_ge(sq_ready, 2 * c + (d + 1))
                    dve.scalar_tensor_tensor(mult[i][d][:], sq[d][:], 1.0, mult[i][d][:], ALU.add, ALU.mult
                                             ).then_inc(m_ready, 1)

            def scans(c, i):
                for d in range(2):
                    a, b, h = gate[i][2 * d], gate[i][2 * d + 1], mult[i][d]
                    dve.wait_ge(root_ready, 2 * c + (d + 1))
                    dve.wait_ge(ib_ready, 2 * c + (d + 1))
                    dve.tensor_tensor(b[:], b[:], h[:], ALU.mult).then_inc(b_step, 1)
                    dve.wait_ge(b_step, 2 * c + (d + 1))
                    for m, (lo, hi) in enumerate(((0, TP), (TP, T))):
                        cols = slice(lo, hi) if d == 0 else slice(hi - 1, lo - 1 if lo else None, -1)
                        v = dve.tensor_tensor_scan(h[:, cols], a[:, cols], b[:, cols],
                                                   0.0 if m == 0 else scalar(h0, c, d), ALU.mult, ALU.add)
                    v.then_inc(scanned, 1)
                dve.wait_ge(scanned, 2 * c + 2)
                for d in range(2):
                    at = TP - 1 if d == 0 else 0
                    dve.tensor_copy(scalar(last, c, d), mult[i][d][:, at:at + 1])
                dve.tensor_tensor(xc[i][:], mult[i][0][:], mult[i][1][:], ALU.add).then_inc(y_step, 1)
                dve.wait_ge(y_step, 2 * c + 1)
                dve.wait_ge(gelu_ready, 1)
                dve.tensor_tensor(xc[i][:], xc[i][:], row(even, c + 4), ALU.mult).then_inc(y_step, 1)

            def low(c, i):
                dve.wait_ge(y_high, c + 1)
                dve.tensor_tensor(row(s.hl, c), xc[i][:], row(s.hh, c).bitcast(F32), ALU.subtract
                                  ).then_inc(chunk_done, 1)

            convolution(0, 0)
            convolution(1, 1)
            multiplier(0, 0)
            scans(0, 0)
            with dve.Fori(0, RG_CH // 2 - 1) as g:
                for i in range(2):
                    multiplier(2 * g + (i + 1), 1 - i)
                    low(2 * g + i, i)
                    convolution(2 * g + (i + 2), i)
                    scans(2 * g + (i + 1), 1 - i)
            multiplier(RG_CH - 1, 1)
            low(RG_CH - 2, 0)
            scans(RG_CH - 1, 1)
            low(RG_CH - 1, 1)


def attention_stage(s, even):
    nc, psum, I = s.nc, s.psum, s.I
    sb = s.placer("att", s.rest, s.rest + 8 * 4 * T)
    cos, sin, turned = sb("cos", [P, TL]), sb("sin", [P, TL]), sb("turned", [P, TL])
    rope = sb("rope", [P, P])
    ctx_k = sb("ctx_k", [P, P])
    vt = sb("v_tokens", [P, NT + 1, P])
    window = sb("window", [P, 8, 2, P], BF16)
    ident_bf = sb("ident_bf", [P, P], BF16)
    prob = sb("prob", [P, 2, 512])
    over = s.placer("att_over", s.rest, s.rest + 8 * TL)
    prob_t = [sb("prob_t0", [P, 2, 512]), over("prob_t1", [P, 2, 512])]
    q_blk = [sb("q_block0", [P, 2, 4, P]), over("q_block1", [P, 2, 4, P])]
    sb = s.placer("att_hi", s.rest + EVEN_PANELS * 4 * T, s.rest + 74592)
    o_sb = sb("o", [P, 512])
    sink, nsink = sb("sink", [P, HEADS]), sb("neg_sink", [P, HEADS])
    top, negm, rows, es, den, rden = (sb(n, [P, HEADS]) for n in ("top", "negm", "rows", "es", "den", "rden"))
    scale = HD ** -0.5
    with ExitStack() as ctx:
        def sem(name):
            return ctx.enter_context(nc.semaphore("att_" + name))
        loaded, turn_full, turn_read, cos_done, roped, v_full, vt_ready = (
            sem(n) for n in ("loaded", "turn_full", "turn_read", "cos_done", "roped", "v_full", "vt_ready"))
        q_ready, s_full, top_step, neg_step, negm_ready, p_ready, pt_full, pt_act, pt_dve = (
            sem(n) for n in ("q_ready", "s_full", "top_step", "neg_step", "negm_ready", "p_ready", "pt_full",
                             "pt_act", "pt_dve"))
        pv_done, es_ready, den_ready, rden_ready, o_ready, y_full, y_high, y_low, nsink_ready = (
            sem(n) for n in ("pv_done", "es_ready", "den_ready", "rden_ready", "o_ready", "y_full", "y_high",
                             "y_low", "nsink_ready"))
        q_zero, x_back = sem("q_zero"), sem("x_back")
        block = ctx.enter_context(nc.Block())
        BLOCKS = NT

        def wait(eng, semaphore, n):
            if not (isinstance(n, int) and n <= 0):
                eng.wait_ge(semaphore, n)

        def blocks(eng, run, finish):
            run(0, 0, None, True)
            finish(0, 0, True)
            run(1, 1, None, False)
            run(2, 0, 1, False)
            with eng.Fori(1, (BLOCKS - 1) // 2) as g:
                for j in range(2):
                    run(2 * g + (1 + j), 1 - j, 2 * g + j, False)
            finish(BLOCKS - 1, (BLOCKS - 1) % 2, False)

        @block.sync
        def _(sp):
            for t, name in ((rope, "rope"), (sin, "sin"), (cos, "cos"), (ctx_k, "ctx_k"), (window, "window"),
                            (ident_bf, "ident_bf"), (sink, "sink")):
                sp.dma_start(t[:], I[name]).then_inc(loaded, 16)
            sp.dma_start(vt[:, NT, :], I["ctx_v"]).then_inc(loaded, 16)
            sp.dma_start(s.x[:], I["x"]).then_inc(x_back, 16)
            sp.wait_ge(x_back, 16)

        @block.tensor
        def _(pe):
            for n in range(NT):
                mm = pe.transpose(psum[:, 4 + n // 4, (n % 4) * P:(n % 4 + 1) * P],
                                  even[:, 13, n * P:(n + 1) * P], s.ident[:])
            mm.then_inc(v_full, 1)
            pe.wait_ge(loaded, 16 * 8)
            for c in range(5):
                wait(pe, turn_read, c - 1)
                for t in range(2):
                    mm = pe.matmul(psum[:, 2 * (c % 2) + t, :], rope[:],
                                   even[:, c + 8, TP + 512 * t:TP + 512 * (t + 1)], start=True, stop=True)
                mm.then_inc(turn_full, 1)
            pe.wait_ge(roped, 5)
            pe.wait_ge(vt_ready, 1)

            def scores(i, par, c, prompt):
                if c == 0:
                    pe.wait_ge(q_ready, i + 1)
                wait(pe, p_ready, 8 * i + (2 * c - 2))
                for h in range(2):
                    q = q_blk[par][:, h, c, :]
                    out = psum[:, 2 * (c % 2) + h, :]
                    if prompt:
                        mm = pe.matmul(out[:, 0:P], q, even[:, 12, 0:P], start=True, stop=True)
                        continue
                    keys = even[:, 12:14, :].rearrange("p a t -> p (a t)")
                    pe.matmul(out[:, 0:TW], q, keys[:, ds(i * P - P, TW)], start=True, stop=False,
                              skip_group_check=True)
                    pe.matmul(out[:, TW:512], q, ctx_k[:], start=False, stop=False, skip_group_check=True)
                    for j in range(2):
                        mm = pe.matmul(out[:, 2 * j * P:(2 * j + 1) * P], ident_bf[:],
                                       window[:, ds(i - 1, 1), j, :].rearrange("p a n -> p (a n)"),
                                       start=False, stop=j == 1, skip_group_check=True)
                mm.then_inc(s_full, 1)

            def turn(i, c, prompt):
                pe.wait_ge(p_ready, 8 * i + (2 * c + 2))
                wait(pe, pt_act, 4 * i + c)
                wait(pe, pt_dve, 4 * i + c)
                for h in range(2):
                    for k in range(1 if prompt else 4):
                        mm = pe.transpose(psum[:, 4 + h, k * P:(k + 1) * P], prob[:, h, k * P:(k + 1) * P],
                                          s.ident[:])
                mm.then_inc(pt_full, 1)

            def weigh(i, c, prompt):
                nk = 1 if prompt else 4
                pe.wait_ge(pt_act, 4 * i + (c + 1))
                pe.wait_ge(pt_dve, 4 * i + (c + 1))
                if c == 0:
                    wait(pe, o_ready, i)
                for h in range(2):
                    out = psum[:, 6, c * P + HD * h:c * P + HD * h + HD]
                    for k in range(nk):
                        if prompt:
                            v = vt[:, 0, HD * h:HD * h + HD]
                        elif k == 3:
                            v = vt[:, NT, HD * h:HD * h + HD]
                        else:
                            v = vt[:, ds(i + (k - 1), 1), HD * h:HD * h + HD].rearrange("p a n -> p (a n)")
                        mm = pe.matmul(out, prob_t[c % 2][:, h, k * P:(k + 1) * P], v, start=k == 0,
                                       stop=k == nk - 1)
                mm.then_inc(pv_done, 1)

            def outputs(i):
                pe.wait_ge(o_ready, i + 1)
                wait(pe, y_low, i)
                for c in range(4):
                    mm = pe.transpose(psum[:, 7, c * P:(c + 1) * P], o_sb[:, c * P:(c + 1) * P], s.ident[:])
                mm.then_inc(y_full, 1)

            def run(i, par, prev, prompt):
                for c in range(4):
                    scores(i, par, c, prompt)
                    if c >= 1:
                        turn(i, c - 1, prompt)
                    elif prev is not None:
                        turn(prev, 3, prompt)
                    if c >= 2:
                        weigh(i, c - 2, prompt)
                    elif prev is not None:
                        weigh(prev, c + 2, prompt)
                    if c == 2 and prev is not None:
                        outputs(prev)

            def finish(i, par, prompt):
                turn(i, 3, prompt)
                weigh(i, 2, prompt)
                weigh(i, 3, prompt)
                outputs(i)

            blocks(pe, run, finish)

        @block.gpsimd
        def _(pool):
            pool.wait_ge(loaded, 16 * 8)
            pool.tensor_scalar(nsink[:], sink[:], -1.0, None, ALU.mult).then_inc(nsink_ready, 1)
            pool.memset(q_blk[0][:], 0.0).then_inc(q_zero, 1)
            for c in range(5):
                x = even[:, c + 8, TP:T]
                pool.wait_ge(turn_full, c + 1)
                pool.tensor_tensor(x, x, cos[:], ALU.mult).then_inc(cos_done, 1)
            pool.wait_ge(roped, 5)
            pool.memset(q_blk[1][:], 0.0).then_inc(q_zero, 1)
            pool.wait_ge(q_zero, 2)

            def load_q(i, par):
                wait(pool, s_full, 4 * i - 4)
                cols = ds(i * P, P)
                pool.tensor_copy(q_blk[par][0:HD, 0], even[0:HD, 8:12, cols])
                pool.tensor_copy(q_blk[par][HD:P, 1], even[HD:P, 8:12, cols]).then_inc(q_ready, 1)
            load_q(0, 0)
            load_q(1, 1)
            load_q(2, 0)
            with pool.Fori(1, (BLOCKS - 1) // 2) as g:
                for j in range(2):
                    load_q(2 * g + (1 + j), 1 - j)

        @block.scalar
        def _(act):
            def exps(i, c, prompt):
                wide = P if prompt else 512
                act.wait_ge(negm_ready, 4 * i + (c + 1))
                wait(act, pt_full, 4 * i + c)
                for h in range(2):
                    j = 2 * c + h
                    act.activation(prob[:, h, 0:wide], psum[:, 2 * (c % 2) + h, 0:wide], ACT.Exp,
                                   bias=negm[:, j:j + 1], scale=scale, accum_out=rows[:, j:j + 1]
                                   ).then_inc(p_ready, 1)
                if c == 3:
                    act.activation(es[:], es[:], ACT.Exp).then_inc(es_ready, 1)

            def copy_t(i, c, prompt):
                wide = P if prompt else 512
                act.wait_ge(pt_full, 4 * i + (c + 1))
                wait(act, pv_done, 4 * i + (c - 1))
                act.activation(prob_t[c % 2][:, 0, 0:wide], psum[:, 4, 0:wide], ACT.Copy).then_inc(pt_act, 1)

            def high(i):
                act.wait_ge(y_full, i + 1)
                act.activation(s.hh[:, 4:8, ds(i * P, P)], psum[:, 7, :].rearrange("p (c w) -> p c w", w=P),
                               ACT.Copy).then_inc(y_high, 1)

            def run(i, par, prev, prompt):
                for c in range(4):
                    if c >= 1:
                        exps(i, c, prompt)
                        if c == 3 and prev is not None:
                            high(prev)
                        copy_t(i, c - 1, prompt)
                    else:
                        exps(i, 0, prompt)
                        if prev is not None:
                            copy_t(prev, 3, prompt)

            def finish(i, par, prompt):
                copy_t(i, 3, prompt)
                high(i)

            blocks(act, run, finish)

        @block.vector
        def _(dve):
            dve.wait_ge(v_full, 1)
            dve.tensor_copy(vt[:, 0:8, :].rearrange("p (a n) w -> p a (n w)", a=2), psum[:, 4:6, :])
            dve.tensor_copy(vt[:, 8, :], psum[:, 6, 0:P]).then_inc(vt_ready, 1)
            dve.wait_ge(loaded, 16 * 8)
            for c in range(5):
                x = even[:, c + 8, TP:T]
                dve.wait_ge(turn_full, c + 1)
                wait(dve, roped, c)
                dve.tensor_tensor(turned[:].rearrange("p (a t) -> p a t", a=2), psum[:, 2 * (c % 2):2 * (c % 2) + 2, :],
                                  sin[:].rearrange("p (a t) -> p a t", a=2), ALU.mult).then_inc(turn_read, 1)
                dve.wait_ge(turn_read, c + 1)
                dve.wait_ge(cos_done, c + 1)
                dve.tensor_tensor(x, x, turned[:], ALU.add).then_inc(roped, 1)
            dve.wait_ge(nsink_ready, 1)

            def largest(i, c, prompt, prev=None):
                wide = P if prompt else 512
                two = slice(2 * c, 2 * c + 2)
                dve.wait_ge(s_full, 4 * i + (c + 1))
                wait(dve, neg_step, 4 * i + c - 3)
                dve.tensor_reduce(top[:, two], psum[:, 2 * (c % 2):2 * (c % 2) + 2, 0:wide], AX.X, ALU.max
                                  ).then_inc(top_step, 1)
                if c == 0:
                    wait(dve, p_ready, 8 * i)
                    wait(dve, es_ready, i)
                    if prev is not None:
                        denominators(prev)
                    wait(dve, den_ready, i)
                dve.wait_ge(top_step, 4 * i + (c + 1))
                dve.scalar_tensor_tensor(negm[:, two], top[:, two], -scale, nsink[:, two], ALU.mult, ALU.min
                                         ).then_inc(neg_step, 1)
                dve.wait_ge(neg_step, 4 * i + (c + 1))
                dve.tensor_tensor(es[:, two], negm[:, two], sink[:, two], ALU.add).then_inc(negm_ready, 1)

            def denominators(i):
                wait(dve, rden_ready, i)
                dve.tensor_tensor(den[:], rows[:], es[:], ALU.add).then_inc(den_ready, 1)
                dve.wait_ge(den_ready, i + 1)
                wait(dve, o_ready, i)
                dve.reciprocal(rden[:], den[:]).then_inc(rden_ready, 1)

            def copy_t(i, c, prompt):
                wide = P if prompt else 512
                dve.wait_ge(pt_full, 4 * i + (c + 1))
                wait(dve, pv_done, 4 * i + (c - 1))
                dve.tensor_copy(prob_t[c % 2][:, 1, 0:wide], psum[:, 5, 0:wide]).then_inc(pt_dve, 1)

            def normalise(i):
                dve.wait_ge(rden_ready, i + 1)
                dve.wait_ge(pv_done, 4 * i + 4)
                wait(dve, y_full, i)
                dve.tensor_tensor(o_sb[:].rearrange("p (h w) -> p h w", w=HD),
                                  psum[:, 6, :].rearrange("p (h w) -> p h w", w=HD),
                                  rden[:].rearrange("p (h o) -> p h o", o=1).to_broadcast([P, HEADS, HD]),
                                  ALU.mult).then_inc(o_ready, 1)

            def low(i):
                cols = ds(i * P, P)
                dve.wait_ge(y_high, i + 1)
                dve.tensor_tensor(s.hl[:, 4:8, cols], psum[:, 7, :].rearrange("p (c w) -> p c w", w=P),
                                  s.hh[:, 4:8, cols].bitcast(F32), ALU.subtract).then_inc(y_low, 1)

            def run(i, par, prev, prompt):
                for c in range(4):
                    largest(i, c, prompt, prev)
                    if c >= 1:
                        copy_t(i, c - 1, prompt)
                    elif prev is not None:
                        copy_t(prev, 3, prompt)
                    if prev is not None and c == 1:
                        normalise(prev)
                    if prev is not None and c == 3:
                        low(prev)

            def finish(i, par, prompt):
                copy_t(i, 3, prompt)
                dve.wait_ge(p_ready, 8 * i + 8)
                dve.wait_ge(es_ready, i + 1)
                denominators(i)
                normalise(i)
                low(i)

            blocks(dve, run, finish)


LEVELS = [2, 4, 8, 16, 32, 64]
NL = len(LEVELS)
NB = 3
SLOTS = NL * NB
(G_, GC_, EG_, EK_, EL_, BETA_, NBETA_) = range(7)


class Delta:

    def __init__(self, s):
        sb = s.placer("dn", s.x_at, s.rest + 74592)
        self.raw = {n: sb(f"raw_{n}", [P, T]) for n in "kqv"}
        self.silu_z = sb("silu_z", [P, T])
        self.kn, self.qn, self.vf = sb("kn", [P, T]), sb("qn", [P, T]), sb("vf", [P, T])
        self.k_tok, self.v_tok = sb("k_tok", [P, T]), sb("v_tok", [P, T])
        self.pt = [sb(f"pt{d}", [P, T]) for d in range(2)]
        self.wt = [sb(f"wt{d}", [P, T]) for d in range(2)]
        self.ub = [sb(f"ub{d}", [P, T]) for d in range(2)]
        self.qg = [sb(f"qg{d}", [P, T]) for d in range(2)]
        kd0 = sb("kd0", [P, T])
        self.kd = [kd0, self.k_tok]
        t0, tt0 = sb("t0", [P, T]), sb("tt0", [P, T])
        self.t, self.tt = [t0, self.vf], [tt0, self.raw["v"]]
        self.osum = sb("osum", [P, T])
        self.xl = [self.osum[:, i * TW:(i + 1) * TW] for i in range(2)]
        self.bm = [self.osum[:, 2 * TW:3 * TW], self.kn[:, 2 * TW:3 * TW]]
        self.fin = [self.kn[:, d * P:(d + 1) * P] for d in range(2)]
        self.vn = [self.kn[:, (3 + d) * P:(4 + d) * P] for d in range(2)]
        self.kk, self.qk = self.raw["k"], self.raw["q"]
        self.tok = sb("token_consts", [P, 7 * 2 * NT * DN_H])
        self.hs = sb("head_consts", [P, 7, 2, NT])
        self.level = sb("level_masks", [P, 2, NL + 1, P], BF16)
        self.low = sb("neg_masks", [P, 2, P], BF16)
        self.tri = sb("tri", [P, 2, P])
        self.state = [[sb(f"state{d}{i}", [P, P]) for i in range(2)] for d in range(2)]
        self.conv = sb("conv", [P, 24, 4])
        self.onorm = sb("onorm", [P, 1])


def decay_stage(s, dn):
    nc, psum, I, p0 = s.nc, s.psum, s.I, s.p0
    sb = s.placer("decay", s.rest, s.rest + 10 * 4 * T)
    gb, u, e, w, r, l = (sb(n, [48, T]) for n in ("gb", "u", "e", "w", "r", "l"))
    gb_tok = sb("gb_tok", [P, NT * 48])
    gl = sb("g_last", [P, 2, NT * DN_H])
    dts = sb("dt_bias", [16, 2])
    tok = dn.tok[:].rearrange("p (v d n) -> p v d n", v=7, d=2)
    with ExitStack() as ctx:
        def sem(name):
            return ctx.enter_context(nc.semaphore("decay_" + name))
        stored, loaded, act_step, dve_step, turned, sums, w_done = (
            sem(n) for n in ("stored", "loaded", "act_step", "dve_step", "turned", "sums", "scale_ready"))
        block = ctx.enter_context(nc.Block())

        @block.sync
        def _(sp):
            sp.dma_start(s.x_dram, s.x[:]).then_inc(stored, 16)
            sp.dma_start(dts[:], I["dts"]).then_inc(loaded, 16)
            sp.wait_ge(stored, 16)
            for t, name in ((dn.level, "level"), (dn.low, "low"), (dn.tri, "tri"), (dn.conv, "conv_dn"),
                            (dn.onorm, "onorm")):
                sp.dma_start(t[:], I[name]).then_inc(loaded, 16)
            s.sp_load(sp, p0 + 2, p0 % 2)

        @block.gpsimd
        def _(pool):
            s.pool_split(pool, p0 + 1, (p0 + 1) % 2)

        @block.tensor
        def _(pe):
            s.set_free.wait(pe, 1)
            pe_panel(s, pe, p0, p0 % 2, 0)
            pe.wait_ge(dve_step, 8)
            pe.wait_ge(act_step, 5)
            for n in range(NT):
                mm = pe.transpose(psum[:, 3, n * 48:(n + 1) * 48], gb[:, n * P:(n + 1) * P], s.ident[0:48, 0:48])
            mm.then_inc(turned, 1)
            pe.wait_ge(dve_step, 9)
            pe.wait_ge(loaded, 96)
            rhs = gb_tok[:].rearrange("p (n c) -> p n c", c=48)
            n = NT * DN_H
            for d in range(2):
                g = rhs[:, :, 8 * d:8 * d + 8]
                pe.matmul(psum[:, 4, d * n:(d + 1) * n], dn.tri[:, d, :], g, start=True, stop=True)
                mm = pe.matmul(psum[:, 5, d * n:(d + 1) * n], s.ones[:], g, start=True, stop=True)
            mm.then_inc(sums, 1)

        @block.scalar
        def _(act):
            s.act_split(act, p0 + 1, (p0 + 1) % 2)
            act.wait_ge(dve_step, 1)
            act.activation(e[0:16], u[0:16], ACT.Abs).then_inc(act_step, 1)
            act.wait_ge(act_step, 1)
            act.activation(e[0:16], e[0:16], ACT.Exp, scale=-1.0).then_inc(act_step, 1)
            act.wait_ge(loaded, 96)
            act.activation(dts[:, 1:2], dts[:, 1:2], ACT.Exp).then_inc(act_step, 1)
            act.wait_ge(dve_step, 2)
            act.activation(l[0:16], w[0:16], ACT.Ln).then_inc(act_step, 1)
            act.wait_ge(dve_step, 3)
            act.activation(tiled(gb[32:48]), banks(s, 0)[32:48], ACT.Sigmoid).then_inc(act_step, 1)
            act.wait_ge(sums, 1)
            n = NT * DN_H
            act.activation(tok[:, GC_], psum[:, 4, 0:2 * n].rearrange("p (d n) -> p d n", d=2), ACT.Copy
                           ).then_inc(act_step, 1)
            act.activation(gl[:], psum[:, 5, 0:2 * n].rearrange("p (d n) -> p d n", d=2), ACT.Copy,
                           scale=float(D)).then_inc(act_step, 1)
            act.wait_ge(act_step, 7)
            act.activation(tok[:, EG_], tok[:, GC_], ACT.Exp)
            act.activation(tok[:, EL_], gl[:], ACT.Exp)
            act.wait_ge(dve_step, 13)
            act.activation(tok[:, EK_], tok[:, EK_], ACT.Exp)

        @block.vector
        def _(dve):
            dve.wait_ge(s.panel_used.sem, p0 + 1)
            dve.wait_ge(loaded, 96)
            dve.tensor_scalar(tiled(u[0:16]), banks(s, 0)[0:16], dts[:, 0:1], None, ALU.add).then_inc(dve_step, 1)
            dve.wait_ge(act_step, 2)
            dve.tensor_scalar(w[0:16], e[0:16], 1.0, None, ALU.add).then_inc(dve_step, 1)
            dve.memset(gb[:], 0.0).then_inc(dve_step, 1)
            dve.wait_ge(dve_step, 3)
            dve.scalar_tensor_tensor(e[0:16], w[0:16], -1.0, e[0:16], ALU.add, ALU.subtract).then_inc(dve_step, 1)
            dve.reciprocal(r[0:16], w[0:16]).then_inc(dve_step, 1)
            dve.wait_ge(dve_step, 5)
            dve.tensor_tensor(e[0:16], e[0:16], r[0:16], ALU.mult).then_inc(dve_step, 1)
            dve.wait_ge(act_step, 4)
            dve.scalar_tensor_tensor(u[0:16], u[0:16], 0.0, l[0:16], ALU.max, ALU.add).then_inc(dve_step, 1)
            dve.wait_ge(dve_step, 7)
            dve.tensor_tensor(u[0:16], u[0:16], e[0:16], ALU.subtract)
            dve.tensor_scalar(dts[:, 1:2], dts[:, 1:2], -1.0, None, ALU.mult).then_inc(w_done, 1)
            dve.wait_ge(w_done, 1)
            dve.tensor_scalar(gb[0:16], u[0:16], dts[:, 1:2], None, ALU.mult).then_inc(dve_step, 1)
            dve.wait_ge(turned, 1)
            dve.tensor_copy(gb_tok[:], psum[:, 3, 0:NT * 48]).then_inc(dve_step, 1)
            dve.wait_ge(dve_step, 9)
            by = gb_tok[:].rearrange("p (n c) -> p n c", c=48)
            for d in range(2):
                for q, o, f in ((G_, 0, 1.0), (BETA_, 32, 1.0), (NBETA_, 32, -1.0)):
                    v = dve.tensor_scalar(tok[:, q, d].rearrange("p (n h) -> p n h", h=DN_H),
                                          by[:, :, o + 8 * d:o + 8 * d + 8], f, None, ALU.mult)
            v.then_inc(dve_step, 3)
            dve.wait_ge(act_step, 7)
            dve.tensor_tensor(tok[:, EK_], gl[:], tok[:, GC_], ALU.subtract).then_inc(dve_step, 1)
            dve.sem_inc(s.set_free.sem, 1)
    s.p0 += 1
    s.set_free.base += 1


def delta_stage(s, dn):
    nc, psum, I, p0 = s.nc, s.psum, s.I, s.p0
    READS, FULLS = 16, 12
    with ExitStack() as ctx:
        def sem(name):
            return ctx.enter_context(nc.semaphore("dn_" + name))
        head_ready, conv_step, silu_done, sq_ready, recip_done, normed = (
            sem(n) for n in ("head_ready", "conv_step", "silu_done", "sq_ready", "recip_done", "normed"))
        grp_read, grp_full = sem("grp_read"), sem("grp_full")
        e_read, e_ready, d_ready, bt_step, bt_ready, tt_init = (
            sem(n) for n in ("e_read", "e_ready", "d_ready", "bt_step", "bt_ready", "tt_init"))
        qg_ready, pt_ready, kg_ready, kd_ready, bm_ready = (
            sem(n) for n in ("qg_ready", "pt_ready", "kg_ready", "kd_ready", "bm_ready"))
        xl_full, xl_ready, d_full, t_upd, u_full, ub_ready = (
            sem(n) for n in ("xl_full", "xl_ready", "d_full", "t_upd", "u_full", "ub_ready"))
        s_loaded, ws_full, vn_ready, sn_full, s_ready, o_full, o_act, o_dve = (
            sem(n) for n in ("s_loaded", "ws_full", "vn_ready", "sn_full", "s_ready", "o_full", "o_act", "o_dve"))
        fin_full, fin_ready, fin_stored, osq_ready, post_full, post_std, post_step, y_done, y_stored = (
            sem(n) for n in ("fin_full", "fin_ready", "fin_stored", "osq_ready", "post_full", "post_std",
                             "post_step", "y_done", "y_stored"))
        block = ctx.enter_context(nc.Block())

        def blk(t, n):
            return t[:, n * P:(n + 1) * P]

        def by_block(t):
            return t[:].rearrange("p (n w) -> p n w", w=P)

        def of_group(g):
            return psum[:, 3 * g:3 * g + 3, 0:TW].rearrange("p b (n w) -> p b n w", w=P)

        def by_bank(t):
            return t[:].rearrange("p (b n w) -> p b n w", b=3, w=P)

        def const(q, d):
            return dn.hs[:, q, d, :].rearrange("p (n o) -> p n o", o=1).to_broadcast([P, NT, P])

        def const_b(q, d):
            return dn.hs[:, q, d, :].rearrange("p (b n o) -> p b n o", b=3, o=1).to_broadcast([P, 3, 3, P])

        def mask(m, n):
            return m.rearrange("p (o w) -> p o w", o=1).to_broadcast([P, n, P])

        def at_head(t, part, h, j):
            return t[:, ds(h + part * DN_H, 1), j:j + 1].rearrange("p a b -> p (a b)")

        PART = {"q": 0, "k": 1, "v": 2}

        @block.sync
        def _(sp):
            def head(h, last):
                for j in range(4):
                    s.sp_load(sp, 4 * h + (p0 + 2 + j), (p0 + j) % 2)
                if not (isinstance(h, int) and h == 0):
                    sp.wait_ge(o_full, 17 * h)
                for d in range(2):
                    sp.dma_start(dn.state[d][0][:], I["state_delta"][d, ds(h, 1)].rearrange("a p n -> p (a n)")
                                 ).then_inc(s_loaded, 16)
                sp.wait_ge(fin_ready, 2 * h + 2)
                for d in range(2):
                    sp.dma_start(s.O["delta"][ds(h, 1), d].rearrange("a p n -> p (a n)"), dn.fin[d]
                                 ).then_inc(fin_stored, 16)
                sp.wait_ge(y_done, h + 1)
                sp.dma_start(s.y_dram[:, ds(h, 1), :].rearrange("p a t -> p (a t)"), dn.osum[:]
                             ).then_inc(y_stored, 16)
            head(0, False)
            with sp.Fori(1, DN_H) as h:
                head(h, False)
            sp.wait_ge(fin_stored, 32 * DN_H)
            sp.wait_ge(y_stored, 16 * DN_H)

        @block.gpsimd
        def _(pool):
            def mul(out, a, b):
                return pool.tensor_tensor(out, a, b, ALU.mult)

            with pool.Fori(0, DN_H) as h:
                for j in range(4):
                    s.pool_split(pool, 4 * h + (p0 + 1 + j), (p0 + 1 + j) % 2)

                def decayed_q(d):
                    pool.wait_ge(grp_read, READS * h + 8 + d)
                    mul(dn.qg[d][:], dn.qn[:], dn.wt[d][:]).then_inc(qg_ready, 1)

                def kg(d):
                    mul(by_block(dn.ub[d]), by_block(dn.k_tok), const(EG_, d)).then_inc(kg_ready, 1)

                def kd(d):
                    if d == 1:
                        pool.wait_ge(kg_ready, 2 * h + 2)
                        pool.wait_ge(kd_ready, 2 * h + 1)
                    mul(by_block(dn.kd[d]), by_block(dn.k_tok), const(EK_, d)).then_inc(kd_ready, 1)

                def decayed(d):
                    pool.wait_ge(d_ready, 2 * h + (d + 1))
                    pool.wait_ge(grp_read, READS * h + 11)
                    pool.wait_ge(bt_ready, 2 * h + (d + 1))
                    mul(dn.pt[d][:], dn.pt[d][:], dn.qk[:]).then_inc(pt_ready, 1)

                def masked(d, c):
                    n = 36 * h + (18 * d + c)
                    if c or d:
                        pool.wait_ge(xl_full, n - 1)
                    if c == 1 and d == 0:
                        pool.wait_ge(grp_full, FULLS * h + 7)
                    g = c % 3
                    cols = slice(g * TW, (g + 1) * TW)
                    mul(dn.bm[c % 2].rearrange("p (n w) -> p n w", w=P),
                        dn.wt[d][:, cols].rearrange("p (n w) -> p n w", w=P),
                        mask(dn.level[:, d, 1 + c // 3, :], 3)).then_inc(bm_ready, 1)

                pool.wait_ge(head_ready, h + 1)
                pool.wait_ge(normed, 2 * h + 2)
                decayed_q(0)
                pool.wait_ge(bt_ready, 2 * h + 1)
                later = {3: (decayed_q, 1), 6: (kg, 0), 9: (kg, 1), 12: (kd, 0), 15: (kd, 1),
                         21: (decayed, 0), 24: (decayed, 1)}
                for d in range(2):
                    if d == 1:
                        pool.wait_ge(bt_ready, 2 * h + 2)
                    for c in range(SLOTS):
                        masked(d, c)
                        if d * SLOTS + c in later:
                            f, of = later[d * SLOTS + c]
                            f(of)

        @block.tensor
        def _(pe):
            def head(h):
                first = isinstance(h, int)

                def panel(j, g):
                    pe_panel(s, pe, 4 * h + (p0 + j), (p0 + j) % 2, g)

                def read(n):
                    pe.wait_ge(grp_read, READS * h + n)

                def sums(g, t):
                    for i in range(TT):
                        mm = pe.matmul(psum[:, 3 * g + i, 0:TW], s.ones[:], t[:, i * TW:(i + 1) * TW],
                                       start=True, stop=True)
                    return mm

                def nine(g, lhs, rhs, turn=False):
                    for n in range(NT):
                        out = psum[:, 3 * g + n // 3, (n % 3) * P:(n % 3 + 1) * P]
                        if turn:
                            mm = pe.transpose(out, blk(lhs, n), s.ident[:])
                        else:
                            mm = pe.matmul(out, lhs(n), rhs(n), start=True, stop=True)
                    return mm

                pe.wait_ge(post_std, h)
                panel(0, 0)
                panel(1, 1)
                read(1)
                pe.wait_ge(sq_ready, 2 * h + 1)
                sums(0, dn.osum).then_inc(grp_full, 1)
                read(2)
                panel(2, 1)
                read(3)
                pe.wait_ge(sq_ready, 2 * h + 2)
                sums(0, dn.t[0]).then_inc(grp_full, 1)
                read(4)
                pe.wait_ge(normed, 2 * h + 1)
                nine(1, dn.kn, None, True).then_inc(grp_full, 1)
                read(5)
                nine(0, lambda n: blk(dn.kn, n), lambda n: blk(dn.kn, n)).then_inc(grp_full, 1)
                pe.wait_ge(head_ready, h + 1)
                for d in range(2):
                    read(6 + d)
                    nine(1 - d, lambda n: dn.hs[:, G_, d, n:n + 1].to_broadcast([P, P]),
                         lambda n: dn.tri[:, d, :]).then_inc(grp_full, 1)
                read(8)
                pe.wait_ge(e_read, 2 * h + 1)
                panel(3, 1)
                read(9)
                pe.wait_ge(e_read, 2 * h + 2)
                pe.wait_ge(normed, 2 * h + 2)
                nine(0, lambda n: blk(dn.kn, n), lambda n: blk(dn.qn, n)).then_inc(grp_full, 1)
                read(10)
                pe.wait_ge(silu_done, 3 * h + 3)
                nine(1, dn.vf, None, True).then_inc(grp_full, 1)

                def levels(d):
                    read(11 if d == 0 else 13)
                    if d == 1:
                        pe.wait_ge(t_upd, 36 * h + 18)
                    pe.wait_ge(tt_init, 2 * h + (d + 1))
                    nine(0, dn.tt[d], None, True).then_inc(grp_full, 1)
                    read(13 + d)

                    def x_of(c):
                        n = 36 * h + (18 * d + c)
                        g = c % 3
                        pe.wait_ge(bm_ready, n + 1)
                        if c >= 3:
                            pe.wait_ge(t_upd, n - 2)
                        if d or c >= 2:
                            pe.wait_ge(xl_ready, n - 1)
                        for i in range(3):
                            mm = pe.matmul(psum[:, 6 + c % 2, i * P:(i + 1) * P],
                                           dn.bm[c % 2][:, i * P:(i + 1) * P], blk(dn.t[d], 3 * g + i),
                                           start=True, stop=True)
                        mm.then_inc(xl_full, 1)

                    def d_of(c):
                        g = c % 3
                        pe.wait_ge(xl_ready, 36 * h + (18 * d + c + 1))
                        for i in range(3):
                            x = dn.xl[c % 2][:, i * P:(i + 1) * P]
                            if c < SLOTS - NB:
                                pe.matmul(psum[:, g, i * P:(i + 1) * P], blk(dn.tt[d], 3 * g + i), x,
                                          start=True, stop=True)
                            mm = pe.matmul(psum[:, 3 + g, i * P:(i + 1) * P], x, blk(dn.tt[d], 3 * g + i),
                                           start=True, stop=True)
                        mm.then_inc(d_full, 1)
                    x_of(0)
                    for c in range(1, SLOTS):
                        x_of(c)
                        d_of(c - 1)
                    d_of(SLOTS - 1)

                levels(0)
                levels(1)
                for d in range(2):
                    if d == 0:
                        pe.wait_ge(t_upd, 36 * h + 36)
                    else:
                        read(15)
                        pe.wait_ge(ub_ready, 2 * h + 1)
                    pe.wait_ge(kg_ready, 2 * h + (d + 1))
                    nine(0, lambda n: blk(dn.ub[d], n), lambda n: blk(dn.tt[d], n)).then_inc(grp_full, 1)
                    nine(1, lambda n: blk(dn.tt[d], n), lambda n: blk(dn.v_tok, n)).then_inc(u_full, 1)
                read(16)
                pe.wait_ge(ub_ready, 2 * h + 2)
                pe.wait_ge(kd_ready, 2 * h + 2)
                pe.wait_ge(pt_ready, 2 * h + 2)
                pe.wait_ge(qg_ready, 2 * h + 2)
                for d in range(2):
                    mm = pe.matmul(psum[:, 4, 0:P], blk(dn.ub[d], 0), blk(dn.pt[d], 0), start=d == 0, stop=d == 1)
                mm.then_inc(o_full, 1)
                for d in range(2):
                    mm = pe.matmul(psum[:, 1 + 2 * d, 0:P], blk(dn.kd[d], 0), blk(dn.ub[d], 0),
                                   start=True, stop=True)
                mm.then_inc(fin_full, 1)
                pe.wait_ge(s_loaded, 32 * h + 32)
                for t in range(8):
                    n_of = (1 + t, 8 - t)
                    for d in range(2):
                        if t:
                            pe.wait_ge(s_ready, 14 * h + (2 * t - 1 + d))
                        pe.matmul(psum[:, 2 * d, 0:P], blk(dn.wt[d], n_of[d]), dn.state[d][t % 2][:],
                                  start=True, stop=True).then_inc(ws_full, 1)
                    for d in range(2):
                        k = 1 + 2 * t + d
                        if k >= 4:
                            j = k - 4
                            if j < 9:
                                pe.wait_ge(o_act, 9 * h + (j + 1))
                            else:
                                pe.wait_ge(o_dve, 8 * h + (j - 8))
                        pe.matmul(psum[:, 4 + k % 4, 0:P], dn.state[d][t % 2][:], blk(dn.qg[d], n_of[d]),
                                  start=True, stop=False)
                    for d in range(2):
                        k = 1 + 2 * t + d
                        pe.wait_ge(vn_ready, 16 * h + (2 * t + d + 1))
                        if t < 7:
                            if t == 0:
                                pe.wait_ge(fin_ready, 2 * h + 2)
                            pe.matmul(psum[:, 1 + 2 * d, 0:P], blk(dn.kd[d], n_of[d]), dn.vn[d],
                                      start=True, stop=True).then_inc(sn_full, 1)
                        pe.matmul(psum[:, 4 + k % 4, 0:P], dn.vn[d], blk(dn.pt[d], n_of[d]),
                                  start=False, stop=True).then_inc(o_full, 1)
                pe.wait_ge(osq_ready, h + 1)
                sums(0, dn.t[0]).then_inc(post_full, 1)
            with pe.Fori(0, DN_H) as h:
                head(h)

        @block.scalar
        def _(act):
            with act.Fori(0, DN_H) as h:
                def split(j):
                    s.act_split(act, 4 * h + (p0 + j), (p0 + j) % 2)

                def used(j):
                    act.wait_ge(s.panel_used.sem, 4 * h + (p0 + j + 1))

                def full(n):
                    act.wait_ge(grp_full, FULLS * h + n)

                def take(out, g, func=ACT.Copy, **kw):
                    return act.activation(tiled(out[:]), banks(s, g), func, **kw).then_inc(grp_read, 1)

                def silu(n, t, sq):
                    act.wait_ge(conv_step, 21 * h + 7 * n)
                    act.activation(t[:], t[:], ACT.Silu).then_inc(silu_done, 1)
                    if sq is not None:
                        act.wait_ge(silu_done, 3 * h + n)
                        act.activation(sq[:], t[:], ACT.Square).then_inc(sq_ready, 1)

                split(1)
                used(0)
                take(dn.raw["k"], 0)
                split(2)
                act.wait_ge(y_stored, 16 * h)
                silu(1, dn.kn, dn.osum)
                used(1)
                take(dn.raw["q"], 1)
                split(3)
                full(1)
                take(dn.osum, 0, ACT.Sqrt, scale=float(D), bias=s.eps[:, 0:1])
                silu(2, dn.qn, dn.t[0])
                used(2)
                act.wait_ge(y_done, h)
                take(dn.silu_z, 1, ACT.Silu)
                split(4)
                full(2)
                take(dn.t[0], 0, ACT.Sqrt, scale=float(D), bias=s.eps[:, 0:1])
                full(3)
                take(dn.k_tok, 1)
                full(4)
                take(dn.kk, 0)
                for d in range(2):
                    full(5 + d)
                    take(dn.wt[d], 1 - d, ACT.Exp)
                for d in range(2):
                    act.wait_ge(e_ready, 2 * h + (d + 1))
                    act.activation(dn.pt[d][:], dn.pt[d][:], ACT.Exp).then_inc(d_ready, 1)
                used(3)
                take(dn.raw["v"], 1)
                silu(3, dn.vf, None)
                full(7)
                take(dn.qk, 0)
                full(8)
                take(dn.v_tok, 1)
                full(9)
                take(dn.t[0], 0)

                def x_copies(d):
                    for c in range(SLOTS):
                        n = 36 * h + (18 * d + c)
                        act.wait_ge(xl_full, n + 1)
                        if d or c >= 2:
                            act.wait_ge(d_full, n - 1)
                        act.activation(dn.xl[c % 2], psum[:, 6 + c % 2, 0:TW], ACT.Copy).then_inc(xl_ready, 1)
                x_copies(0)
                full(10)
                take(dn.t[1], 0)
                x_copies(1)
                for d in range(2):
                    full(11 + d)
                    take(dn.wt[d], 0)
                act.wait_ge(o_full, 17 * h + 1)
                act.activation(blk(dn.osum, 0), psum[:, 4, 0:P], ACT.Copy).then_inc(o_act, 1)
                act.wait_ge(fin_full, h + 1)
                for d in range(2):
                    act.activation(dn.fin[d], psum[:, 1 + 2 * d, 0:P], ACT.Copy).then_inc(fin_ready, 1)
                for t in range(4):
                    for d in range(2):
                        k = 1 + 2 * t + d
                        act.wait_ge(o_full, 17 * h + (k + 1))
                        act.activation(blk(dn.osum, (1 + t, 8 - t)[d]), psum[:, 4 + k % 4, 0:P], ACT.Copy
                                       ).then_inc(o_act, 1)
                act.wait_ge(o_dve, 8 * h + 8)
                act.activation(dn.t[0][:], dn.osum[:], ACT.Square).then_inc(osq_ready, 1)
                act.wait_ge(post_full, h + 1)
                act.activation(tiled(dn.tt[0][:]), banks(s, 0), ACT.Sqrt, scale=float(D // P),
                               bias=s.eps[:, 0:1]).then_inc(post_std, 1)

        @block.vector
        def _(dve):
            tok = dn.tok[:].rearrange("p (v h) -> p v h", h=DN_H)
            with dve.Fori(0, DN_H) as h:
                dve.tensor_copy(dn.hs[:].rearrange("p a d n -> p (a d n)"),
                                tok[:, :, ds(h, 1)].rearrange("p v a -> p (v a)")).then_inc(head_ready, 1)

                def conv(n, name, out, reads):
                    part, x = PART[name], dn.raw[name]
                    dve.wait_ge(grp_read, READS * h + reads)
                    base = 21 * h + 7 * n
                    dve.tensor_scalar(out[:], x[:], at_head(dn.conv, part, h, 2), None, ALU.mult
                                      ).then_inc(conv_step, 1)
                    for i, (tap, off) in enumerate(((0, -2), (1, -1), (3, 1))):
                        for m, (lo, hi) in enumerate(((0, TP), (TP, T))):
                            a, b = (lo - off, hi) if off < 0 else (lo, hi - off)
                            dve.wait_ge(conv_step, base + (2 * i + m + 1 if i else 1))
                            dve.scalar_tensor_tensor(out[:, a:b], x[:, a + off:b + off],
                                                     at_head(dn.conv, part, h, tap), out[:, a:b],
                                                     ALU.mult, ALU.add).then_inc(conv_step, 1)

                def norm(n, std, t, scale, reads):
                    dve.wait_ge(grp_read, READS * h + reads)
                    dve.reciprocal(std[:], std[:]).then_inc(recip_done, 1)
                    dve.wait_ge(recip_done, 2 * h + n)
                    dve.scalar_tensor_tensor(t[:], t[:], scale, std[:], ALU.mult, ALU.mult).then_inc(normed, 1)

                dve.wait_ge(fin_stored, 32 * h)
                conv(0, "k", dn.kn, 1)
                conv(1, "q", dn.qn, 2)
                norm(1, dn.osum, dn.kn, 1.0, 3)
                norm(2, dn.t[0], dn.qn, P ** -0.5, 5)

                def decay(d):
                    dve.wait_ge(grp_read, READS * h + 8 + d)
                    dve.tensor_tensor(by_bank(dn.pt[d]), of_group(1 - d), const_b(GC_, d), ALU.subtract
                                      ).then_inc(e_read, 1)
                    dve.wait_ge(e_read, 2 * h + (d + 1))
                    dve.tensor_tensor(by_block(dn.pt[d]), by_block(dn.pt[d]), mask(dn.low[:, d, :], NT), ALU.min
                                      ).then_inc(e_ready, 1)

                def kk_beta(d):
                    dve.wait_ge(qg_ready, 2 * h + (d + 1))
                    dve.wait_ge(d_ready, 2 * h + (d + 1))
                    dve.tensor_tensor(dn.wt[d][:], dn.pt[d][:], dn.kk[:], ALU.mult).then_inc(bt_step, 1)
                    dve.wait_ge(bt_step, 4 * h + (2 * d + 1))
                    dve.tensor_tensor(by_block(dn.wt[d]), by_block(dn.wt[d]), const(BETA_, d), ALU.mult
                                      ).then_inc(bt_ready, 1)

                def t_start(d):
                    dve.wait_ge(bt_ready, 2 * h + (d + 1))
                    dve.tensor_tensor(by_block(dn.tt[d]), by_block(dn.wt[d]), mask(dn.level[:, d, 0, :], NT),
                                      ALU.mult).then_inc(bt_step, 1)
                    dve.wait_ge(bt_step, 4 * h + (2 * d + 2))
                    dve.tensor_tensor(by_block(dn.tt[d]), mask(s.ident[:], NT), by_block(dn.tt[d]), ALU.subtract
                                      ).then_inc(tt_init, 1)

                decay(0)
                decay(1)
                kk_beta(0)
                t_start(0)
                conv(2, "v", dn.vf, 10)
                for d in range(2):
                    for c in range(SLOTS):
                        n = 36 * h + (18 * d + c)
                        g = c % 3
                        cols = slice(g * TW, (g + 1) * TW)
                        dve.wait_ge(d_full, n + 1)
                        if c < SLOTS - NB:
                            dve.tensor_tensor(dn.t[d][:, cols], dn.t[d][:, cols], psum[:, g, 0:TW], ALU.subtract)
                        dve.tensor_tensor(dn.tt[d][:, cols], dn.tt[d][:, cols], psum[:, 3 + g, 0:TW],
                                          ALU.subtract).then_inc(t_upd, 1)
                        if d == 0 and c == 9:
                            kk_beta(1)
                        if d == 0 and c == 12:
                            t_start(1)
                for d in range(2):
                    dve.wait_ge(u_full, 2 * h + (d + 1))
                    dve.tensor_tensor(by_bank(dn.ub[d]), of_group(1), const_b(BETA_, d), ALU.mult
                                      ).then_inc(ub_ready, 1)
                for t in range(8):
                    n_of = (1 + t, 8 - t)
                    for d in range(2):
                        n = n_of[d]
                        dve.wait_ge(ws_full, 16 * h + (2 * t + d + 1))
                        if t:
                            dve.wait_ge(o_full, 17 * h + (2 * t + d))
                        else:
                            dve.wait_ge(ub_ready, 2 * h + 2)
                        dve.scalar_tensor_tensor(dn.vn[d], psum[:, 2 * d, 0:P], dn.hs[:, NBETA_, d, n:n + 1],
                                                 blk(dn.ub[d], n), ALU.mult, ALU.add).then_inc(vn_ready, 1)
                    if t < 7:
                        for d in range(2):
                            n = n_of[d]
                            dve.wait_ge(sn_full, 14 * h + (2 * t + d + 1))
                            if t:
                                dve.wait_ge(s_ready, 14 * h + (2 * t + d - 1))
                            dve.scalar_tensor_tensor(dn.state[d][(t + 1) % 2][:], dn.state[d][t % 2][:],
                                                     dn.hs[:, EL_, d, n:n + 1], psum[:, 1 + 2 * d, 0:P],
                                                     ALU.mult, ALU.add).then_inc(s_ready, 1)
                    if t >= 4:
                        for d in range(2):
                            k = 1 + 2 * t + d
                            dve.wait_ge(o_full, 17 * h + (k + 1))
                            dve.wait_ge(o_act, 9 * h + 9)
                            o = blk(dn.osum, n_of[d])
                            dve.tensor_tensor(o, o, psum[:, 4 + k % 4, 0:P], ALU.add).then_inc(o_dve, 1)
                dve.wait_ge(post_std, h + 1)
                dve.reciprocal(dn.tt[0][:], dn.tt[0][:]).then_inc(post_step, 1)
                dve.wait_ge(post_step, 2 * h + 1)
                dve.scalar_tensor_tensor(dn.osum[:], dn.osum[:], dn.onorm[:, 0:1], dn.tt[0][:], ALU.mult, ALU.mult
                                         ).then_inc(post_step, 1)
                dve.wait_ge(post_step, 2 * h + 2)
                dve.tensor_tensor(dn.osum[:], dn.osum[:], dn.silu_z[:], ALU.mult).then_inc(y_done, 1)
    s.p0 += ODD_PANELS


def reload_stage(s):
    nc = s.nc
    with ExitStack() as ctx:
        x_in = ctx.enter_context(nc.semaphore("x_in"))
        y_in = ctx.enter_context(nc.semaphore("y_in"))
        high = ctx.enter_context(nc.semaphore("y_high"))
        y = s.at("y_delta", [P, KC, T], F32, s.rest)
        block = ctx.enter_context(nc.Block())

        @block.sync
        def _(sp):
            sp.dma_start(y[:], s.y_dram).then_inc(y_in, 16)
            sp.dma_start(s.x[:], s.x_dram).then_inc(x_in, 16)
            sp.wait_ge(x_in, 16)

        @block.scalar
        def _(act):
            act.wait_ge(y_in, 16)
            for c in range(KC):
                act.activation(s.hh[:, c, :], y[:, c, :], ACT.Copy).then_inc(high, 1)

        @block.vector
        def _(dve):
            for c in range(KC):
                dve.wait_ge(high, c + 1)
                dve.tensor_tensor(s.hl[:, c, :], y[:, c, :], s.hh[:, c, :].bitcast(F32), ALU.subtract)


def pack_delta(f):
    bf = mybir.dt.np(BF16)
    i = np.arange(P)
    j, c = i[:, None], i[None, :]
    level = np.zeros((P, 2, NL + 1, P), np.float32)
    for n, b in enumerate([1] + LEVELS):
        pair = (j // (2 * b) == c // (2 * b)) & (j // b % 2 == 0) & (c // b % 2 == 1)
        level[:, 0, n], level[:, 1, n] = pair, pair.T
    low = np.stack([np.where(j <= c, 0, NEG), np.where(j >= c, 0, NEG)], 1)
    tri = np.stack([j <= c, j >= c], 1).astype(np.float32)
    return {
        "level": level.astype(bf), "low": low.astype(bf), "tri": tri,
        "dts": np.stack([f["dn_dt_bias"][0].reshape(16), f["dn_a_log"][0].reshape(16)], 1),
        "conv_dn": columns(f["conv_dn"][0]).transpose(0, 2, 1),
        "onorm": f["dn_o_norm"][0][:, None],
        "state_delta": f["state_delta"][0, 0],
    }


def build(nc, I, O):
    with ExitStack() as ctx:
        s = Trunk(nc, ctx, I, O)
        norm_stage(s, 0, 0, load=True)
        even = even_buffer(s)
        in_proj_stage(s, even, EVEN_PANELS)
        rg_stage(s, even)
        attention_stage(s, even)
        out_proj_stage(s, 0)
        norm_stage(s, 0, 1)
        ffn_stage(s, 0)
        norm_stage(s, 1, 0)
        s.x_dram = nc.dram_tensor("x_spill", [P, KC, T], F32).ap()
        s.y_dram = nc.dram_tensor("y_spill", [P, KC, T], F32).ap()
        dn = Delta(s)
        decay_stage(s, dn)
        delta_stage(s, dn)
        reload_stage(s)
        out_proj_stage(s, 1)
        norm_stage(s, 1, 1)
        ffn_stage(s, 1)
        final_stage(s)


def feature_major(a):
    return np.asarray(a).T.reshape(-1, P, a.shape[0]).transpose(1, 0, 2)


def columns(v):
    v = np.asarray(v)
    return np.moveaxis(v.reshape(*v.shape[:-1], -1, P), -1, 0)


def panels(w):
    w = np.asarray(w)
    return w.reshape(KC, P, -1, P).transpose(2, 1, 0, 3).reshape(-1, P, 1024)


def pack(inp):
    f = {k: np.asarray(v) for k, v in inp.items()}
    qperm = np.concatenate([np.arange(HD) + HD * h for c in range(4) for h in (c, c + 4)])
    w_in = f["w_in_even"][0]
    w_in = np.concatenate([w_in[:, :1024], w_in[:, 1024:1536][:, qperm], w_in[:, 1536:]], axis=1)
    w_out = f["w_out_even"][0]
    w_out = np.concatenate([w_out[:512], w_out[512:][qperm]], axis=0)
    stream = [panels(w_in), panels(w_out)]

    def ffn(layer):
        gate_up = panels(f["w_gu"][layer])
        down = f["w_down"][layer].reshape(FF_G, 2, P, 2, D // 2).transpose(0, 3, 2, 1, 4).reshape(-1, P, D)
        order = []
        for j in range(FF_G):
            for c in (2 * j, 2 * j + 1):
                order += [gate_up[c], gate_up[FF_CH + c]]
            if j:
                order += [down[2 * j - 2], down[2 * j - 1]]
        return np.stack(order + [down[-2], down[-1]])

    stream.append(ffn(0))
    w_odd = f["w_in_odd"][0]
    ab = w_odd[:, 4096:].reshape(D, 2, 16)
    ab_panel = np.zeros((D, P), np.float32)
    ab_panel[:, 0:16], ab_panel[:, 32:48] = ab[:, 0], ab[:, 1]
    stream.append(panels(ab_panel))
    heads = panels(w_odd[:, :4096]).reshape(4, DN_H, P, 1024)[[1, 0, 3, 2]]
    stream.append(heads.transpose(1, 0, 2, 3).reshape(-1, P, 1024))
    stream += [panels(f["w_out_odd"][0]), ffn(1), np.zeros((PAD, P, 1024), np.float32)]

    rgw = np.zeros((RG_CH, P, 4, P), np.float32)
    for d in range(2):
        for j, w in enumerate((f["rg_wa"], f["rg_wx"])):
            for b in range(8):
                o = 64 * (b % 2)
                rgw[b // 2, o:o + 64, 2 * d + j, o:o + 64] = w[0, d, b]
    rgb = np.stack([f["rg_ba"][0], f["rg_bx"][0]], axis=1).reshape(4, 512)
    i = np.arange(P)
    prev = np.where(i[None, :] >= i[:, None], 0, NEG).astype(np.float32)
    nxt = np.where(i[None, :] <= i[:, None], 0, NEG).astype(np.float32)
    none = np.full((P, P), NEG, np.float32)
    window = np.stack([np.stack([none if b == 0 else prev, none if b == 7 else nxt], 1) for b in range(8)], 1)
    inv = ROPE_BASE ** (-np.arange(0, 32, 2, dtype=np.float32) / 32)
    tok = np.arange(TL)
    ang = [(tok // GRID_W)[None].astype(np.float32) * inv[:, None],
           (tok % GRID_W)[None].astype(np.float32) * inv[:, None]]
    ang = np.concatenate([ang[0], ang[0], ang[1], ang[1]] * 2).astype(np.float32)
    rope = np.zeros((P, P), np.float32)
    for m in range(P):
        if m % 32 < 16:
            rope[m + 16, m] = -1.0
        else:
            rope[m - 16, m] = 1.0
    head_of = [h for c in range(4) for h in (c, c + 4)]
    bf = mybir.dt.np(BF16)
    return {
        "x": feature_major(np.concatenate([f["x_prompt"][0], f["x_sample"][0]])),
        "cond": np.broadcast_to(np.stack([f["c_ctx"], f["c"][0]]), (P, 2, D)),
        "stream": np.concatenate(stream),
        "wmod": np.concatenate([w.T for w in f["w_mod"]]).reshape(-1, P, D),
        "bmod": np.repeat(columns(f["b_mod"].reshape(-1))[:, :, None], 2, 2),
        "gain": columns(np.stack([f["g_mix"][0], f["g_ffn"][0], f["g_mix"][1], f["g_ffn"][1], f["g_final"]])),
        "ones": np.full((P, P), 1.0 / D, np.float32),
        "ident": np.eye(P, dtype=np.float32),
        "eps": np.full((P, 1), EPS, np.float32),
        "conv_rg": columns(np.concatenate([f["conv_rg"][0], f["conv_rg_b"]])).transpose(0, 2, 1),
        "rgw": rgw.reshape(RG_CH, P, 4 * P),
        "rgb": columns(rgb).transpose(0, 2, 1),
        "lam": columns(f["rg_lam"][0]).transpose(0, 2, 1),
        "h0": columns(f["state_rglru"][0, 0]).transpose(0, 2, 1),
        "ctx_k": f["cache_attn_k"][0, 0].reshape(TP, P).T,
        "ctx_v": f["cache_attn_v"][0, 0].reshape(TP, P),
        "sink": np.broadcast_to(f["attn_sink"][0][head_of], (P, HEADS)),
        "window": window.astype(bf),
        "ident_bf": np.eye(P, dtype=bf),
        "cos": np.cos(ang), "sin": np.sin(ang), "rope": rope,
    } | pack_delta(f)


def kernel(**inputs):
    import concourse.bacc as bacc
    from concourse.bass_utils import run_bass_kernel_spmd

    arrays = {f"in_{k}": np.ascontiguousarray(v) for k, v in pack(inputs).items()}
    nc = bacc.Bacc("TRN2", target_bir_lowering=False, num_devices=1)
    I = {k[3:]: nc.dram_tensor(k, v.shape, mybir.dt.from_np(v.dtype), kind="ExternalInput").ap()
         for k, v in arrays.items()}
    O = {k: nc.dram_tensor(f"out_{k}", shape, F32, kind="ExternalOutput").ap() for k, shape in OUTS.items()}
    build(nc, I, O)
    r = run_bass_kernel_spmd(nc, [arrays], core_ids=[0]).results[0]
    return unpack({k: r[f"out_{k}"] for k in OUTS})


OUTS = {"y": (P, KC, T), "k": (P, TP), "v": (P, TP), "rg": (P, RG_CH, 2), "delta": (DN_H, 2, P, P)}


def unpack(r):
    y = r["y"].transpose(2, 1, 0).reshape(T, D)
    kv = [r[n].T.reshape(1, 1, TP, 2, HD) for n in ("k", "v")]
    rg = r["rg"].transpose(2, 1, 0).reshape(1, 1, 2, 512)
    delta = r["delta"].transpose(1, 0, 2, 3).reshape(1, 1, 2, DN_H, P, P)
    return (y[None, :TP], y[None, TP:], *(np.ascontiguousarray(a) for a in (*kv, rg, delta)))
```

```python
from contextlib import ExitStack

import numpy as np

import concourse.bass as bass
from concourse import mybir

F32 = mybir.dt.float32
F32R = mybir.dt.float32r
BF16 = mybir.dt.bfloat16
ACT = mybir.ActivationFunctionType
ALU = mybir.AluOpType
AX = mybir.AxisListType
ds = bass.ds

P = 128
D = 1024
KC = D // P
TP = 128
TL = 1024
T = TP + TL
NT = T // P
TW = 384
TT = T // TW
EPS = 1e-6
NEG = -1e30
RG_CH = 4
RG_C = 8.0
HD = 64
HEADS = 8
GRID_W = 64
ROPE_BASE = 10000.0
DN_H = 8
FF_CH = 22
FF_G = FF_CH // 2
EVEN_PANELS = 14
ODD_PANELS = 4 * DN_H
OUT_PANELS = 8
FFN_PANELS = 6 * FF_G
STREAM = EVEN_PANELS + OUT_PANELS + FFN_PANELS + 1 + ODD_PANELS + OUT_PANELS + FFN_PANELS
PAD = 2
SH1, SC1, GA1, SH2, SC2, GA2 = range(6)


def three_products(pe, out, wh, wl, xh, xl, first, last):
    pe.matmul(out, wh, xh, start=first, stop=False)
    pe.matmul(out, wh, xl, start=False, stop=False)
    return pe.matmul(out, wl, xh, start=False, stop=last)


class Count:

    def __init__(self, nc, ctx, name):
        self.sem = ctx.enter_context(nc.semaphore(name))
        self.base = 0

    def wait(self, eng, n):
        eng.wait_ge(self.sem, n + self.base)


class Trunk:

    def __init__(self, nc, ctx, I, O):
        self.nc, self.I, self.O = nc, I, O
        self.top = (nc.sbuf_base + 31) // 32 * 32

        def sb(name, shape, dt=F32):
            t = self.at(name, shape, dt, self.top)
            self.top = (self.top + self.size(shape, dt) + 31) // 32 * 32
            return t

        self.psum = ctx.enter_context(nc.psum_tensor("psum", [P, 8, 512], F32))
        self.mod = sb("mod", [P, 96, 2])
        self.gain = sb("gain", [P, 5, KC])
        self.ones = sb("ones", [P, P])
        self.ident = sb("ident", [P, P])
        self.onep = sb("one_plus_scale", [P, KC, 2])
        self.eps = sb("eps", [P, 1])
        self.acc = sb("mod_sums", [P, 2, 2])
        self.raw = [sb(f"panel_raw{i}", [P, 1024]) for i in range(2)]
        self.wh = [sb(f"panel_high{i}", [P, 1024], F32R) for i in range(2)]
        self.wl = [sb(f"panel_low{i}", [P, 1024], F32R) for i in range(2)]
        self.h_at = self.top
        self.hh = sb("h_high", [P, KC, T], F32R)
        self.hl = sb("h_low", [P, KC, T], F32R)
        self.x_at = self.top
        self.x = sb("x", [P, KC, T])
        self.rest = self.top
        self.hi_chunk = self.h_at
        self.lo_chunk = self.h_at + 4 * KC * T

        def count(name):
            return Count(nc, ctx, name)

        self.raw_full = [count(f"raw_full{i}") for i in range(2)]
        self.split_high = count("split_high")
        self.split_low = count("split_low")
        self.panel_used = count("panel_used")
        self.p0 = 0
        self.modvec_ready = count("modvec_ready")
        self.squared = count("squared")
        self.mean_ready = count("mean_ready")
        self.std_ready = count("std_ready")
        self.rstd_ready = count("rstd_ready")
        self.normed, self.normed_pool = count("normed"), count("normed_pool")
        self.high_ready = count("high_ready")
        self.low_ready = count("low_ready")
        self.low_pool = count("low_pool")
        self.shifted, self.high_pool = count("shifted"), count("high_pool")
        self.set_free = count("set_free")
        self.gate_ready = count("gate_ready")
        self.prod_ready = count("prod_ready")
        self.mid_high = count("mid_high")
        self.mid_low = count("mid_low")
        self.added = count("added")
        self.down_full = count("down_full")
        self.mod_full = [count(f"mod_full{i}") for i in range(2)]
        self.mod_step = count("mod_step")
        self.rows_full, self.rows_ready = count("cond_rows_full"), count("cond_rows_ready")

    def at(self, name, shape, dt, offset):
        return self.nc.alloc_sbuf_tensor_at(name, shape, dt, offset=offset)

    @staticmethod
    def size(shape, dt=F32):
        n = 2 if dt == BF16 else 4
        for x in shape[1:]:
            n *= x
        return n

    def placer(self, stage, offset, end):
        where = [offset]

        def sb(name, shape, dt=F32):
            t = self.at(f"{stage}_{name}", shape, dt, where[0])
            where[0] = (where[0] + self.size(shape, dt) + 31) // 32 * 32
            assert where[0] <= end, (stage, name, where[0] - end)
            return t
        return sb

    def sp_load(self, sp, p, buf):
        sp.wait_ge(self.split_low.sem, p - 1)
        src = self.I["stream"][p] if isinstance(p, int) else self.I["stream"][ds(p, 1)].rearrange("a p n -> p (a n)")
        sp.dma_start(self.raw[buf][:], src).then_inc(self.raw_full[buf].sem, 16)

    def sp_stream(self, sp, n):
        p0 = self.p0
        with sp.Fori(0, n // 2) as g:
            for i in range(2):
                self.sp_load(sp, 2 * g + (p0 + 2 + i), (p0 + i) % 2)
        if n % 2:
            self.sp_load(sp, p0 + n + 1, (p0 + n + 1) % 2)

    def act_split(self, act, p, buf):
        act.wait_ge(self.raw_full[buf].sem, (p + (2 - buf)) * 8)
        if not (isinstance(p, int) and p < 2):
            act.wait_ge(self.panel_used.sem, p - 1)
        act.activation(self.wh[buf][:], self.raw[buf][:], ACT.Copy).then_inc(self.split_high.sem, 1)

    def pool_split(self, pool, p, buf):
        pool.wait_ge(self.split_high.sem, p + 1)
        pool.tensor_tensor(self.wl[buf][:], self.raw[buf][:], self.wh[buf][:].bitcast(F32),
                           ALU.subtract).then_inc(self.split_low.sem, 1)

    def pool_stream(self, pool, n, done=0):
        p0, n = self.p0 + done, n - done
        with pool.Fori(0, n // 2) as g:
            for i in range(2):
                self.pool_split(pool, 2 * g + (p0 + 1 + i), (p0 + 1 + i) % 2)
        if n % 2:
            self.pool_split(pool, p0 + n, (p0 + n) % 2)


def segments(t):
    return [(0, TP, 0), (TP, TW - TP, 1)] if t == 0 else [(0, TW, 1)]


FIRST_MOD = 8
MOD_LAYER = 24


class Mod:

    def __init__(self, s, name, offset, pairs=2):
        self.rows = s.at(f"{name}_cond_rows", [P, 2, D], F32, offset)
        self.panels = [s.at(f"{name}_mod_panels{i}", [P, 2, D], F32, offset + 8192 * (i + 1))
                       for i in range(pairs)]


def sp_mod(s, sp, m, g, par):
    if not (isinstance(g, int) and g < FIRST_MOD + 2):
        sp.wait_ge(s.mod_step.sem, 5 * g - 6)
    sp.dma_start(m.panels[par][:], s.I["wmod"][ds(2 * g, 2)].rearrange("a p n -> p a n")
                 ).then_inc(s.mod_full[par].sem, 16)


def dve_mod(s, dve, panels, rows, g):
    for a in range(2):
        for m in range(2):
            n = 2 * a + m
            if n or not isinstance(g, int) or g > 0:
                dve.wait_ge(s.mod_step.sem, 5 * g + n)
            s.nc.vector.tensor_tensor_reduce(
                out=s.psum[:, 6:8, :], in0=panels[:, a, :].rearrange("p (b w) -> p b w", b=2),
                in1=rows[:, m, :].rearrange("p (b w) -> p b w", b=2), scale=1.0, scalar=0.0,
                op0=ALU.mult, op1=ALU.add, accum_out=s.acc[:, a, m:m + 1]).then_inc(s.mod_step.sem, 1)
    dve.wait_ge(s.mod_step.sem, 5 * g + 4)
    to = s.mod[:, ds(2 * g, 2), :]
    dve.tensor_tensor(to, to, s.acc[:], ALU.add).then_inc(s.mod_step.sem, 1)


def dve_mod_ring(s, dve, m, g, par):
    dve.wait_ge(s.mod_full[par].sem, 8 * g - (48 + 8 * par))
    dve_mod(s, dve, m.panels[par], m.rows, g)


class Squares:

    STEPS = 2 * (KC - 1)
    BANKS = (6, 7, 5)

    def __init__(self, s):
        self.s = s
        self.acc, self.sq = (s.at(part, [P, T], F32, s.rest + (8 + i) * 4 * T)
                             for i, part in enumerate(("square_sum", "square")))

    def dve(self, dve, f):
        s, x = self.s, self.s.x[:, f, :]
        if f >= 2:
            s.squared.wait(dve, 2 * f - 1)
        dve.tensor_tensor((self.sq if f else self.acc)[:], x, x, ALU.mult).then_inc(s.squared.sem, 1)
        if 0 < f < KC - 1:
            s.squared.wait(dve, 2 * f)
            dve.tensor_tensor(self.acc[:], self.acc[:], self.sq[:], ALU.add).then_inc(s.squared.sem, 1)

    def pe(self, pe):
        s = self.s
        s.squared.wait(pe, 0)
        for t in range(TT):
            cols = slice(t * TW, (t + 1) * TW)
            pe.matmul(s.psum[:, self.BANKS[t], 0:TW], s.ones[:], self.acc[:, cols], start=True, stop=False)
            pe.matmul(s.psum[:, self.BANKS[t], 0:TW], s.ones[:], self.sq[:, cols], start=False, stop=True
                      ).then_inc(s.mean_ready.sem, 1)

    def done(self):
        self.s.squared.base += self.STEPS


class Norm:

    POOL = (5, 6, 7)

    def __init__(self, s, ctx, layer, which, load=False, squares=None):
        self.s, self.layer, self.which, self.load = s, layer, which, load
        shift, scale = (SH1, SC1) if which == 0 else (SH2, SC2)
        self.squares = squares
        self.sh = (layer * 6 + shift) * 8
        self.sc = (layer * 6 + scale) * 8
        sb = s.placer(f"norm{layer}{which}", s.rest, s.rest + 46080)
        if load:
            self.sq = [sb(f"square{i}", [P, KC, TW]) for i in range(2)]
        self.std = [sb(f"std{i}", [P, TW]) for i in range(TT)]
        self.rstd = [sb(f"rstd{i}", [P, TW]) for i in range(TT)]
        self.xn = sb("x_scaled", [P, KC, TW])
        if load:
            def sem(name):
                return ctx.enter_context(s.nc.semaphore(name))
            self.small = sem("constants_full")
            self.x_full = [sem(f"x_full{t}") for t in range(TT)]
            self.pair_full = [sem(f"first_mod{i}") for i in range(5)]
            self.m = Mod(s, "first", s.h_at, FIRST_MOD)

    @staticmethod
    def load_of(g):
        return g if g < 2 else 1 + g // 2

    def wait_tile(self, eng, t):
        s = self.s
        s.low_ready.wait(eng, (t + 1) * (KC - len(self.POOL)))
        s.low_pool.wait(eng, (t + 1) * len(self.POOL))

    def wait_chunk(self, eng, t, c):
        s, mine = self.s, self.dves()
        if c in self.POOL:
            s.low_pool.wait(eng, t * len(self.POOL) + self.POOL.index(c) + 1)
        else:
            s.low_ready.wait(eng, t * len(mine) + mine.index(c) + 1)

    def sp(self, sp):
        s, I = self.s, self.s.I
        if self.load:
            m, x = self.m, s.x
            sp.dma_start(m.rows[:], I["cond"]).then_inc(s.rows_full.sem, 16)
            for t, name in ((s.mod, "bmod"), (s.gain, "gain"), (s.ones, "ones"), (s.eps, "eps"),
                            (s.ident, "ident")):
                sp.dma_start(t[:], I[name]).then_inc(self.small, 16)
            for g in range(FIRST_MOD):
                sp.dma_start(m.panels[g][:], I["wmod"][2 * g:2 * g + 2].rearrange("a p n -> p a n")
                             ).then_inc(self.pair_full[self.load_of(g)], 16)
                if 2 <= g < 2 + TT:
                    cols = slice((g - 2) * TW, (g - 1) * TW)
                    sp.dma_start(x[:, :, cols], I["x"][:, :, cols]).then_inc(self.x_full[g - 2], 16)
            for p in range(2):
                sp.dma_start(s.raw[p][:], I["stream"][p]).then_inc(s.raw_full[p].sem, 16)

    def bank(self, t):
        return 4 + t % 2 if self.load else Squares.BANKS[t]

    def act(self, act):
        s, x, psum, load = self.s, self.s.x, self.s.psum, self.load
        if load:
            act.wait_ge(s.rows_full.sem, 16)
            act.activation(self.m.rows[:], self.m.rows[:], ACT.Silu).then_inc(s.rows_ready.sem, 1)
            act.wait_ge(self.small, 16 * 5)

        def square(t):
            if t >= 2:
                s.mean_ready.wait(act, t - 1)
            act.wait_ge(self.x_full[t], 16)
            for i in range(2):
                act.activation(self.sq[t % 2][:, 4 * i:4 * i + 4, :], x[:, 4 * i:4 * i + 4, t * TW:(t + 1) * TW],
                               ACT.Square).then_inc(s.squared.sem, 1)

        def root(t):
            s.mean_ready.wait(act, t + 1)
            act.activation(self.std[t][:], psum[:, self.bank(t), 0:TW], ACT.Sqrt, bias=s.eps[:, 0:1]
                           ).then_inc(s.std_ready.sem, 1)
        if load:
            square(0)
            square(1)
        root(0)
        root(1)
        if load:
            square(2)
        root(2)
        if load:
            act.wait_ge(s.raw_full[0].sem, 16)
            act.activation(s.wh[0][:], s.raw[0][:], ACT.Copy).then_inc(s.split_high.sem, 1)
        mine, pools = self.dves(), len(self.POOL)

        def high(t, n):
            c = mine[n]
            s.normed.wait(act, t * len(mine) + n + 1)
            for o, w, i in segments(t):
                a = act.activation(s.hh[:, c, t * TW + o:t * TW + o + w], self.xn[:, c, o:o + w],
                                   ACT.Identity, bias=s.mod[:, self.sh + c, i:i + 1])
            a.then_inc(s.high_ready.sem, 1)

        def shift(t, n):
            c = self.POOL[n]
            s.normed_pool.wait(act, t * pools + n + 1)
            if t == n == 0:
                s.modvec_ready.wait(act, 1)
            for o, w, i in segments(t):
                xs = self.xn[:, c, o:o + w]
                a = act.activation(xs, xs, ACT.Identity, bias=s.mod[:, self.sh + c, i:i + 1],
                                   scale=s.onep[:, c, i:i + 1])
            a.then_inc(s.shifted.sem, 1)

        def high_pool(t, n):
            s.shifted.wait(act, t * pools + n + 1)
            act.activation(s.hh[:, self.POOL[n], t * TW:(t + 1) * TW], self.xn[:, self.POOL[n], :], ACT.Copy
                           ).then_inc(s.high_pool.sem, 1)

        for t in range(TT):
            for n in range(len(mine)):
                high(t, n)
                (shift, high_pool)[n % 2](t, n // 2)
            high_pool(t, len(self.POOL) - 1)

    def pe(self, pe):
        s = self.s
        if not self.load:
            self.squares.pe(pe)
            return
        for t in range(TT):
            if t >= 2:
                s.std_ready.wait(pe, t - 1)
            for c in range(KC):
                if c % 4 == 0:
                    s.squared.wait(pe, 2 * t + 1 + c // 4)
                mm = pe.matmul(s.psum[:, self.bank(t), 0:TW], s.ones[:], self.sq[t % 2][:, c, :],
                               start=c == 0, stop=c == KC - 1)
            mm.then_inc(s.mean_ready.sem, 1)

    def dves(self):
        return [c for c in range(KC) if c not in self.POOL]

    def pool(self, pool):
        s, pools = self.s, len(self.POOL)
        if self.load:
            s.pool_split(pool, 0, 0)
        for t in range(TT):
            cols = slice(t * TW, (t + 1) * TW)
            s.rstd_ready.wait(pool, t + 1)
            for i, c in enumerate(self.POOL):
                if t:
                    s.low_pool.wait(pool, (t - 1) * pools + i + 1)
                pool.tensor_tensor(self.xn[:, c, :], s.x[:, c, cols], self.rstd[t][:], ALU.mult
                                   ).then_inc(s.normed_pool.sem, 1)
            for i, c in enumerate(self.POOL):
                s.high_pool.wait(pool, t * pools + i + 1)
                pool.tensor_tensor(s.hl[:, c, cols], self.xn[:, c, :], s.hh[:, c, cols].bitcast(F32),
                                   ALU.subtract).then_inc(s.low_pool.sem, 1)

    def dve(self, dve):
        s, x = self.s, self.s.x

        def reciprocal(t):
            s.std_ready.wait(dve, t + 1)
            dve.reciprocal(self.rstd[t][:], self.std[t][:]).then_inc(s.rstd_ready.sem, 1)

        if self.load:
            dve.sem_inc(s.set_free.sem, 2)
            dve.sem_inc(s.added.sem, 2)
            dve.wait_ge(self.small, 16 * 5)
            dve.wait_ge(s.rows_ready.sem, 1)
            for g in range(FIRST_MOD):
                dve.wait_ge(self.pair_full[self.load_of(g)], 16 if g < 2 else 32)
                dve_mod(s, dve, self.m.panels[g], self.m.rows, g)
                for t in {3: (0, 1), FIRST_MOD - 2: (2,)}.get(g, ()):
                    reciprocal(t)
            dve.wait_ge(s.mod_step.sem, 5 * FIRST_MOD)
        for i in range(2):
            v = dve.scalar_tensor_tensor(s.onep[:, :, i], s.mod[:, self.sc:self.sc + KC, i], 1.0,
                                         s.gain[:, 2 * self.layer + self.which, :], ALU.add, ALU.mult)
        v.then_inc(s.modvec_ready.sem, 1)
        s.modvec_ready.wait(dve, 1)
        mine = self.dves()
        for t in range(TT):
            if not self.load:
                reciprocal(t)
            s.rstd_ready.wait(dve, t + 1)
            for n, c in enumerate(mine):
                if t >= 1:
                    s.low_ready.wait(dve, (t - 1) * len(mine) + n + 1)
                for o, w, i in segments(t):
                    v = dve.scalar_tensor_tensor(self.xn[:, c, o:o + w], x[:, c, t * TW + o:t * TW + o + w],
                                                 s.onep[:, c, i:i + 1], self.rstd[t][:, o:o + w],
                                                 ALU.mult, ALU.mult)
                v.then_inc(s.normed.sem, 1)
            for n, c in enumerate(mine):
                s.high_ready.wait(dve, t * len(mine) + n + 1)
                for o, w, i in segments(t):
                    cols = slice(t * TW + o, t * TW + o + w)
                    v = dve.scalar_tensor_tensor(s.hl[:, c, cols], self.xn[:, c, o:o + w],
                                                 s.mod[:, self.sh + c, i:i + 1],
                                                 s.hh[:, c, cols].bitcast(F32), ALU.add, ALU.subtract)
                v.then_inc(s.low_ready.sem, 1)

    def done(self):
        s = self.s
        s.modvec_ready.base += 1
        s.std_ready.base += TT
        s.rstd_ready.base += TT
        s.mean_ready.base += TT
        if self.load:
            s.squared.base += 2 * TT
        for c in (s.normed_pool, s.shifted, s.high_pool, s.low_pool):
            c.base += TT * len(self.POOL)
        for c in (s.normed, s.high_ready, s.low_ready):
            c.base += TT * (KC - len(self.POOL))


def pe_chunk(s, pe, buf, k):
    w = slice(k * P, (k + 1) * P)
    for t in range(TT):
        cols = slice(t * TW, (t + 1) * TW)
        mm = three_products(pe, s.psum[:, t, 0:TW], s.wh[buf][:, w], s.wl[buf][:, w], s.hh[:, k, cols],
                            s.hl[:, k, cols], k == 0, k == KC - 1)
    return mm


def pe_panel(s, pe, p, buf, group, norm=None):
    pe.wait_ge(s.split_low.sem, p + 1)
    for t in range(TT):
        for k in range(KC):
            if norm is not None:
                norm.wait_chunk(pe, t, k)
            mm = three_products(pe, s.psum[:, 3 * group + t, 0:TW], s.wh[buf][:, k * P:(k + 1) * P],
                                s.wl[buf][:, k * P:(k + 1) * P], s.hh[:, k, t * TW:(t + 1) * TW],
                                s.hl[:, k, t * TW:(t + 1) * TW], k == 0, k == KC - 1)
    mm.then_inc(s.panel_used.sem, 1)


def pe_first_panels(s, pe, p, norm):
    for t in range(TT):
        cols = slice(t * TW, (t + 1) * TW)
        for i in range(2):
            buf = (p + i) % 2
            if t == 0:
                pe.wait_ge(s.split_low.sem, p + i + 1)
            for k in range(KC):
                if i == 0:
                    norm.wait_chunk(pe, t, k)
                w = slice(k * P, (k + 1) * P)
                mm = three_products(pe, s.psum[:, 3 * i + t, 0:TW], s.wh[buf][:, w], s.wl[buf][:, w],
                                    s.hh[:, k, cols], s.hl[:, k, cols], k == 0, k == KC - 1)
            if t == TT - 1:
                mm.then_inc(s.panel_used.sem, 1)


def banks(s, group):
    return s.psum[:, 3 * group:3 * group + TT, 0:TW]


def tiled(ap):
    return ap.rearrange("p (t w) -> p t w", w=TW)


def row(ap, c):
    return ap[:, c, :] if isinstance(c, int) else ap[:, ds(c, 1), :].rearrange("p a t -> p (a t)")


def in_proj_stage(s, out, n, norm):
    p0 = s.p0
    m = s.mods = Mod(s, "in", s.x_at)
    with s.nc.Block() as block:

        @block.sync
        def _(sp):
            norm.sp(sp)
            norm.wait_tile(sp, TT - 1)
            sp.dma_start(m.rows[:], s.I["cond"]).then_inc(s.rows_full.sem, 16)
            for i in range(2):
                sp_mod(s, sp, m, FIRST_MOD + i, i)

            def body(g):
                for i in range(2):
                    s.sp_load(sp, 2 * g + (p0 + 2 + i), (p0 + i) % 2)
                    sp_mod(s, sp, m, 2 * g + (FIRST_MOD + 2 + i), i)
            with sp.Fori(0, n // 2) as g:
                body(g)

        @block.gpsimd
        def _(pool):
            norm.pool(pool)
            s.pool_stream(pool, n)

        @block.scalar
        def _(act):
            norm.act(act)

            def body(g, rows=False):
                for i in range(2):
                    s.act_split(act, 2 * g + (p0 + i + 1), (p0 + i + 1) % 2)
                    if rows and i == 0:
                        act.wait_ge(s.rows_full.sem, 32)
                        act.activation(m.rows[:], m.rows[:], ACT.Silu).then_inc(s.rows_ready.sem, 1)
                    act.wait_ge(s.panel_used.sem, 2 * g + (p0 + i + 1))
                    act.activation(tiled(row(out, 2 * g + i)), banks(s, i), ACT.Copy
                                   ).then_inc(s.set_free.sem, 1)
            body(0, rows=True)
            with act.Fori(1, n // 2) as g:
                body(g)

        @block.tensor
        def _(pe):
            norm.pe(pe)

            def body(g, norm=None):
                for i in range(2):
                    s.set_free.wait(pe, 2 * g + (i + 1))
                    pe_panel(s, pe, 2 * g + (p0 + i), (p0 + i) % 2, i, norm if i == 0 else None)
            body(0, norm)
            with pe.Fori(1, n // 2) as g:
                body(g)

        @block.vector
        def _(dve):
            norm.dve(dve)
            dve.wait_ge(s.rows_ready.sem, 2)
            with dve.Fori(0, n // 2) as g:
                for i in range(2):
                    dve_mod_ring(s, dve, m, 2 * g + (FIRST_MOD + i), i)
            for i in range(2):
                dve_mod_ring(s, dve, m, n + FIRST_MOD + i, i)
    norm.done()
    s.p0 += n
    s.set_free.base += n


def add_gated(s, dve, f, group, gate):
    xf = row(s.x, f)
    g = [s.mod[:, ds(gate + f, 1), m:m + 1].rearrange("p a b -> p (a b)") for m in range(2)]
    b0 = 3 * group
    dve.scalar_tensor_tensor(xf[:, 0:TP], s.psum[:, b0, 0:TP], g[0], xf[:, 0:TP], ALU.mult, ALU.add)
    dve.scalar_tensor_tensor(xf[:, TP:TW], s.psum[:, b0, TP:TW], g[1], xf[:, TP:TW], ALU.mult, ALU.add)
    later = xf[:, TW:T].rearrange("p (t w) -> p t w", w=TW)
    return dve.scalar_tensor_tensor(later, s.psum[:, b0 + 1:b0 + 3, 0:TW], g[1], later, ALU.mult, ALU.add)


def out_proj_stage(s, layer, squares, y_last=None, back=None):
    p0, n = s.p0, OUT_PANELS
    reload = layer == 1
    with ExitStack() as ctx:
        if reload:
            x_in = ctx.enter_context(s.nc.semaphore("x_in"))
        block = ctx.enter_context(s.nc.Block())

        @block.sync
        def _(sp):
            if reload:
                sp.dma_start(s.x[:], s.x_dram).then_inc(x_in, 16)
            s.sp_stream(sp, n)

        @block.gpsimd
        def _(pool):
            s.pool_stream(pool, n)

        @block.scalar
        def _(act):
            if reload:
                act.activation(s.hh[:, KC - 1, :], y_last, ACT.Copy).then_inc(back.high, 1)
            with act.Fori(0, n // 2) as g:
                for i in range(2):
                    s.act_split(act, 2 * g + (p0 + i + 1), (p0 + i + 1) % 2)

        @block.tensor
        def _(pe):
            for f in range(n):
                s.set_free.wait(pe, f + 1)
                if reload and f == 0:
                    pe.wait_ge(back.low, KC)
                    pe_chunk(s, pe, p0 % 2, KC - 1).then_inc(s.panel_used.sem, 1)
                else:
                    pe_panel(s, pe, p0 + f, (p0 + f) % 2, f % 2)

        @block.vector
        def _(dve):
            if reload:
                dve.wait_ge(back.high, KC)
                dve.tensor_tensor(s.hl[:, KC - 1, :], y_last, s.hh[:, KC - 1, :].bitcast(F32), ALU.subtract
                                  ).then_inc(back.low, 1)
                dve.wait_ge(x_in, 16)
            for f in range(n):
                dve.wait_ge(s.panel_used.sem, p0 + f + 1)
                add_gated(s, dve, f, f % 2, (layer * 6 + GA1) * 8).then_inc(s.set_free.sem, 1)
                s.set_free.wait(dve, f + 3)
                squares.dve(dve, f)
    squares.done()
    s.p0 += n
    s.set_free.base += n


def ffn_stage(s, layer, norm, squares):
    p0 = s.p0
    gate_vec = (layer * 6 + GA2) * 8
    sb = s.placer(f"ffn{layer}", s.rest, s.rest + 74592)
    mid_h = [sb(f"mid_high{i}", [P, T], F32R) for i in range(4)]
    mid_l = [sb(f"mid_low{i}", [P, T], F32R) for i in range(4)]
    silu = sb("silu_gate", [P, T])
    prod = sb("product", [P, T])
    added, used = s.added, s.panel_used
    has_mod = layer == 0
    if has_mod:
        mods = Mod(s, "ffn", s.rest + 10 * 4 * T)
    MOD0 = MOD_LAYER

    with s.nc.Block() as block:
        def start(j):
            return 6 * j + (p0 - 2)

        @block.sync
        def _(sp):
            norm.sp(sp)
            if has_mod:
                sp.dma_start(mods.rows[:], s.I["cond"]).then_inc(s.rows_full.sem, 16)
                for i in range(2):
                    sp_mod(s, sp, mods, MOD0 + i, i)
            with sp.Fori(0, FFN_PANELS // 6) as g:
                for i in range(6):
                    s.sp_load(sp, 6 * g + (p0 + 2 + i), (p0 + i) % 2)
                    if has_mod and i == 1:
                        for k in range(2):
                            sp_mod(s, sp, mods, 2 * g + (MOD0 + 2 + k), k)

        @block.gpsimd
        def _(pool):
            s.pool_split(pool, p0 + 1, (p0 + 1) % 2)
            norm.pool(pool)
            s.pool_stream(pool, FFN_PANELS, done=1)

        @block.scalar
        def _(act):
            s.act_split(act, p0 + 1, (p0 + 1) % 2)
            norm.act(act)
            if has_mod:
                act.wait_ge(s.rows_full.sem, 48)
                act.activation(mods.rows[:], mods.rows[:], ACT.Silu).then_inc(s.rows_ready.sem, 1)

            def hidden(c, slot, g_panel, buf):
                if not (isinstance(c, int) and c == 0):
                    s.act_split(act, g_panel + 1, (buf + 1) % 2)
                act.wait_ge(used.sem, g_panel + 1)
                if not (isinstance(c, int) and c == 0):
                    s.prod_ready.wait(act, c)
                act.activation(tiled(silu[:]), banks(s, 0), ACT.Silu).then_inc(s.gate_ready.sem, 1)
                s.act_split(act, g_panel + 2, buf)
                s.prod_ready.wait(act, c + 1)
                act.activation(mid_h[slot][:], prod[:], ACT.Copy).then_inc(s.mid_high.sem, 1)

            def pair(j, q, par):
                buf = p0 % 2
                hidden(2 * j, 2 * par, q, buf)
                hidden(2 * j + 1, 2 * par + 1, q + 2, buf)

            pair(0, p0, 0)
            with act.Fori(0, (FF_G - 1) // 2) as g:
                for i in range(2):
                    q = 12 * g + (start(1) + 6 * i)
                    pair(2 * g + (1 + i), q, 1 - i)
                    s.act_split(act, q + 5, (p0 + 1) % 2)
                    s.act_split(act, q + 6, p0 % 2)
            for p in range(p0 + FFN_PANELS - 1, p0 + FFN_PANELS + 1):
                s.act_split(act, p, p % 2)

        @block.tensor
        def _(pe):
            norm.pe(pe)

            def gate_up(c, g_panel, adds=None):
                s.gate_ready.wait(pe, c)
                if adds is not None:
                    added.wait(pe, adds)
                pe_panel(s, pe, g_panel, p0 % 2, 0)
                s.prod_ready.wait(pe, c)
                if adds is not None:
                    added.wait(pe, adds + 1)
                pe_panel(s, pe, g_panel + 1, (p0 + 1) % 2, 1)

            def down(j, p, par, last=False):
                for f in range(KC):
                    buf = (p0 + f // 4) % 2
                    if f % 4 == 0:
                        pe.wait_ge(s.split_low.sem, p + (1 + f // 4))
                    if f == 0:
                        s.mid_low.wait(pe, 2 * j + 2)
                    if f < 2 and not last:
                        (s.gate_ready if f == 0 else s.prod_ready).wait(pe, 2 * j + 4)
                    else:
                        added.wait(pe, 8 * j + (f + 1))
                    for t in range(TT):
                        for i in range(2):
                            w = slice((4 * i + f % 4) * P, (4 * i + f % 4 + 1) * P)
                            cols = slice(t * TW, (t + 1) * TW)
                            mm = three_products(pe, s.psum[:, 3 * (f % 2) + t, 0:TW], s.wh[buf][:, w],
                                                s.wl[buf][:, w], mid_h[2 * par + i][:, cols],
                                                mid_l[2 * par + i][:, cols], i == 0, i == 1)
                    if f % 4 == 3:
                        mm.then_inc(used.sem, 1)
                    else:
                        mm.then_inc(s.down_full.sem, 1)

            pe_first_panels(s, pe, p0, norm)
            gate_up(1, p0 + 2)
            with pe.Fori(0, (FF_G - 1) // 2) as g:
                for i in range(2):
                    j, q = 2 * g + (1 + i), 12 * g + (start(1) + 6 * i)
                    for k in range(2):
                        gate_up(2 * j + k, q + 2 * k, 8 * j - 7 if k == 0 else None)
                    down(2 * g + i, q + 4, i)
            last = FF_G - 1
            down(last, p0 + FFN_PANELS - 2, last % 2, True)

        @block.vector
        def _(dve):
            def product(c, u_used):
                s.gate_ready.wait(dve, c + 1)
                dve.wait_ge(used.sem, u_used)
                if not (isinstance(c, int) and c == 0):
                    s.mid_high.wait(dve, c)
                    s.mid_low.wait(dve, c)
                dve.tensor_tensor(tiled(prod[:]), tiled(silu[:]), banks(s, 1), ALU.mult
                                  ).then_inc(s.prod_ready.sem, 1)

            def low(c, slot):
                s.mid_high.wait(dve, c + 1)
                dve.tensor_tensor(mid_l[slot][:], prod[:], mid_h[slot][:].bitcast(F32), ALU.subtract
                                  ).then_inc(s.mid_low.sem, 1)

            def add(j, f, d_used):
                if f % 4 == 3:
                    dve.wait_ge(used.sem, d_used + f // 4)
                else:
                    s.down_full.wait(dve, 6 * j + (f + 1 - f // 4))
                added.wait(dve, 8 * j + (f + 1))
                add_gated(s, dve, f, f % 2, gate_vec).then_inc(added.sem, 1)

            norm.dve(dve)
            if has_mod:
                dve.wait_ge(s.rows_ready.sem, 3)
            for c in range(2):
                product(c, p0 + 2 + 2 * c)
                low(c, c)
                if has_mod:
                    for k in range(2):
                        dve_mod_ring(s, dve, mods, MOD0 + 2 * c + k, k)
            with dve.Fori(0, (FF_G - 1) // 2) as g:
                for i in range(2):
                    j, q = 2 * g + (1 + i), 12 * g + (start(1) + 6 * i)
                    for k in range(2):
                        product(2 * j + k, q + (2 + 2 * k))
                        if k == 0:
                            low(2 * j, 2 * (1 - i))
                            if has_mod:
                                for k_ in range(2):
                                    dve_mod_ring(s, dve, mods, 4 * g + (MOD0 + 4 + 2 * i + k_), k_)
                    for f in range(KC):
                        add(2 * g + i, f, q + 5)
                        if f == 1:
                            low(2 * j + 1, 2 * (1 - i) + 1)
            last = FF_G - 1
            for f in range(KC):
                add(last, f, p0 + FFN_PANELS - 1)
                added.wait(dve, 8 * last + f + 3)
                squares.dve(dve, f)
    norm.done()
    squares.done()
    s.p0 += FFN_PANELS
    for c, n in ((s.gate_ready, FF_CH), (s.prod_ready, FF_CH), (s.mid_high, FF_CH), (s.mid_low, FF_CH),
                 (s.down_full, 6 * FF_G), (s.added, 8 * FF_G)):
        c.base += n


def final_stage(s, squares):
    nc, x, psum = s.nc, s.x, s.psum
    sb = s.placer("final", s.rest, s.rest + 64512)
    std = [sb(f"std{i}", [P, TW]) for i in range(2)]
    rstd = [sb(f"rstd{i}", [P, TW]) for i in range(2)]
    with nc.semaphore("y_stored") as y_stored, nc.Block() as block:

        @block.scalar
        def _(act):
            for t in range(TT):
                s.mean_ready.wait(act, t + 1)
                if t >= 2:
                    s.rstd_ready.wait(act, t - 1)
                act.activation(std[t % 2][:], psum[:, Squares.BANKS[t], 0:TW], ACT.Sqrt, bias=s.eps[:, 0:1]
                               ).then_inc(s.std_ready.sem, 1)

        @block.tensor
        def _(pe):
            squares.pe(pe)

        @block.vector
        def _(dve):
            for t in range(TT):
                s.std_ready.wait(dve, t + 1)
                dve.reciprocal(rstd[t % 2][:], std[t % 2][:]).then_inc(s.rstd_ready.sem, 1)
                s.rstd_ready.wait(dve, t + 1)
                for c in range(KC):
                    xt = x[:, c, t * TW:(t + 1) * TW]
                    v = dve.scalar_tensor_tensor(xt, xt, s.gain[:, 4, c:c + 1], rstd[t % 2][:],
                                                 ALU.mult, ALU.mult)
                v.then_inc(s.normed.sem, 1)

        @block.sync
        def _(sp):
            for t in range(TT):
                s.normed.wait(sp, t + 1)
                sp.dma_start(s.O["y"][:, :, t * TW:(t + 1) * TW], x[:, :, t * TW:(t + 1) * TW]
                             ).then_inc(y_stored, 16)
            sp.wait_ge(y_stored, 16 * TT)
            for i in range(2):
                n = (STREAM + PAD + 1 - i) // 2
                sp.wait_ge(s.raw_full[i].sem, 16 * n)


def even_buffer(s):
    return s.at("even", [P, EVEN_PANELS, T], F32, s.rest)


def rg_stage(s, even):
    nc, psum, I = s.nc, s.psum, s.I
    sq = [s.at(f"rg_square{d}", [P, T], F32, at + 12 * T) for d, at in enumerate((s.hi_chunk, s.lo_chunk))]
    hi = s.placer("rg_hi", s.hi_chunk + 16 * T, s.lo_chunk)
    lo = s.placer("rg_lo", s.lo_chunk + 16 * T, s.x_at)
    up = s.placer("rg_x", s.x_at, s.rest)
    gate = [[sb(f"gate{i}{j}", [P, T]) for j in range(4)] for i, sb in enumerate((hi, up))]
    mult = [[sb(f"mult{i}{d}", [P, T]) for d in range(2)] for i, sb in enumerate((lo, up))]
    xc = [sb(f"xc{i}", [P, T]) for i, sb in enumerate((lo, up))]
    turned, rope = up("turned", [P, TL]), up("rope", [P, P])
    end = s.placer("rg_end", s.rest + EVEN_PANELS * 4 * T, s.rest + 74592)
    cos, sin = end("cos", [P, TL]), end("sin", [P, TL])
    gw = lo("gate_weights", [P, 4 * P])
    conv = lo("conv", [P, RG_CH, 5])
    bias = lo("gate_bias", [P, RG_CH, 4])
    lam = lo("lam", [P, RG_CH, 2])
    h0 = lo("h0", [P, RG_CH, 2])
    sp_ = [lo(f"softplus{i}", [P, RG_CH, 2]) for i in range(4)]
    last = lo("last", [P, RG_CH, 2])
    with ExitStack() as ctx:
        def sem(name):
            return ctx.enter_context(nc.semaphore("rg_" + name))
        small, gelu_ready, sp_step, sp_done = sem("small"), sem("gelu"), sem("sp_step"), sem("sp_done")
        gw_full, gates_done, gate_full, gate_read = sem("gw_full"), sem("gates_done"), sem("gate_full"), sem("gate_read")
        conv_step, tanh_ready, a_ready, sq_ready = sem("conv_step"), sem("tanh_ready"), sem("a_ready"), sem("square_ready")
        m_ready, root_ready, b_step, scanned = sem("m_ready"), sem("root_ready"), sem("b_step"), sem("scanned")
        y_step, y_high, chunk_done, stored = sem("y_step"), sem("y_high"), sem("chunk_done"), sem("stored")
        ib_ready, rope_in, turn_full, turn_read, cos_done, roped = (
            sem(n) for n in ("ib_ready", "rope_in", "turn_full", "turn_read", "cos_done", "roped"))
        block = ctx.enter_context(nc.Block())

        def scalar(t, c, j):
            return t[:, ds(c, 1), j:j + 1].rearrange("p a b -> p (a b)")

        @block.sync
        def _(sp):
            for t, name in ((conv, "conv_rg"), (bias, "rgb"), (lam, "lam"), (h0, "h0")):
                sp.dma_start(t[:], I[name]).then_inc(small, 16)
            sp.dma_start(gw[:], I["rgw"][0]).then_inc(gw_full, 16)
            for t, name in ((rope, "rope"), (sin, "sin"), (cos, "cos")):
                sp.dma_start(t[:], I[name]).then_inc(rope_in, 16)
            sp.dma_start(s.O["k"], even[:, 12, 0:TP]).then_inc(stored, 16)
            sp.dma_start(s.O["v"], even[:, 13, 0:TP]).then_inc(stored, 16)
            for c in range(1, RG_CH):
                sp.wait_ge(gates_done, c)
                sp.dma_start(gw[:], I["rgw"][c]).then_inc(gw_full, 16)
            sp.wait_ge(chunk_done, RG_CH)
            sp.dma_start(s.O["rg"], last[:]).then_inc(stored, 16)
            sp.wait_ge(stored, 48)

        @block.tensor
        def _(pe):
            def turn(c):
                if c == 0:
                    pe.wait_ge(rope_in, 48)
                else:
                    pe.wait_ge(turn_read, c)
                for t in range(2):
                    mm = pe.matmul(psum[:, 6 + t, :], rope[:], even[:, c + 8, TP + 512 * t:TP + 512 * (t + 1)],
                                   start=True, stop=True)
                mm.then_inc(turn_full, 1)

            for g in range(RG_CH // 2):
                for i in range(2):
                    c = 2 * g + i
                    pe.wait_ge(gw_full, 16 * c + 16)
                    pe.wait_ge(conv_step, 7 * c + 7)
                    for j in range(4):
                        pe.wait_ge(gate_read, 4 * c + (j + 1))
                        for t in range(TT):
                            mm = pe.matmul(psum[:, 3 * (j % 2) + t, 0:TW], gw[:, j * P:(j + 1) * P],
                                           xc[i][:, t * TW:(t + 1) * TW], start=True, stop=True)
                        if j == 3:
                            mm.then_inc(gates_done, 1)
                        else:
                            mm.then_inc(gate_full, 1)
                    turn(c)
            turn(4)

        @block.scalar
        def _(act):
            act.sem_inc(gate_read, 2)
            act.activation(even[:, 4:8, :], even[:, 4:8, :], ACT.Gelu_apprx_tanh).then_inc(gelu_ready, 1)
            act.wait_ge(small, 64)
            act.activation(sp_[0][:], lam[:], ACT.Abs).then_inc(sp_step, 1)
            act.wait_ge(sp_step, 1)
            act.activation(sp_[1][:], sp_[0][:], ACT.Exp, scale=-1.0).then_inc(sp_step, 1)
            act.wait_ge(sp_done, 1)
            act.activation(sp_[0][:], sp_[2][:], ACT.Ln).then_inc(sp_step, 1)
            act.wait_ge(sp_done, 6)

            def front(c, i):
                if not (isinstance(c, int) and c < 2):
                    act.wait_ge(chunk_done, c - 1)
                for j in range(4):
                    if j < 3:
                        act.wait_ge(gate_full, 3 * c + (j + 1))
                    else:
                        act.wait_ge(gates_done, c + 1)
                    act.activation(tiled(gate[i][j][:]), banks(s, j % 2), ACT.Sigmoid,
                                   bias=scalar(bias, c, j)).then_inc(gate_read, 1)
                act.wait_ge(gate_read, 4 * c + 6)
                for d in range(2):
                    act.activation(mult[i][d][:], gate[i][2 * d][:], ACT.Tanh, scale=scalar(sp_[0], c, d)
                                   ).then_inc(tanh_ready, 1)
                for d in range(2):
                    act.wait_ge(tanh_ready, 2 * c + (d + 1))
                    act.activation(gate[i][2 * d][:], gate[i][2 * d][:], ACT.Exp, scale=scalar(sp_[1], c, d)
                                   ).then_inc(a_ready, 1)
                for d in range(2):
                    act.wait_ge(a_ready, 2 * c + (d + 1))
                    if not (isinstance(c, int) and c == 0):
                        act.wait_ge(m_ready, 2 * c + (d - 1))
                    act.activation(sq[d][:], gate[i][2 * d][:], ACT.Square).then_inc(sq_ready, 1)

            def root(c, i):
                for d in range(2):
                    act.wait_ge(m_ready, 2 * c + (d + 1))
                    act.activation(mult[i][d][:], mult[i][d][:], ACT.Sqrt).then_inc(root_ready, 1)

            def high(c, i):
                act.wait_ge(y_step, 2 * c + 2)
                act.activation(row(s.hh, c), xc[i][:], ACT.Copy).then_inc(y_high, 1)

            front(0, 0)
            root(0, 0)
            with act.Fori(0, RG_CH // 2 - 1) as g:
                for i in range(2):
                    c = 2 * g + i
                    front(2 * g + (i + 1), 1 - i)
                    high(c, i)
                    root(2 * g + (i + 1), 1 - i)
            front(RG_CH - 1, 1)
            high(RG_CH - 2, 0)
            root(RG_CH - 1, 1)
            high(RG_CH - 1, 1)

        @block.gpsimd
        def _(pool):
            def cosine(c):
                x = even[:, c + 8, TP:T]
                pool.wait_ge(turn_full, c + 1)
                pool.tensor_tensor(x, x, cos[:], ALU.mult).then_inc(cos_done, 1)

            pool.wait_ge(rope_in, 48)
            for c in range(RG_CH):
                b, x = [gate[c % 2][2 * d + 1] for d in range(2)], xc[c % 2]
                for d in range(2):
                    pool.wait_ge(gate_read, 4 * c + (2 * d + 4))
                    pool.tensor_tensor(b[d][:], b[d][:], x[:], ALU.mult).then_inc(ib_ready, 1)
                cosine(c)
            cosine(4)

        @block.vector
        def _(dve):
            dve.wait_ge(small, 64)
            dve.wait_ge(sp_step, 2)
            dve.tensor_scalar(sp_[2][:], sp_[1][:], 1.0, None, ALU.add).then_inc(sp_done, 1)
            dve.wait_ge(sp_done, 1)
            dve.scalar_tensor_tensor(sp_[3][:], sp_[2][:], -1.0, sp_[1][:], ALU.add, ALU.subtract
                                     ).then_inc(sp_done, 1)
            dve.wait_ge(sp_step, 3)
            dve.reciprocal(sp_[2][:], sp_[2][:]).then_inc(sp_done, 1)
            dve.wait_ge(sp_done, 3)
            dve.tensor_tensor(sp_[3][:], sp_[3][:], sp_[2][:], ALU.mult)
            dve.tensor_scalar(sp_[1][:], lam[:], -RG_C, 0.0, ALU.mult, ALU.max).then_inc(sp_done, 1)
            dve.wait_ge(sp_done, 4)
            dve.tensor_tensor(sp_[0][:], sp_[0][:], sp_[3][:], ALU.subtract).then_inc(sp_done, 1)
            dve.wait_ge(sp_done, 5)
            dve.scalar_tensor_tensor(sp_[0][:], sp_[0][:], RG_C, sp_[1][:], ALU.mult, ALU.add
                                     ).then_inc(sp_step, 1)
            dve.wait_ge(sp_step, 4)
            dve.tensor_scalar(sp_[1][:], sp_[0][:], -1.0, None, ALU.mult).then_inc(sp_done, 1)

            def convolution(c, i):
                xr = row(even, c)
                if not (isinstance(c, int) and c < 2):
                    dve.wait_ge(chunk_done, c - 1)
                    dve.wait_ge(y_high, c - 1)
                dve.tensor_scalar(xc[i][:], xr, scalar(conv, c, 2), scalar(conv, c, 4), ALU.mult, ALU.add
                                  ).then_inc(conv_step, 1)
                for n, (tap, off) in enumerate(((0, -2), (1, -1), (3, 1))):
                    for m, (lo, hi) in enumerate(((0, TP), (TP, T))):
                        a, b = (lo - off, hi) if off < 0 else (lo, hi - off)
                        dve.wait_ge(conv_step, 7 * c + (2 * n + m + 1) if n else 7 * c + 1)
                        dve.scalar_tensor_tensor(xc[i][:, a:b], xr[:, a + off:b + off], scalar(conv, c, tap),
                                                 xc[i][:, a:b], ALU.mult, ALU.add).then_inc(conv_step, 1)

            def multiplier(c, i):
                for d in range(2):
                    dve.wait_ge(tanh_ready, 2 * c + (d + 1))
                    dve.wait_ge(sq_ready, 2 * c + (d + 1))
                    dve.scalar_tensor_tensor(mult[i][d][:], sq[d][:], 1.0, mult[i][d][:], ALU.add, ALU.mult
                                             ).then_inc(m_ready, 1)

            def scans(c, i):
                for d in range(2):
                    a, b, h = gate[i][2 * d], gate[i][2 * d + 1], mult[i][d]
                    dve.wait_ge(root_ready, 2 * c + (d + 1))
                    dve.wait_ge(ib_ready, 2 * c + (d + 1))
                    dve.tensor_tensor(b[:], b[:], h[:], ALU.mult).then_inc(b_step, 1)
                    dve.wait_ge(b_step, 2 * c + (d + 1))
                    for m, (lo, hi) in enumerate(((0, TP), (TP, T))):
                        cols = slice(lo, hi) if d == 0 else slice(hi - 1, lo - 1 if lo else None, -1)
                        v = dve.tensor_tensor_scan(h[:, cols], a[:, cols], b[:, cols],
                                                   0.0 if m == 0 else scalar(h0, c, d), ALU.mult, ALU.add)
                    v.then_inc(scanned, 1)
                dve.wait_ge(scanned, 2 * c + 2)
                for d in range(2):
                    at = TP - 1 if d == 0 else 0
                    dve.tensor_copy(scalar(last, c, d), mult[i][d][:, at:at + 1])
                dve.tensor_tensor(xc[i][:], mult[i][0][:], mult[i][1][:], ALU.add).then_inc(y_step, 1)
                dve.wait_ge(y_step, 2 * c + 1)
                dve.wait_ge(gelu_ready, 1)
                dve.tensor_tensor(xc[i][:], xc[i][:], row(even, c + 4), ALU.mult).then_inc(y_step, 1)

            def turn(c):
                x = even[:, ds(c + 8, 1), TP:T].rearrange("p a t -> p (a t)")
                dve.wait_ge(turn_full, c + 1)
                if not (isinstance(c, int) and c == 0):
                    dve.wait_ge(roped, c)
                dve.tensor_tensor(turned[:].rearrange("p (a t) -> p a t", a=2), psum[:, 6:8, :],
                                  sin[:].rearrange("p (a t) -> p a t", a=2), ALU.mult).then_inc(turn_read, 1)
                dve.wait_ge(turn_read, c + 1)
                dve.wait_ge(cos_done, c + 1)
                dve.tensor_tensor(x, x, turned[:], ALU.add).then_inc(roped, 1)

            def low(c, i):
                dve.wait_ge(y_high, c + 1)
                dve.tensor_tensor(row(s.hl, c), xc[i][:], row(s.hh, c).bitcast(F32), ALU.subtract
                                  ).then_inc(chunk_done, 1)

            convolution(0, 0)
            convolution(1, 1)
            multiplier(0, 0)
            scans(0, 0)
            turn(0)
            with dve.Fori(0, RG_CH // 2 - 1) as g:
                for i in range(2):
                    multiplier(2 * g + (i + 1), 1 - i)
                    low(2 * g + i, i)
                    convolution(2 * g + (i + 2), i)
                    scans(2 * g + (i + 1), 1 - i)
                    turn(2 * g + (i + 1))
            multiplier(RG_CH - 1, 1)
            low(RG_CH - 2, 0)
            turn(RG_CH - 1)
            scans(RG_CH - 1, 1)
            turn(4)
            low(RG_CH - 1, 1)


def attention_stage(s, even):
    nc, psum, I = s.nc, s.psum, s.I
    sb = s.placer("att", s.rest, s.rest + 8 * 4 * T)
    ctx_k = sb("ctx_k", [P, P])
    vt = sb("v_tokens", [P, NT + 1, P])
    window = sb("window", [P, 8, 2, P], BF16)
    ident_bf = sb("ident_bf", [P, P], BF16)
    prob = sb("prob", [P, 2, 512])
    prob_t = [sb(f"prob_t{i}", [P, 2, 512]) for i in range(2)]
    q_blk = [sb(f"q_block{i}", [P, 2, 4, P]) for i in range(2)]
    sb = s.placer("att_hi", s.rest + EVEN_PANELS * 4 * T, s.rest + 74592)
    o_sb = sb("o", [P, 512])
    sink, nsink = sb("sink", [P, HEADS]), sb("neg_sink", [P, HEADS])
    top, negm, rows, es, den, rden = (sb(n, [P, HEADS]) for n in ("top", "negm", "rows", "es", "den", "rden"))
    scale = HD ** -0.5
    with ExitStack() as ctx:
        def sem(name):
            return ctx.enter_context(nc.semaphore("att_" + name))
        loaded, v_full, vt_ready = sem("loaded"), sem("v_full"), sem("vt_ready")
        q_ready, s_full, top_step, neg_step, negm_ready, p_ready, pt_full, pt_act, pt_dve = (
            sem(n) for n in ("q_ready", "s_full", "top_step", "neg_step", "negm_ready", "p_ready", "pt_full",
                             "pt_act", "pt_dve"))
        pv_done, es_ready, den_ready, rden_ready, o_ready, y_full, y_high, y_low, nsink_ready = (
            sem(n) for n in ("pv_done", "es_ready", "den_ready", "rden_ready", "o_ready", "y_full", "y_high",
                             "y_low", "nsink_ready"))
        q_zero, x_back = sem("q_zero"), sem("x_back")
        block = ctx.enter_context(nc.Block())
        BLOCKS = NT

        def wait(eng, semaphore, n):
            if not (isinstance(n, int) and n <= 0):
                eng.wait_ge(semaphore, n)

        def blocks(eng, run, finish):
            run(0, 0, None, True)
            finish(0, 0, True)
            run(1, 1, None, False)
            run(2, 0, 1, False)
            with eng.Fori(1, (BLOCKS - 1) // 2) as g:
                for j in range(2):
                    run(2 * g + (1 + j), 1 - j, 2 * g + j, False)
            finish(BLOCKS - 1, (BLOCKS - 1) % 2, False)

        @block.sync
        def _(sp):
            for t, name in ((sink, "sink"), (ctx_k, "ctx_k"), (window, "window"), (ident_bf, "ident_bf")):
                sp.dma_start(t[:], I[name]).then_inc(loaded, 16)
            sp.dma_start(vt[:, NT, :], I["ctx_v"]).then_inc(loaded, 16)
            sp.dma_start(s.x[:], I["x"]).then_inc(x_back, 16)
            sp.wait_ge(x_back, 16)

        @block.tensor
        def _(pe):
            for n in range(NT):
                mm = pe.transpose(psum[:, 4 + n // 4, (n % 4) * P:(n % 4 + 1) * P],
                                  even[:, 13, n * P:(n + 1) * P], s.ident[:])
            mm.then_inc(v_full, 1)
            pe.wait_ge(loaded, 16 * 5)
            pe.wait_ge(vt_ready, 1)

            def scores(i, par, c, prompt):
                if c == 0:
                    pe.wait_ge(q_ready, i + 1)
                wait(pe, p_ready, 8 * i + (2 * c - 2))
                for h in range(2):
                    q = q_blk[par][:, h, c, :]
                    out = psum[:, 2 * (c % 2) + h, :]
                    if prompt:
                        mm = pe.matmul(out[:, 0:P], q, even[:, 12, 0:P], start=True, stop=True)
                        continue
                    keys = even[:, 12:14, :].rearrange("p a t -> p (a t)")
                    pe.matmul(out[:, 0:TW], q, keys[:, ds(i * P - P, TW)], start=True, stop=False,
                              skip_group_check=True)
                    pe.matmul(out[:, TW:512], q, ctx_k[:], start=False, stop=False, skip_group_check=True)
                    for j in range(2):
                        mm = pe.matmul(out[:, 2 * j * P:(2 * j + 1) * P], ident_bf[:],
                                       window[:, ds(i - 1, 1), j, :].rearrange("p a n -> p (a n)"),
                                       start=False, stop=j == 1, skip_group_check=True)
                mm.then_inc(s_full, 1)

            def turn(i, c, prompt):
                pe.wait_ge(p_ready, 8 * i + (2 * c + 2))
                wait(pe, pt_act, 4 * i + c)
                wait(pe, pt_dve, 4 * i + c)
                for h in range(2):
                    for k in range(1 if prompt else 4):
                        mm = pe.transpose(psum[:, 4 + h, k * P:(k + 1) * P], prob[:, h, k * P:(k + 1) * P],
                                          s.ident[:])
                mm.then_inc(pt_full, 1)

            def weigh(i, c, prompt):
                nk = 1 if prompt else 4
                pe.wait_ge(pt_act, 4 * i + (c + 1))
                pe.wait_ge(pt_dve, 4 * i + (c + 1))
                if c == 0:
                    wait(pe, o_ready, i)
                for h in range(2):
                    out = psum[:, 6, c * P + HD * h:c * P + HD * h + HD]
                    for k in range(nk):
                        if prompt:
                            v = vt[:, 0, HD * h:HD * h + HD]
                        elif k == 3:
                            v = vt[:, NT, HD * h:HD * h + HD]
                        else:
                            v = vt[:, ds(i + (k - 1), 1), HD * h:HD * h + HD].rearrange("p a n -> p (a n)")
                        mm = pe.matmul(out, prob_t[c % 2][:, h, k * P:(k + 1) * P], v, start=k == 0,
                                       stop=k == nk - 1)
                mm.then_inc(pv_done, 1)

            def outputs(i):
                pe.wait_ge(o_ready, i + 1)
                wait(pe, y_low, i)
                for c in range(4):
                    mm = pe.transpose(psum[:, 7, c * P:(c + 1) * P], o_sb[:, c * P:(c + 1) * P], s.ident[:])
                mm.then_inc(y_full, 1)

            def run(i, par, prev, prompt):
                for c in range(4):
                    scores(i, par, c, prompt)
                    if c >= 1:
                        turn(i, c - 1, prompt)
                    elif prev is not None:
                        turn(prev, 3, prompt)
                    if c >= 2:
                        weigh(i, c - 2, prompt)
                    elif prev is not None:
                        weigh(prev, c + 2, prompt)
                    if c == 2 and prev is not None:
                        outputs(prev)

            def finish(i, par, prompt):
                turn(i, 3, prompt)
                weigh(i, 2, prompt)
                weigh(i, 3, prompt)
                outputs(i)

            blocks(pe, run, finish)

        @block.gpsimd
        def _(pool):
            for q in q_blk:
                pool.memset(q[:], 0.0).then_inc(q_zero, 1)
            pool.wait_ge(q_zero, 2)

            def load_q(i, par):
                wait(pool, s_full, 4 * i - 4)
                cols = ds(i * P, P)
                pool.tensor_copy(q_blk[par][0:HD, 0], even[0:HD, 8:12, cols])
                pool.tensor_copy(q_blk[par][HD:P, 1], even[HD:P, 8:12, cols]).then_inc(q_ready, 1)
            load_q(0, 0)
            load_q(1, 1)
            load_q(2, 0)
            with pool.Fori(1, (BLOCKS - 1) // 2) as g:
                for j in range(2):
                    load_q(2 * g + (1 + j), 1 - j)

        @block.scalar
        def _(act):
            def exps(i, c, prompt):
                wide = P if prompt else 512
                act.wait_ge(negm_ready, 4 * i + (c + 1))
                wait(act, pt_full, 4 * i + c)
                for h in range(2):
                    j = 2 * c + h
                    act.activation(prob[:, h, 0:wide], psum[:, 2 * (c % 2) + h, 0:wide], ACT.Exp,
                                   bias=negm[:, j:j + 1], scale=scale, accum_out=rows[:, j:j + 1]
                                   ).then_inc(p_ready, 1)
                if c == 3:
                    act.activation(es[:], es[:], ACT.Exp).then_inc(es_ready, 1)

            def copy_t(i, c, prompt):
                wide = P if prompt else 512
                act.wait_ge(pt_full, 4 * i + (c + 1))
                wait(act, pv_done, 4 * i + (c - 1))
                act.activation(prob_t[c % 2][:, 0, 0:wide], psum[:, 4, 0:wide], ACT.Copy).then_inc(pt_act, 1)

            def high(i):
                act.wait_ge(y_full, i + 1)
                act.activation(s.hh[:, 4:8, ds(i * P, P)], psum[:, 7, :].rearrange("p (c w) -> p c w", w=P),
                               ACT.Copy).then_inc(y_high, 1)

            def run(i, par, prev, prompt):
                for c in range(4):
                    if c >= 1:
                        exps(i, c, prompt)
                        if c == 3 and prev is not None:
                            high(prev)
                        copy_t(i, c - 1, prompt)
                    else:
                        exps(i, 0, prompt)
                        if prev is not None:
                            copy_t(prev, 3, prompt)

            def finish(i, par, prompt):
                copy_t(i, 3, prompt)
                high(i)

            blocks(act, run, finish)

        @block.vector
        def _(dve):
            dve.wait_ge(v_full, 1)
            dve.tensor_copy(vt[:, 0:8, :].rearrange("p (a n) w -> p a (n w)", a=2), psum[:, 4:6, :])
            dve.tensor_copy(vt[:, 8, :], psum[:, 6, 0:P]).then_inc(vt_ready, 1)
            dve.wait_ge(loaded, 16 * 5)
            dve.tensor_scalar(nsink[:], sink[:], -1.0, None, ALU.mult).then_inc(nsink_ready, 1)
            dve.wait_ge(nsink_ready, 1)

            def largest(i, c, prompt, prev=None):
                wide = P if prompt else 512
                two = slice(2 * c, 2 * c + 2)
                dve.wait_ge(s_full, 4 * i + (c + 1))
                wait(dve, neg_step, 4 * i + c - 3)
                dve.tensor_reduce(top[:, two], psum[:, 2 * (c % 2):2 * (c % 2) + 2, 0:wide], AX.X, ALU.max
                                  ).then_inc(top_step, 1)
                if c == 0:
                    wait(dve, p_ready, 8 * i)
                    wait(dve, es_ready, i)
                    if prev is not None:
                        denominators(prev)
                    wait(dve, den_ready, i)
                dve.wait_ge(top_step, 4 * i + (c + 1))
                dve.scalar_tensor_tensor(negm[:, two], top[:, two], -scale, nsink[:, two], ALU.mult, ALU.min
                                         ).then_inc(neg_step, 1)
                dve.wait_ge(neg_step, 4 * i + (c + 1))
                dve.tensor_tensor(es[:, two], negm[:, two], sink[:, two], ALU.add).then_inc(negm_ready, 1)

            def denominators(i):
                wait(dve, rden_ready, i)
                dve.tensor_tensor(den[:], rows[:], es[:], ALU.add).then_inc(den_ready, 1)
                dve.wait_ge(den_ready, i + 1)
                wait(dve, o_ready, i)
                dve.reciprocal(rden[:], den[:]).then_inc(rden_ready, 1)

            def copy_t(i, c, prompt):
                wide = P if prompt else 512
                dve.wait_ge(pt_full, 4 * i + (c + 1))
                wait(dve, pv_done, 4 * i + (c - 1))
                dve.tensor_copy(prob_t[c % 2][:, 1, 0:wide], psum[:, 5, 0:wide]).then_inc(pt_dve, 1)

            def normalise(i):
                dve.wait_ge(rden_ready, i + 1)
                dve.wait_ge(pv_done, 4 * i + 4)
                wait(dve, y_full, i)
                dve.tensor_tensor(o_sb[:].rearrange("p (h w) -> p h w", w=HD),
                                  psum[:, 6, :].rearrange("p (h w) -> p h w", w=HD),
                                  rden[:].rearrange("p (h o) -> p h o", o=1).to_broadcast([P, HEADS, HD]),
                                  ALU.mult).then_inc(o_ready, 1)

            def low(i):
                cols = ds(i * P, P)
                dve.wait_ge(y_high, i + 1)
                dve.tensor_tensor(s.hl[:, 4:8, cols], psum[:, 7, :].rearrange("p (c w) -> p c w", w=P),
                                  s.hh[:, 4:8, cols].bitcast(F32), ALU.subtract).then_inc(y_low, 1)

            def run(i, par, prev, prompt):
                for c in range(4):
                    largest(i, c, prompt, prev)
                    if c >= 1:
                        copy_t(i, c - 1, prompt)
                    elif prev is not None:
                        copy_t(prev, 3, prompt)
                    if prev is not None and c == 1:
                        normalise(prev)
                    if prev is not None and c == 3:
                        low(prev)

            def finish(i, par, prompt):
                copy_t(i, 3, prompt)
                dve.wait_ge(p_ready, 8 * i + 8)
                dve.wait_ge(es_ready, i + 1)
                denominators(i)
                normalise(i)
                low(i)

            blocks(dve, run, finish)


LEVELS = [2, 4, 8, 16, 32, 64]
NL = len(LEVELS)
NB = 3
SLOTS = NL * NB
(G_, GC_, EG_, EK_, EL_, BETA_, NBETA_) = range(7)


class Delta:

    def __init__(self, s):
        sb = s.placer("dn", s.x_at, s.rest + 74592)
        self.raw = {n: sb(f"raw_{n}", [P, T]) for n in "kqv"}
        self.silu_z = sb("silu_z", [P, T])
        self.kn, self.qn, self.vf = sb("kn", [P, T]), sb("qn", [P, T]), sb("vf", [P, T])
        self.k_tok, self.v_tok = sb("k_tok", [P, T]), sb("v_tok", [P, T])
        self.pt = [sb(f"pt{d}", [P, T]) for d in range(2)]
        self.wt = [sb(f"wt{d}", [P, T]) for d in range(2)]
        self.ub = [sb(f"ub{d}", [P, T]) for d in range(2)]
        self.qg = [sb(f"qg{d}", [P, T]) for d in range(2)]
        kd0 = sb("kd0", [P, T])
        self.kd = [kd0, self.k_tok]
        t0, tt0 = sb("t0", [P, T]), sb("tt0", [P, T])
        self.t, self.tt = [t0, self.vf], [tt0, self.raw["v"]]
        self.osum = sb("osum", [P, T])
        self.xl = [self.osum[:, i * TW:(i + 1) * TW] for i in range(2)]
        self.bm1 = sb("bm1", [P, TW])
        self.bm = [self.osum[:, 2 * TW:3 * TW], self.bm1[:]]
        self.fin = [self.vf[:, d * P:(d + 1) * P] for d in range(2)]
        self.vn = [self.vf[:, (3 + d) * P:(4 + d) * P] for d in range(2)]
        self.kk, self.qk = self.raw["k"], self.raw["q"]
        self.tok = sb("token_consts", [P, 7 * 2 * NT * DN_H])
        self.hs = sb("head_consts", [P, 7, 2, NT])
        self.level = sb("level_masks", [P, 2, NL + 1, P], BF16)
        self.low = sb("neg_masks", [P, 2, P], BF16)
        self.tri = sb("tri", [P, 2, P])
        self.state = [[sb(f"state{d}{i}", [P, P]) for i in range(2)] for d in range(2)]
        self.conv = sb("conv", [P, 24, 4])
        self.onorm = sb("onorm", [P, 1])


def decay_stage(s, dn, norm):
    nc, psum, I, p0 = s.nc, s.psum, s.I, s.p0
    sb = s.placer("decay", s.rest, s.rest + 10 * 4 * T)
    ab = sb("ab", [48, T])
    ab_tok = sb("ab_tok", [P, NT * 48])
    u, e, w, r, l, g = (sb(n, [P, NT, 16]) for n in ("u", "e", "w", "r", "l", "g"))
    gl = sb("g_last", [P, 2, NT * DN_H])
    dts = sb("dt_bias", [P, 2, 16])
    tok = dn.tok[:].rearrange("p (v d n) -> p v d n", v=7, d=2)
    N = NT * DN_H
    with ExitStack() as ctx:
        def sem(name):
            return ctx.enter_context(nc.semaphore("decay_" + name))
        stored, loaded, ab_ready, act_step, dve_step, turned, sums, beta_ready = (
            sem(n) for n in ("stored", "loaded", "ab_ready", "act_step", "dve_step", "turned", "sums", "beta_ready"))
        block = ctx.enter_context(nc.Block())

        def to_all(row):
            return row.rearrange("p (o c) -> p o c", o=1).to_broadcast([P, NT, 16])

        @block.sync
        def _(sp):
            norm.sp(sp)
            sp.dma_start(s.x_dram, s.x[:]).then_inc(stored, 16)
            norm.wait_tile(sp, TT - 1)
            sp.dma_start(dts[:], I["dts"]).then_inc(loaded, 16)
            sp.wait_ge(stored, 16)
            for t, name in ((dn.level, "level"), (dn.low, "low"), (dn.tri, "tri"), (dn.conv, "conv_dn"),
                            (dn.onorm, "onorm")):
                sp.dma_start(t[:], I[name]).then_inc(loaded, 16)
            s.sp_load(sp, p0 + 2, p0 % 2)

        @block.gpsimd
        def _(pool):
            norm.pool(pool)
            s.pool_split(pool, p0 + 1, (p0 + 1) % 2)

        @block.tensor
        def _(pe):
            norm.pe(pe)
            s.set_free.wait(pe, 1)
            pe_panel(s, pe, p0, p0 % 2, 0, norm)
            pe.wait_ge(ab_ready, 1)
            for n in range(NT):
                mm = pe.transpose(psum[:, 3, n * 48:(n + 1) * 48], ab[:, n * P:(n + 1) * P], s.ident[0:48, 0:48])
            mm.then_inc(turned, 1)
            pe.wait_ge(dve_step, 9)
            pe.wait_ge(loaded, 96)
            for d in range(2):
                gd = g[:, :, 8 * d:8 * d + 8]
                pe.matmul(psum[:, 4, d * N:(d + 1) * N], dn.tri[:, d, :], gd, start=True, stop=True)
                mm = pe.matmul(psum[:, 5, d * N:(d + 1) * N], s.ones[:], gd, start=True, stop=True)
            mm.then_inc(sums, 1)

        @block.scalar
        def _(act):
            norm.act(act)
            s.act_split(act, p0 + 1, (p0 + 1) % 2)
            act.wait_ge(s.panel_used.sem, p0 + 1)
            act.activation(tiled(ab[:]), banks(s, 0)[0:48], ACT.Copy).then_inc(ab_ready, 1)
            act.wait_ge(loaded, 96)
            act.activation(dts[:, 1, :], dts[:, 1, :], ACT.Exp).then_inc(act_step, 1)
            act.wait_ge(dve_step, 2)
            act.activation(e[:], u[:], ACT.Abs).then_inc(act_step, 1)
            act.wait_ge(act_step, 2)
            act.activation(e[:], e[:], ACT.Exp, scale=-1.0).then_inc(act_step, 1)
            act.wait_ge(dve_step, 4)
            act.activation(l[:], w[:], ACT.Ln).then_inc(act_step, 1)
            by = ab_tok[:].rearrange("p (n c) -> p n c", c=48)
            act.activation(by[:, :, 32:48], by[:, :, 32:48], ACT.Sigmoid).then_inc(beta_ready, 1)
            act.wait_ge(sums, 1)
            act.activation(tok[:, GC_], psum[:, 4, 0:2 * N].rearrange("p (d n) -> p d n", d=2), ACT.Copy
                           ).then_inc(act_step, 1)
            act.activation(gl[:], psum[:, 5, 0:2 * N].rearrange("p (d n) -> p d n", d=2), ACT.Copy,
                           scale=float(D)).then_inc(act_step, 1)
            act.wait_ge(act_step, 6)
            act.activation(tok[:, EG_], tok[:, GC_], ACT.Exp)
            act.activation(tok[:, EL_], gl[:], ACT.Exp)
            act.wait_ge(dve_step, 10)
            act.activation(tok[:, EK_], tok[:, EK_], ACT.Exp)

        @block.vector
        def _(dve):
            norm.dve(dve)
            by = ab_tok[:].rearrange("p (n c) -> p n c", c=48)
            dve.wait_ge(turned, 1)
            dve.tensor_copy(ab_tok[:], psum[:, 3, 0:NT * 48]).then_inc(dve_step, 1)
            dve.wait_ge(dve_step, 1)
            dve.wait_ge(loaded, 96)
            dve.tensor_tensor(u[:], by[:, :, 0:16], to_all(dts[:, 0, :]), ALU.add).then_inc(dve_step, 1)
            dve.wait_ge(act_step, 3)
            dve.tensor_scalar(w[:], e[:], 1.0, None, ALU.add).then_inc(dve_step, 2)
            dve.wait_ge(dve_step, 4)
            dve.scalar_tensor_tensor(e[:], w[:], -1.0, e[:], ALU.add, ALU.subtract)
            dve.reciprocal(r[:], w[:]).then_inc(dve_step, 1)
            dve.wait_ge(dve_step, 5)
            dve.tensor_tensor(e[:], e[:], r[:], ALU.mult).then_inc(dve_step, 1)
            dve.wait_ge(act_step, 4)
            dve.scalar_tensor_tensor(u[:], u[:], 0.0, l[:], ALU.max, ALU.add).then_inc(dve_step, 1)
            dve.wait_ge(dve_step, 7)
            dve.tensor_tensor(u[:], u[:], e[:], ALU.subtract).then_inc(dve_step, 1)
            dve.wait_ge(dve_step, 8)
            dve.scalar_tensor_tensor(g[:], u[:], -1.0, to_all(dts[:, 1, :]), ALU.mult, ALU.mult
                                     ).then_inc(dve_step, 1)
            dve.wait_ge(dve_step, 9)
            dve.wait_ge(beta_ready, 1)
            for d in range(2):
                for q, src, f in ((G_, g[:, :, 8 * d:8 * d + 8], 1.0), (BETA_, by[:, :, 32 + 8 * d:40 + 8 * d], 1.0),
                                  (NBETA_, by[:, :, 32 + 8 * d:40 + 8 * d], -1.0)):
                    dve.tensor_scalar(tok[:, q, d].rearrange("p (n h) -> p n h", h=DN_H), src, f, None, ALU.mult)
            dve.wait_ge(act_step, 6)
            dve.tensor_tensor(tok[:, EK_], gl[:], tok[:, GC_], ALU.subtract).then_inc(dve_step, 1)
            dve.sem_inc(s.set_free.sem, 1)
    norm.done()
    s.p0 += 1
    s.set_free.base += 1


class Back:

    def __init__(self, s, ctx):
        self.landed, self.high, self.low = (ctx.enter_context(s.nc.semaphore(f"y_{n}"))
                                            for n in ("landed", "high", "low"))


def delta_stage(s, dn, back):
    nc, psum, I, p0 = s.nc, s.psum, s.I, s.p0
    FULL_R0, FULL_KK, FULL_R1, FULL_T0, FULL_KTR, FULL_L2Q, FULL_VTR, FULL_T1, FULL_QK, FULL_W0, FULL_W1 = range(1, 12)
    (READ_R0, READ_V, READ_KK, READ_R1, READ_Z, READ_T0, READ_KTR, READ_L2Q, READ_VTR, READ_T1, READ_QK, READ_W0,
     READ_W1) = range(1, 14)
    FULLS, READS = FULL_W1, READ_W1
    FILL = [4] * 6 + [3] * 4 + [2] * 6
    with ExitStack() as ctx:
        def sem(name):
            return ctx.enter_context(nc.semaphore("dn_" + name))
        head_ready, k_read, q_read, grp_read, grp_full = (
            sem(n) for n in ("head_ready", "k_read", "q_read", "grp_read", "grp_full"))
        conv_step = {n: sem(f"conv_{n}") for n in "kqv"}
        silu_done = {n: sem(f"silu_{n}") for n in "kqv"}
        sq_ready = {n: sem(f"square_{n}") for n in "kq"}
        l2k_full, l2k_read, recip_k, recip_q, kn_ready, qn_ready = (
            sem(n) for n in ("l2k_full", "l2k_read", "recip_k", "recip_q", "kn_ready", "qn_ready"))
        e_read, e_ready, d_ready, bt_step, bt_ready, tt_init = (
            sem(n) for n in ("e_read", "e_ready", "d_ready", "bt_step", "bt_ready", "tt_init"))
        qg_ready, kg_ready, kd_ready, bm_ready = (
            sem(n) for n in ("qg_ready", "kg_ready", "kd_ready", "bm_ready"))
        pt_ready = [sem(f"pt_ready{d}") for d in range(2)]
        xl_full, xl_ready, d_full, t_upd, u_full, ub_ready = (
            sem(n) for n in ("xl_full", "xl_ready", "d_full", "t_upd", "u_full", "ub_ready"))
        s_loaded, ws_full, vn_ready, sn_full, s_ready, o_full, o_act, o_dve = (
            sem(n) for n in ("s_loaded", "ws_full", "vn_ready", "sn_full", "s_ready", "o_full", "o_act", "o_dve"))
        fin_full, fin_ready, fin_stored, osq_ready, post_full, post_std, post_step, y_done, y_stored = (
            sem(n) for n in ("fin_full", "fin_ready", "fin_stored", "osq_ready", "post_full", "post_std",
                             "post_step", "y_done", "y_stored"))
        block = ctx.enter_context(nc.Block())

        def blk(t, n):
            return t[:, n * P:(n + 1) * P]

        def by_block(t):
            return t[:].rearrange("p (n w) -> p n w", w=P)

        def of_group(g):
            return psum[:, 3 * g:3 * g + 3, 0:TW].rearrange("p b (n w) -> p b n w", w=P)

        def by_bank(t):
            return t[:].rearrange("p (b n w) -> p b n w", b=3, w=P)

        def const(q, d):
            return dn.hs[:, q, d, :].rearrange("p (n o) -> p n o", o=1).to_broadcast([P, NT, P])

        def const_b(q, d):
            return dn.hs[:, q, d, :].rearrange("p (b n o) -> p b n o", b=3, o=1).to_broadcast([P, 3, 3, P])

        def mask(m, n):
            return m.rearrange("p (o w) -> p o w", o=1).to_broadcast([P, n, P])

        def at_head(t, part, h, j):
            return t[:, ds(h + part * DN_H, 1), j:j + 1].rearrange("p a b -> p (a b)")

        PART = {"q": 0, "k": 1, "v": 2}
        LAST = DN_H - 1

        def heads(eng, body):
            with eng.Fori(0, LAST) as h:
                body(h, True)
            body(LAST, False)

        @block.sync
        def _(sp):
            def load(h, j):
                s.sp_load(sp, 4 * h + (p0 + j), (p0 + j) % 2)

            sp.sem_inc(fin_stored, 32)
            sp.sem_inc(y_stored, 16)
            for j in range(2, 6):
                load(0, j)

            def body(h, more):
                for d in range(2):
                    sp.dma_start(dn.state[d][0][:], I["state_delta"][d, ds(h, 1)].rearrange("a p n -> p (a n)")
                                 ).then_inc(s_loaded, 16)
                if more:
                    load(h, 6)
                    load(h, 7)
                else:
                    sp.wait_ge(s.panel_used.sem, p0 + 4 * DN_H)
                    sp.wait_ge(y_stored, 16 * DN_H)
                    sp.dma_start(s.hl[:, 0:LAST, :].bitcast(F32), s.y_dram).then_inc(back.landed, 16)
                sp.wait_ge(fin_ready, 2 * h + 2)
                for d in range(2):
                    sp.dma_start(s.O["delta"][ds(h, 1), d].rearrange("a p n -> p (a n)"), dn.fin[d]
                                 ).then_inc(fin_stored, 16)
                if more:
                    load(h, 8)
                    load(h, 9)
                    sp.wait_ge(y_done, h + 2)
                    sp.dma_start(s.y_dram[:, ds(h, 1), :].rearrange("p a t -> p (a t)"), dn.osum[:]
                                 ).then_inc(y_stored, 16)
            heads(sp, body)
            sp.wait_ge(fin_stored, 32 * DN_H + 32)

        @block.gpsimd
        def _(pool):
            def mul(out, a, b):
                return pool.tensor_tensor(out, a, b, ALU.mult)

            def split(h, j):
                s.pool_split(pool, 4 * h + (p0 + j), (p0 + j) % 2)

            split(0, 1)
            split(0, 2)

            def body(h, more):
                def decayed_q(d):
                    if d == 0:
                        pool.wait_ge(qn_ready, h + 1)
                    mul(dn.qg[d][:], dn.qn[:], dn.qg[d][:]).then_inc(qg_ready, 1)

                def kg(d):
                    mul(by_block(dn.ub[d]), by_block(dn.k_tok), const(EG_, d)).then_inc(kg_ready, 1)

                def kd(d):
                    if d == 1:
                        pool.wait_ge(kg_ready, 2 * h + 2)
                        pool.wait_ge(kd_ready, 2 * h + 1)
                    mul(by_block(dn.kd[d]), by_block(dn.k_tok), const(EK_, d)).then_inc(kd_ready, 1)

                def decayed():
                    pool.wait_ge(grp_read, READS * h + READ_QK)
                    mul(dn.pt[1][:], dn.pt[1][:], dn.qk[:]).then_inc(pt_ready[1], 1)

                def masked(d, c):
                    n = 36 * h + (18 * d + c)
                    if d or c >= 2:
                        pool.wait_ge(xl_full, n - 1)
                    elif c == 0:
                        pool.wait_ge(y_stored, 16 * h + 16)
                    g = c % 3
                    cols = slice(g * TW, (g + 1) * TW)
                    mul(dn.bm[c % 2].rearrange("p (n w) -> p n w", w=P),
                        dn.wt[d][:, cols].rearrange("p (n w) -> p n w", w=P),
                        mask(dn.level[:, d, 1 + c // 3, :], 3)).then_inc(bm_ready, 1)

                split(h, 3)
                split(h, 4)
                pool.wait_ge(head_ready, h + 1)
                later = {3: (kg, 0), 7: (kg, 1), 31: (decayed_q, 0), 33: (decayed_q, 1), 34: (kd, 0), 35: (kd, 1)}
                for d in range(2):
                    pool.wait_ge(bt_ready, 2 * h + (d + 1))
                    for c in range(SLOTS):
                        masked(d, c)
                        if more and (d, c) == (0, 1):
                            split(h, 5)
                        if d * SLOTS + c in later:
                            if (d, c) == (0, 3):
                                pool.wait_ge(grp_read, READS * h + READ_KTR)
                            f, of = later[d * SLOTS + c]
                            f(of)
                decayed()
                if more:
                    split(h, 6)
                else:
                    for c in range(LAST):
                        pool.wait_ge(back.high, c + 1)
                        hl = s.hl[:, c, :]
                        pool.tensor_tensor(hl, hl.bitcast(F32), s.hh[:, c, :].bitcast(F32), ALU.subtract
                                           ).then_inc(back.low, 1)
            heads(pool, body)

        @block.tensor
        def _(pe):
            def sums(g, t):
                for i in range(TT):
                    mm = pe.matmul(psum[:, 3 * g + i, 0:TW], s.ones[:], t[:, i * TW:(i + 1) * TW],
                                   start=True, stop=True)
                return mm

            def nine(g, lhs, rhs, turn=False):
                for n in range(NT):
                    out = psum[:, 3 * g + n // 3, (n % 3) * P:(n % 3 + 1) * P]
                    if turn:
                        mm = pe.transpose(out, blk(lhs, n), s.ident[:])
                    else:
                        mm = pe.matmul(out, lhs(n), rhs(n), start=True, stop=True)
                return mm

            def ahead(p, m0, m1, k_reads):
                for m in range(m0, m1):
                    j, t, k = m // 24, m % 24 // KC, m % KC
                    buf = (p0 + j) % 2
                    if m % 24 == 0:
                        pe.wait_ge(s.split_low.sem, p + (j + 1))
                    if m == 24:
                        pe.wait_ge(k_read, k_reads)
                    mm = three_products(pe, psum[:, t, 0:TW], s.wh[buf][:, k * P:(k + 1) * P],
                                        s.wl[buf][:, k * P:(k + 1) * P], s.hh[:, k, t * TW:(t + 1) * TW],
                                        s.hl[:, k, t * TW:(t + 1) * TW], k == 0, k == KC - 1)
                    if m % 24 == 23:
                        mm.then_inc(s.panel_used.sem, 1)

            ahead(p0, 0, 48, 1)
            pe.wait_ge(sq_ready["k"], 1)
            sums(1, dn.raw["v"]).then_inc(l2k_full, 1)

            def body(h, more):
                def panel(j, g):
                    pe_panel(s, pe, 4 * h + (p0 + j), (p0 + j) % 2, g)

                def read(n):
                    pe.wait_ge(grp_read, READS * h + n)

                def rows(d, g):
                    nine(g, lambda n: dn.hs[:, G_, d, n:n + 1].to_broadcast([P, P]),
                         lambda n: dn.tri[:, d, :]).then_inc(grp_full, 1)

                pe.wait_ge(l2k_read, h + 1)
                pe.wait_ge(head_ready, h + 1)
                rows(0, 1)
                pe.wait_ge(post_std, h + 1)
                pe.wait_ge(q_read, h + 1)
                panel(2, 0)
                read(READ_R0)
                pe.wait_ge(e_read, 2 * h + 1)
                pe.wait_ge(kn_ready, h + 1)
                nine(1, lambda n: blk(dn.kn, n), lambda n: blk(dn.kn, n)).then_inc(grp_full, 1)
                read(READ_V)
                rows(1, 0)
                read(READ_KK)
                panel(3, 1)
                read(READ_R1)
                pe.wait_ge(e_read, 2 * h + 2)
                pe.wait_ge(tt_init, 2 * h + 1)
                nine(0, dn.tt[0], None, True).then_inc(grp_full, 1)
                read(READ_Z)
                nine(1, dn.kn, None, True).then_inc(grp_full, 1)

                def levels(d):
                    def x_of(c):
                        n = 36 * h + (18 * d + c)
                        g = c % 3
                        pe.wait_ge(bm_ready, n + 1)
                        if c >= 3:
                            pe.wait_ge(t_upd, n - 2)
                        if d or c >= 2:
                            pe.wait_ge(xl_ready, n - 1)
                        for i in range(3):
                            mm = pe.matmul(psum[:, 6 + c % 2, i * P:(i + 1) * P],
                                           dn.bm[c % 2][:, i * P:(i + 1) * P], blk(dn.t[d], 3 * g + i),
                                           start=True, stop=True)
                        mm.then_inc(xl_full, 1)

                    def d_of(c):
                        g = c % 3
                        if c == 0:
                            read(READ_VTR if d else READ_KTR)
                        pe.wait_ge(xl_ready, 36 * h + (18 * d + c + 1))
                        for i in range(3):
                            x = dn.xl[c % 2][:, i * P:(i + 1) * P]
                            if c < SLOTS - NB:
                                pe.matmul(psum[:, g, i * P:(i + 1) * P], blk(dn.tt[d], 3 * g + i), x,
                                          start=True, stop=True)
                            mm = pe.matmul(psum[:, 3 + g, i * P:(i + 1) * P], x, blk(dn.tt[d], 3 * g + i),
                                           start=True, stop=True)
                        mm.then_inc(d_full, 1)
                    x_of(0)
                    for c in range(1, SLOTS):
                        x_of(c)
                        d_of(c - 1)
                    d_of(SLOTS - 1)

                read(READ_T0)
                levels(0)
                pe.wait_ge(t_upd, 36 * h + SLOTS - NB)
                pe.wait_ge(sq_ready["q"], h + 1)
                sums(0, dn.kd[0]).then_inc(grp_full, 1)
                pe.wait_ge(t_upd, 36 * h + 18)
                pe.wait_ge(silu_done["v"], h + 1)
                nine(1, dn.vf, None, True).then_inc(grp_full, 1)
                pe.wait_ge(tt_init, 2 * h + 2)
                read(READ_L2Q)
                nine(0, dn.tt[1], None, True).then_inc(grp_full, 1)
                read(READ_T1)
                levels(1)
                pe.wait_ge(t_upd, 36 * h + 36)
                pe.wait_ge(qn_ready, h + 1)
                nine(1, lambda n: blk(dn.kn, n), lambda n: blk(dn.qn, n)).then_inc(grp_full, 1)
                for d in range(2):
                    if d:
                        read(READ_W0)
                    pe.wait_ge(kg_ready, 2 * h + (d + 1))
                    nine(0, lambda n: blk(dn.ub[d], n), lambda n: blk(dn.tt[d], n)).then_inc(grp_full, 1)
                    if d:
                        pe.wait_ge(ub_ready, 2 * h + 1)
                    else:
                        read(READ_QK)
                    nine(1, lambda n: blk(dn.tt[d], n), lambda n: blk(dn.v_tok, n)).then_inc(u_full, 1)
                read(READ_W1)
                pe.wait_ge(ub_ready, 2 * h + 2)
                pe.wait_ge(kd_ready, 2 * h + 2)
                for d in range(2):
                    pe.wait_ge(pt_ready[d], h + 1)
                pe.wait_ge(qg_ready, 2 * h + 2)

                def fill(i):
                    if more:
                        m = sum(FILL[:i])
                        ahead(4 * h + (p0 + 4), m, m + FILL[i], h + 2)

                for d in range(2):
                    mm = pe.matmul(psum[:, 5, 0:P], blk(dn.ub[d], 0), blk(dn.pt[d], 0), start=d == 0, stop=d == 1)
                mm.then_inc(o_full, 1)
                for d in range(2):
                    mm = pe.matmul(psum[:, 3 + d, 0:P], blk(dn.kd[d], 0), blk(dn.ub[d], 0), start=True, stop=True)
                mm.then_inc(fin_full, 1)
                pe.wait_ge(s_loaded, 32 * h + 32)
                for t in range(8):
                    n_of = (1 + t, 8 - t)
                    if t == 0:
                        fill(0)
                        pe.wait_ge(fin_ready, 2 * h + 2)
                    for d in range(2):
                        if t:
                            pe.wait_ge(s_ready, 14 * h + (2 * t - 1 + d))
                        pe.matmul(psum[:, 3 + d, 0:P], blk(dn.wt[d], n_of[d]), dn.state[d][t % 2][:],
                                  start=True, stop=True).then_inc(ws_full, 1)
                    if t:
                        fill(2 * t)
                    for d in range(2):
                        k = 1 + 2 * t + d
                        if k >= 3:
                            j = k - 3
                            if j < 9:
                                pe.wait_ge(o_act, 9 * h + (j + 1))
                            else:
                                pe.wait_ge(o_dve, 8 * h + (j - 8))
                        pe.matmul(psum[:, 5 + k % 3, 0:P], dn.state[d][t % 2][:], blk(dn.qg[d], n_of[d]),
                                  start=True, stop=False)
                    for d in range(2):
                        k = 1 + 2 * t + d
                        pe.wait_ge(vn_ready, 16 * h + (2 * t + d + 1))
                        if t < 7:
                            pe.matmul(psum[:, 3 + d, P:2 * P], blk(dn.kd[d], n_of[d]), dn.vn[d],
                                      start=True, stop=True).then_inc(sn_full, 1)
                        pe.matmul(psum[:, 5 + k % 3, 0:P], dn.vn[d], blk(dn.pt[d], n_of[d]),
                                  start=False, stop=True).then_inc(o_full, 1)
                    fill(2 * t + 1)
                if more:
                    pe.wait_ge(s_ready, 14 * h + 14)
                    pe.wait_ge(o_dve, 8 * h + 8)
                    pe.wait_ge(sq_ready["k"], h + 2)
                    sums(1, dn.raw["v"]).then_inc(l2k_full, 1)
                    pe.wait_ge(q_read, h + 2)
                else:
                    pe.wait_ge(o_dve, 8 * h + 8)
                    pe.wait_ge(s_ready, 14 * h + 14)
                pe.wait_ge(osq_ready, h + 1)
                sums(0 if more else 1, dn.t[0]).then_inc(post_full, 1)
                if not more:
                    pe.wait_ge(s.split_low.sem, p0 + 4 * DN_H + 1)
                    for c in range(LAST):
                        pe.wait_ge(back.low, c + 1)
                        pe_chunk(s, pe, p0 % 2, c)
            heads(pe, body)

        @block.scalar
        def _(act):
            def split(h, j):
                s.act_split(act, 4 * h + (p0 + j), (p0 + j) % 2)

            def used(h, j):
                act.wait_ge(s.panel_used.sem, 4 * h + (p0 + j + 1))

            def evac(out, g):
                return act.activation(tiled(out[:]), banks(s, g), ACT.Copy)

            def silu(n, t, i):
                act.wait_ge(conv_step[n], 7 * i)
                act.activation(t[:], t[:], ACT.Silu).then_inc(silu_done[n], 1)

            def square(n, t, sq, i):
                act.wait_ge(silu_done[n], i)
                act.activation(sq[:], t[:], ACT.Square).then_inc(sq_ready[n], 1)

            def norm_k(i):
                act.wait_ge(l2k_full, i)
                act.activation(tiled(dn.raw["v"][:]), banks(s, 1), ACT.Sqrt, scale=float(D), bias=s.eps[:, 0:1]
                               ).then_inc(l2k_read, 1)

            act.sem_inc(post_std, 1)
            split(0, 1)
            used(0, 0)
            evac(dn.raw["k"], 0).then_inc(k_read, 1)
            split(0, 2)
            silu("k", dn.kn, 1)
            square("k", dn.kn, dn.raw["v"], 1)
            used(0, 1)
            evac(dn.raw["q"], 0).then_inc(q_read, 1)
            norm_k(1)

            def body(h, more):
                def full(n):
                    act.wait_ge(grp_full, FULLS * h + n)

                def take(out, g, func=ACT.Copy, **kw):
                    return act.activation(tiled(out[:]), banks(s, g), func, **kw).then_inc(grp_read, 1)

                def decay(d):
                    act.wait_ge(e_ready, 2 * h + (d + 1))
                    act.activation(dn.pt[d][:], dn.pt[d][:], ACT.Exp).then_inc(d_ready, 1)

                def x_copies(d):
                    for c in range(SLOTS):
                        n = 36 * h + (18 * d + c)
                        act.wait_ge(xl_full, n + 1)
                        if d or c >= 2:
                            act.wait_ge(d_full, n - 1)
                        elif c == 0:
                            act.wait_ge(y_stored, 16 * h + 16)
                        act.activation(dn.xl[c % 2], psum[:, 6 + c % 2, 0:TW], ACT.Copy).then_inc(xl_ready, 1)
                        if more and d == 0 and c == 0:
                            split(h, 5)
                        if d == 0 and c == 10:
                            act.wait_ge(grp_read, READS * h + READ_Z)
                            act.activation(dn.silu_z[:], dn.silu_z[:], ACT.Silu)
                            silu("q", dn.qn, h + 1)
                            square("q", dn.qn, dn.kd[0], h + 1)
                        if d == 0 and c == 16:
                            silu("v", dn.vf, h + 1)

                split(h, 3)
                full(FULL_R0)
                take(dn.qg[0], 1, ACT.Exp)
                used(h, 2)
                act.wait_ge(kn_ready, h + 1)
                take(dn.raw["v"], 0)
                split(h, 4)
                full(FULL_KK)
                take(dn.kk, 1)
                decay(0)
                full(FULL_R1)
                take(dn.qg[1], 0, ACT.Exp)
                decay(1)
                used(h, 3)
                act.wait_ge(y_done, h + 1)
                take(dn.silu_z, 1)
                full(FULL_T0)
                take(dn.t[0], 0)
                full(FULL_KTR)
                take(dn.k_tok, 1)
                x_copies(0)
                full(FULL_L2Q)
                take(dn.kd[0], 0, ACT.Sqrt, scale=float(D), bias=s.eps[:, 0:1])
                full(FULL_VTR)
                take(dn.v_tok, 1)
                full(FULL_T1)
                take(dn.t[1], 0)
                x_copies(1)
                full(FULL_QK)
                take(dn.qk, 1)
                for d in range(2):
                    full(FULL_W0 + d)
                    take(dn.wt[d], 0)

                def output(n, k):
                    act.wait_ge(o_full, 17 * h + (k + 1))
                    act.activation(blk(dn.osum, n), psum[:, 5 + k % 3, 0:P], ACT.Copy).then_inc(o_act, 1)
                output(0, 0)
                act.wait_ge(fin_full, h + 1)
                for d in range(2):
                    act.activation(dn.fin[d], psum[:, 3 + d, 0:P], ACT.Copy).then_inc(fin_ready, 1)
                for t in range(4):
                    for d in range(2):
                        output((1 + t, 8 - t)[d], 1 + 2 * t + d)
                    if not more:
                        if t == 0:
                            act.wait_ge(back.landed, 16)
                        for c in range(2 * t, min(2 * t + 2, LAST)):
                            act.activation(s.hh[:, c, :], s.hl[:, c, :].bitcast(F32), ACT.Copy
                                           ).then_inc(back.high, 1)
                    if more and t == 2:
                        used(h, 4)
                        evac(dn.raw["k"], 0).then_inc(k_read, 1)
                if more:
                    split(h, 6)
                    silu("k", dn.kn, h + 2)
                    square("k", dn.kn, dn.raw["v"], h + 2)
                    used(h, 5)
                    evac(dn.raw["q"], 0).then_inc(q_read, 1)
                act.wait_ge(o_dve, 8 * h + 8)
                act.activation(dn.t[0][:], dn.osum[:], ACT.Square).then_inc(osq_ready, 1)
                if more:
                    norm_k(h + 2)
                act.wait_ge(post_full, h + 1)
                act.activation(tiled(dn.tt[0][:]), banks(s, 0 if more else 1), ACT.Sqrt, scale=float(D // P),
                               bias=s.eps[:, 0:1]).then_inc(post_std, 1)
            heads(act, body)

        @block.vector
        def _(dve):
            tok = dn.tok[:].rearrange("p (v h) -> p v h", h=DN_H)
            TAPS = ((0, -2), (1, -1), (3, 1))
            NORM_Q = (1, 2, 4, 5, 7, 8)
            NQ = len(NORM_Q)

            def conv(name, out, i, h, m):
                part, x = PART[name], dn.raw[name]
                base = 7 * i - 7
                if m == 0:
                    dve.tensor_scalar(out[:], x[:], at_head(dn.conv, part, h, 2), None, ALU.mult
                                      ).then_inc(conv_step[name], 1)
                    return
                tap, off = TAPS[(m - 1) // 2]
                lo, hi = ((0, TP), (TP, T))[(m - 1) % 2]
                a, b = (lo - off, hi) if off < 0 else (lo, hi - off)
                dve.wait_ge(conv_step[name], base + (m - 1 if m > 2 else 1))
                dve.scalar_tensor_tensor(out[:, a:b], x[:, a + off:b + off], at_head(dn.conv, part, h, tap),
                                         out[:, a:b], ALU.mult, ALU.add).then_inc(conv_step[name], 1)

            def norm_k(i):
                dve.wait_ge(l2k_read, i)
                dve.reciprocal(dn.raw["v"][:], dn.raw["v"][:]).then_inc(recip_k, 1)
                dve.wait_ge(recip_k, i)
                dve.tensor_tensor(dn.kn[:], dn.kn[:], dn.raw["v"][:], ALU.mult).then_inc(kn_ready, 1)

            def constants(h):
                dve.tensor_copy(dn.hs[:].rearrange("p a d n -> p (a d n)"),
                                tok[:, :, ds(h, 1)].rearrange("p v a -> p (v a)")).then_inc(head_ready, 1)

            def decay(h, d):
                dve.wait_ge(grp_read, READS * h + (READ_R1 if d else READ_R0))
                dve.wait_ge(head_ready, h + 1)
                dve.tensor_tensor(by_bank(dn.pt[d]), of_group(1 - d), const_b(GC_, d), ALU.subtract
                                  ).then_inc(e_read, 1)
                dve.wait_ge(e_read, 2 * h + (d + 1))
                dve.tensor_tensor(by_block(dn.pt[d]), by_block(dn.pt[d]), mask(dn.low[:, d, :], NT), ALU.min
                                  ).then_inc(e_ready, 1)

            dve.sem_inc(y_done, 1)
            constants(0)
            dve.wait_ge(k_read, 1)
            for m in range(7):
                conv("k", dn.kn, 1, 0, m)
            norm_k(1)
            decay(0, 0)

            def body(h, more):
                def norm_q(t):
                    cols = slice(t * T // NQ, (t + 1) * T // NQ)
                    std, q = dn.kd[0][:, cols], dn.qn[:, cols]
                    dve.wait_ge(grp_read, READS * h + READ_L2Q)
                    dve.reciprocal(std, std).then_inc(recip_q, 1)
                    dve.wait_ge(recip_q, NQ * h + (t + 1))
                    v = dve.scalar_tensor_tensor(q, q, P ** -0.5, std, ALU.mult, ALU.mult)
                    if t == NQ - 1:
                        v.then_inc(qn_ready, 1)

                def kk_beta(d):
                    dve.wait_ge(d_ready, 2 * h + (d + 1))
                    dve.wait_ge(grp_read, READS * h + READ_KK)
                    dve.tensor_tensor(dn.wt[d][:], dn.pt[d][:], dn.kk[:], ALU.mult).then_inc(bt_step, 1)
                    dve.wait_ge(bt_step, 4 * h + (2 * d + 1))
                    dve.tensor_tensor(by_block(dn.wt[d]), by_block(dn.wt[d]), const(BETA_, d), ALU.mult
                                      ).then_inc(bt_ready, 1)

                def t_start(d):
                    dve.wait_ge(bt_ready, 2 * h + (d + 1))
                    if d:
                        dve.wait_ge(conv_step["v"], 7 * h + 7)
                    dve.tensor_tensor(by_block(dn.tt[d]), by_block(dn.wt[d]), mask(dn.level[:, d, 0, :], NT),
                                      ALU.mult).then_inc(bt_step, 1)
                    dve.wait_ge(bt_step, 4 * h + (2 * d + 2))
                    dve.tensor_tensor(by_block(dn.tt[d]), mask(s.ident[:], NT), by_block(dn.tt[d]), ALU.subtract
                                      ).then_inc(tt_init, 1)

                kk_beta(0)
                t_start(0)
                decay(h, 1)
                for d in range(2):
                    for c in range(SLOTS):
                        n = 36 * h + (18 * d + c)
                        g = c % 3
                        cols = slice(g * TW, (g + 1) * TW)
                        dve.wait_ge(d_full, n + 1)
                        if c < SLOTS - NB:
                            dve.tensor_tensor(dn.t[d][:, cols], dn.t[d][:, cols], psum[:, g, 0:TW], ALU.subtract)
                        dve.tensor_tensor(dn.tt[d][:, cols], dn.tt[d][:, cols], psum[:, 3 + g, 0:TW],
                                          ALU.subtract).then_inc(t_upd, 1)
                        if d == 0 and c == 0:
                            kk_beta(1)
                        if d == 0 and 1 <= c < 8:
                            if c == 1:
                                dve.wait_ge(q_read, h + 1)
                            conv("q", dn.qn, h + 1, h, c - 1)
                        if d == 0 and 8 <= c < 15:
                            if c == 8:
                                dve.wait_ge(grp_read, READS * h + READ_V)
                                dve.wait_ge(fin_stored, 32 * h + 32)
                            conv("v", dn.vf, h + 1, h, c - 8)
                        if d == 0 and c == 15:
                            t_start(1)
                        if d == 1 and c in NORM_Q:
                            norm_q(NORM_Q.index(c))
                dve.wait_ge(grp_read, READS * h + READ_QK)
                dve.wait_ge(d_ready, 2 * h + 1)
                dve.tensor_tensor(dn.pt[0][:], dn.pt[0][:], dn.qk[:], ALU.mult).then_inc(pt_ready[0], 1)
                for d in range(2):
                    dve.wait_ge(u_full, 2 * h + (d + 1))
                    dve.tensor_tensor(by_bank(dn.ub[d]), of_group(1), const_b(BETA_, d), ALU.mult
                                      ).then_inc(ub_ready, 1)
                k_steps = {3: (0,), 4: (1, 2), 5: (3, 4), 6: (5, 6)}
                for t in range(8):
                    n_of = (1 + t, 8 - t)
                    for d in range(2):
                        n = n_of[d]
                        dve.wait_ge(ws_full, 16 * h + (2 * t + d + 1))
                        if t:
                            dve.wait_ge(o_full, 17 * h + (2 * t + d))
                        else:
                            dve.wait_ge(ub_ready, 2 * h + 2)
                        dve.scalar_tensor_tensor(dn.vn[d], psum[:, 3 + d, 0:P], dn.hs[:, NBETA_, d, n:n + 1],
                                                 blk(dn.ub[d], n), ALU.mult, ALU.add).then_inc(vn_ready, 1)
                    if t < 7:
                        for d in range(2):
                            n = n_of[d]
                            dve.wait_ge(sn_full, 14 * h + (2 * t + d + 1))
                            if t:
                                dve.wait_ge(s_ready, 14 * h + (2 * t + d - 1))
                            dve.scalar_tensor_tensor(dn.state[d][(t + 1) % 2][:], dn.state[d][t % 2][:],
                                                     dn.hs[:, EL_, d, n:n + 1], psum[:, 3 + d, P:2 * P],
                                                     ALU.mult, ALU.add).then_inc(s_ready, 1)
                    if t >= 4:
                        for d in range(2):
                            k = 1 + 2 * t + d
                            dve.wait_ge(o_full, 17 * h + (k + 1))
                            dve.wait_ge(o_act, 9 * h + 9)
                            o = blk(dn.osum, n_of[d])
                            dve.tensor_tensor(o, o, psum[:, 5 + k % 3, 0:P], ALU.add).then_inc(o_dve, 1)
                    if more:
                        for m in k_steps.get(t, ()):
                            if m == 0:
                                dve.wait_ge(k_read, h + 2)
                            conv("k", dn.kn, h + 2, h + 1, m)
                if more:
                    constants(h + 1)
                    norm_k(h + 2)
                    decay(h + 1, 0)
                dve.wait_ge(post_std, h + 2)
                dve.reciprocal(dn.tt[0][:], dn.tt[0][:]).then_inc(post_step, 1)
                dve.wait_ge(post_step, 2 * h + 1)
                dve.scalar_tensor_tensor(dn.osum[:], dn.osum[:], dn.onorm[:, 0:1], dn.tt[0][:], ALU.mult, ALU.mult
                                         ).then_inc(post_step, 1)
                dve.wait_ge(post_step, 2 * h + 2)
                dve.tensor_tensor(dn.osum[:], dn.osum[:], dn.silu_z[:], ALU.mult).then_inc(y_done, 1)
            heads(dve, body)
    s.p0 += ODD_PANELS


def pack_delta(f):
    bf = mybir.dt.np(BF16)
    i = np.arange(P)
    j, c = i[:, None], i[None, :]
    level = np.zeros((P, 2, NL + 1, P), np.float32)
    for n, b in enumerate([1] + LEVELS):
        pair = (j // (2 * b) == c // (2 * b)) & (j // b % 2 == 0) & (c // b % 2 == 1)
        level[:, 0, n], level[:, 1, n] = pair, pair.T
    low = np.stack([np.where(j <= c, 0, NEG), np.where(j >= c, 0, NEG)], 1)
    tri = np.stack([j <= c, j >= c], 1).astype(np.float32)
    return {
        "level": level.astype(bf), "low": low.astype(bf), "tri": tri,
        "dts": np.broadcast_to(np.stack([f["dn_dt_bias"][0].reshape(16), f["dn_a_log"][0].reshape(16)]), (P, 2, 16)),
        "conv_dn": columns(f["conv_dn"][0]).transpose(0, 2, 1),
        "onorm": f["dn_o_norm"][0][:, None],
        "state_delta": f["state_delta"][0, 0],
    }


def build(nc, I, O):
    with ExitStack() as ctx:
        s = Trunk(nc, ctx, I, O)
        even = even_buffer(s)
        squares = Squares(s)
        in_proj_stage(s, even, EVEN_PANELS, Norm(s, ctx, 0, 0, load=True))
        rg_stage(s, even)
        attention_stage(s, even)
        out_proj_stage(s, 0, squares)
        ffn_stage(s, 0, Norm(s, ctx, 0, 1, squares=squares), squares)
        s.x_dram = nc.dram_tensor("x_spill", [P, KC, T], F32).ap()
        s.y_dram = nc.dram_tensor("y_spill", [P, KC - 1, T], F32).ap()
        dn = Delta(s)
        decay_stage(s, dn, Norm(s, ctx, 1, 0, squares=squares))
        back = Back(s, ctx)
        delta_stage(s, dn, back)
        out_proj_stage(s, 1, squares, dn.osum[:], back)
        ffn_stage(s, 1, Norm(s, ctx, 1, 1, squares=squares), squares)
        final_stage(s, squares)


def feature_major(a):
    return np.asarray(a).T.reshape(-1, P, a.shape[0]).transpose(1, 0, 2)


def columns(v):
    v = np.asarray(v)
    return np.moveaxis(v.reshape(*v.shape[:-1], -1, P), -1, 0)


def panels(w):
    w = np.asarray(w)
    return w.reshape(KC, P, -1, P).transpose(2, 1, 0, 3).reshape(-1, P, 1024)


def pack(inp):
    f = {k: np.asarray(v) for k, v in inp.items()}
    qperm = np.concatenate([np.arange(HD) + HD * h for c in range(4) for h in (c, c + 4)])
    w_in = f["w_in_even"][0]
    w_in = np.concatenate([w_in[:, :1024], w_in[:, 1024:1536][:, qperm], w_in[:, 1536:]], axis=1)
    w_out = f["w_out_even"][0]
    w_out = np.concatenate([w_out[:512], w_out[512:][qperm]], axis=0)
    stream = [panels(w_in), panels(w_out)]

    def ffn(layer):
        gate_up = panels(f["w_gu"][layer])
        down = f["w_down"][layer].reshape(FF_G, 2, P, 2, D // 2).transpose(0, 3, 2, 1, 4).reshape(-1, P, D)
        order = []
        for j in range(FF_G):
            for c in (2 * j, 2 * j + 1):
                order += [gate_up[c], gate_up[FF_CH + c]]
            if j:
                order += [down[2 * j - 2], down[2 * j - 1]]
        return np.stack(order + [down[-2], down[-1]])

    stream.append(ffn(0))
    w_odd = f["w_in_odd"][0]
    ab = w_odd[:, 4096:].reshape(D, 2, 16)
    ab_panel = np.zeros((D, P), np.float32)
    ab_panel[:, 0:16], ab_panel[:, 32:48] = ab[:, 0], ab[:, 1]
    stream.append(panels(ab_panel))
    heads = panels(w_odd[:, :4096]).reshape(4, DN_H, P, 1024)[[1, 0, 2, 3]]
    stream.append(heads.transpose(1, 0, 2, 3).reshape(-1, P, 1024))
    stream += [panels(f["w_out_odd"][0]), ffn(1), np.zeros((PAD, P, 1024), np.float32)]

    rgw = np.zeros((RG_CH, P, 4, P), np.float32)
    for d in range(2):
        for j, w in enumerate((f["rg_wa"], f["rg_wx"])):
            for b in range(8):
                o = 64 * (b % 2)
                rgw[b // 2, o:o + 64, 2 * d + j, o:o + 64] = w[0, d, b]
    rgb = np.stack([f["rg_ba"][0], f["rg_bx"][0]], axis=1).reshape(4, 512)
    i = np.arange(P)
    prev = np.where(i[None, :] >= i[:, None], 0, NEG).astype(np.float32)
    nxt = np.where(i[None, :] <= i[:, None], 0, NEG).astype(np.float32)
    none = np.full((P, P), NEG, np.float32)
    window = np.stack([np.stack([none if b == 0 else prev, none if b == 7 else nxt], 1) for b in range(8)], 1)
    inv = ROPE_BASE ** (-np.arange(0, 32, 2, dtype=np.float32) / 32)
    tok = np.arange(TL)
    ang = [(tok // GRID_W)[None].astype(np.float32) * inv[:, None],
           (tok % GRID_W)[None].astype(np.float32) * inv[:, None]]
    ang = np.concatenate([ang[0], ang[0], ang[1], ang[1]] * 2).astype(np.float32)
    rope = np.zeros((P, P), np.float32)
    for m in range(P):
        if m % 32 < 16:
            rope[m + 16, m] = -1.0
        else:
            rope[m - 16, m] = 1.0
    head_of = [h for c in range(4) for h in (c, c + 4)]
    bf = mybir.dt.np(BF16)
    return {
        "x": feature_major(np.concatenate([f["x_prompt"][0], f["x_sample"][0]])),
        "cond": np.broadcast_to(np.stack([f["c_ctx"], f["c"][0]]), (P, 2, D)),
        "stream": np.concatenate(stream),
        "wmod": np.concatenate([w.T for w in f["w_mod"]]).reshape(-1, P, D),
        "bmod": np.repeat(columns(f["b_mod"].reshape(-1))[:, :, None], 2, 2),
        "gain": columns(np.stack([f["g_mix"][0], f["g_ffn"][0], f["g_mix"][1], f["g_ffn"][1], f["g_final"]])),
        "ones": np.full((P, P), 1.0 / D, np.float32),
        "ident": np.eye(P, dtype=np.float32),
        "eps": np.full((P, 1), EPS, np.float32),
        "conv_rg": columns(np.concatenate([f["conv_rg"][0], f["conv_rg_b"]])).transpose(0, 2, 1),
        "rgw": rgw.reshape(RG_CH, P, 4 * P),
        "rgb": columns(rgb).transpose(0, 2, 1),
        "lam": columns(f["rg_lam"][0]).transpose(0, 2, 1),
        "h0": columns(f["state_rglru"][0, 0]).transpose(0, 2, 1),
        "ctx_k": f["cache_attn_k"][0, 0].reshape(TP, P).T,
        "ctx_v": f["cache_attn_v"][0, 0].reshape(TP, P),
        "sink": np.broadcast_to(f["attn_sink"][0][head_of], (P, HEADS)),
        "window": window.astype(bf),
        "ident_bf": np.eye(P, dtype=bf),
        "cos": np.cos(ang), "sin": np.sin(ang), "rope": rope,
    } | pack_delta(f)


def kernel(**inputs):
    import concourse.bacc as bacc
    from concourse.bass_utils import run_bass_kernel_spmd

    arrays = {f"in_{k}": np.ascontiguousarray(v) for k, v in pack(inputs).items()}
    nc = bacc.Bacc("TRN2", target_bir_lowering=False, num_devices=1)
    I = {k[3:]: nc.dram_tensor(k, v.shape, mybir.dt.from_np(v.dtype), kind="ExternalInput").ap()
         for k, v in arrays.items()}
    O = {k: nc.dram_tensor(f"out_{k}", shape, F32, kind="ExternalOutput").ap() for k, shape in OUTS.items()}
    build(nc, I, O)
    r = run_bass_kernel_spmd(nc, [arrays], core_ids=[0]).results[0]
    return unpack({k: r[f"out_{k}"] for k in OUTS})


OUTS = {"y": (P, KC, T), "k": (P, TP), "v": (P, TP), "rg": (P, RG_CH, 2), "delta": (DN_H, 2, P, P)}


def unpack(r):
    y = r["y"].transpose(2, 1, 0).reshape(T, D)
    kv = [r[n].T.reshape(1, 1, TP, 2, HD) for n in ("k", "v")]
    rg = r["rg"].transpose(2, 1, 0).reshape(1, 1, 2, 512)
    delta = r["delta"].transpose(1, 0, 2, 3).reshape(1, 1, 2, DN_H, P, P)
    return (y[None, :TP], y[None, TP:], *(np.ascontiguousarray(a) for a in (*kv, rg, delta)))
```
